# Optimizing a Trainium2 kernel written in Bass

```python
import math
import jax, jax.numpy as jnp
from jax import lax
import numpy as np

D_MODEL = 1024
BATCH = 1
SEQ = 1024
DEPTH = 1
DEC_BATCH = 8
DEC_SEQ = 4
PAST_LEN = 2048
PAGE_SIZE = 128

ATT_HEADS = 8
ATT_DH = 64
ATT_VD = 2 * ATT_DH
QK_WIDTH = ATT_HEADS * 2 * ATT_DH
ATT_WIDTH = ATT_HEADS * ATT_VD
ROPE_THETA = 10000.0
Q_BLOCK = 128
GM_GROUPS = 8
GM_CHUNK = 128
GM_WIDTH = 1024
GM_GC = GM_WIDTH // GM_GROUPS
SPLITS = (QK_WIDTH, 2 * QK_WIDTH, 2 * QK_WIDTH + ATT_WIDTH, 2 * QK_WIDTH + ATT_WIDTH + 2 * GM_WIDTH)
IN_WIDTH = SPLITS[-1] + 2 * D_MODEL
PEER_HEADS = 8
PEER_NKEYS = 128
PEER_EXPERTS = PEER_NKEYS * PEER_NKEYS
PEER_DKEY = 256
PEER_DHALF = PEER_DKEY // 2
PEER_TOPK = 16
PEER_TOK_BLOCK = 256
EPS = 1e-6

kernel_name = "hybrid_diffattn_gmlp_peer_step"

def lambda_init_fn(layer):
    return 0.8 - 0.6 * math.exp(-0.3 * layer)

def rms_norm(x, g):
    xf = x.astype(jnp.float32)
    y = xf * lax.rsqrt(jnp.mean(xf * xf, axis=-1, keepdims=True) + EPS)
    return (y * g.astype(jnp.float32)).astype(x.dtype)

def rope(x, pos):
    half = ATT_DH // 2
    inv = 1.0 / (ROPE_THETA ** (jnp.arange(0, ATT_DH, 2, dtype=jnp.float32) / ATT_DH))
    ang = pos.astype(jnp.float32)[:, None] * inv[None, :]
    cos = jnp.cos(ang)[None, :, None, None, :]
    sin = jnp.sin(ang)[None, :, None, None, :]
    xf = x.astype(jnp.float32)
    x1, x2 = xf[..., :half], xf[..., half:]
    return jnp.concatenate([x1 * cos - x2 * sin, x2 * cos + x1 * sin], axis=-1).astype(x.dtype)

def adaln(c, w_ada, b_ada):
    m = jax.nn.silu(c) @ w_ada + b_ada
    return jnp.split(m[:, None, :], 6, axis=-1)

def modulate(x, g, shift, scale):
    return rms_norm(x, g) * (1 + scale) + shift

def diff_lambda(lq1, lk1, lq2, lk2, lambda_init):
    f = lambda a: a.astype(jnp.float32)
    return jnp.exp(jnp.sum(f(lq1) * f(lk1))) - jnp.exp(jnp.sum(f(lq2) * f(lk2))) + lambda_init

def diff_attend(q, k, v, q_pos, k_pos, lam):
    s = jnp.einsum('bqhmd,bkhmd->bhmqk', q, k, preferred_element_type=jnp.float32) * (ATT_DH ** -0.5)
    s = jnp.where(k_pos[None, :] <= q_pos[:, None], s, -jnp.inf)
    p = jax.nn.softmax(s, axis=-1)
    a = p[:, :, 0] - lam * p[:, :, 1]
    return jnp.einsum('bhqk,bkhe->bqhe', a.astype(v.dtype), v)

def spatial_gating(zuv, v_g, ws, bs):
    B, T, _ = zuv.shape
    u, v = jnp.split(jax.nn.gelu(zuv, approximate=False), 2, axis=-1)
    v = rms_norm(v.reshape(B, T, GM_GROUPS, GM_GC), v_g)
    nc = -(-T // GM_CHUNK)
    vp = jnp.pad(v, ((0, 0), (0, nc * GM_CHUNK - T), (0, 0), (0, 0))).reshape(B, nc, GM_CHUNK, GM_GROUPS, GM_GC)
    w = ws * jnp.tril(jnp.ones((GM_CHUNK, GM_CHUNK), ws.dtype))
    mixed = jnp.einsum('gij,bcjgd->bcigd', w, vp) + bs.T[:, :, None]
    mixed = mixed.reshape(B, nc * GM_CHUNK, GM_GROUPS, GM_GC)[:, :T].reshape(B, T, GM_WIDTH)
    return u * mixed, v.reshape(B, T, GM_WIDTH)

def peer(h, w_q, subkeys, u_tab, v_tab):
    lead = h.shape[:-1]
    xt = h.reshape(-1, D_MODEL)
    n = xt.shape[0]
    blk = min(PEER_TOK_BLOCK, n)
    nb = -(-n // blk)
    xt = jnp.pad(xt, ((0, nb * blk - n), (0, 0)))

    def one(xb):
        q = (xb @ w_q).reshape(blk, PEER_HEADS, 2, PEER_DHALF)
        s = jnp.einsum('thpd,hpkd->thpk', q, subkeys, preferred_element_type=jnp.float32)
        s1, i1 = lax.top_k(s[:, :, 0], PEER_TOPK)
        s2, i2 = lax.top_k(s[:, :, 1], PEER_TOPK)
        cand = (s1[..., :, None] + s2[..., None, :]).reshape(blk, PEER_HEADS, PEER_TOPK * PEER_TOPK)
        cidx = (i1[..., :, None] * PEER_NKEYS + i2[..., None, :]).reshape(blk, PEER_HEADS, PEER_TOPK * PEER_TOPK)
        top_s, sel = lax.top_k(cand, PEER_TOPK)
        idx = jnp.take_along_axis(cidx, sel, axis=-1)
        g = jax.nn.softmax(top_s, axis=-1)
        a = jnp.einsum('td,thkd->thk', xb, u_tab[idx], preferred_element_type=jnp.float32)
        wgt = (g * jax.nn.gelu(a, approximate=False)).astype(xb.dtype)
        return jnp.einsum('thk,thkd->td', wgt, v_tab[idx])

    out = lax.map(one, xt.reshape(nb, blk, D_MODEL))
    return out.reshape(nb * blk, D_MODEL)[:n].reshape(*lead, D_MODEL)

def decoder_layer(x, c, pos, attend, lambda_init, p):
    B, T, _ = x.shape
    sh1, sc1, g1, sh2, sc2, g2 = adaln(c, p['w_ada'], p['b_ada'])
    h = modulate(x, p['norm1_g'], sh1, sc1)
    z = h @ p['w_in']
    zq, zk, zv, zuv, zg = jnp.split(z, SPLITS, axis=-1)
    q = rope(rms_norm(zq.reshape(B, T, ATT_HEADS, 2, ATT_DH), p['q_norm_g']), pos)
    k = rope(rms_norm(zk.reshape(B, T, ATT_HEADS, 2, ATT_DH), p['k_norm_g']), pos)
    v = zv.reshape(B, T, ATT_HEADS, ATT_VD)
    lam = diff_lambda(p['lambda_q1'], p['lambda_k1'], p['lambda_q2'], p['lambda_k2'], lambda_init)
    o = attend(q, k, v, lam)
    a_out = (rms_norm(o, p['subln_g']) * (1 - lambda_init)).reshape(B, T, ATT_WIDTH)
    s_out, v_rows = spatial_gating(zuv, p['gm_v_norm_g'], p['gm_ws'], p['gm_bs'])
    ga, gb = jnp.split(jax.nn.sigmoid(zg), 2, axis=-1)
    mix = (ga * (a_out @ p['w_att_out']) + gb * (s_out @ p['w_gm_out'])) @ p['w_out']
    x = x + g1 * mix
    h2 = modulate(x, p['norm2_g'], sh2, sc2)
    x = x + g2 * peer(h2, p['peer_w_q'], p['peer_subkeys'], p['peer_u'], p['peer_v'])
    return x, k, v, v_rows

def setup_inputs(seed: int = 0) -> dict:
    key = jax.random.key(seed)
    ks = jax.random.split(key, 32)
    f32 = jnp.float32

    def nrm(i, shape, std):
        return std * jax.random.normal(ks[i], shape, f32)

    def gain(i, shape):
        return 1.0 + nrm(i, shape, 0.01)

    n_pages = PAST_LEN // PAGE_SIZE
    used = DEC_BATCH * n_pages
    n_pool = used + used // 4
    page_table = jax.random.permutation(ks[4], n_pool)[:used].reshape(DEC_BATCH, n_pages).astype(jnp.int32)
    L = DEPTH
    D = D_MODEL
    return {
        'x_prompt': nrm(0, (BATCH, SEQ, D), 1.0),
        'x_sample': nrm(1, (DEC_BATCH, DEC_SEQ, D), 1.0),
        'cache_k': nrm(2, (L, n_pool, PAGE_SIZE, ATT_HEADS, 2, ATT_DH), 1.0),
        'cache_v': nrm(3, (L, n_pool, PAGE_SIZE, ATT_HEADS, ATT_VD), 1.0),
        'page_table': page_table,
        'c_prompt': nrm(5, (BATCH, D), 1.0),
        'c_sample': nrm(6, (DEC_BATCH, D), 1.0),
        'w_ada': nrm(7, (L, D, 6 * D), 0.5 * D ** -0.5),
        'b_ada': nrm(8, (L, 6 * D), 0.01),
        'norm1_g': gain(9, (L, D)),
        'w_in': nrm(10, (L, D, IN_WIDTH), D ** -0.5),
        'q_norm_g': gain(11, (L, ATT_DH)),
        'k_norm_g': gain(12, (L, ATT_DH)),
        'lambda_q1': nrm(13, (L, ATT_DH), 0.1),
        'lambda_k1': nrm(14, (L, ATT_DH), 0.1),
        'lambda_q2': nrm(15, (L, ATT_DH), 0.1),
        'lambda_k2': nrm(16, (L, ATT_DH), 0.1),
        'subln_g': gain(17, (L, ATT_VD)),
        'gm_v_norm_g': gain(18, (L, GM_GC)),
        'gm_ws': nrm(19, (L, GM_GROUPS, GM_CHUNK, GM_CHUNK), GM_CHUNK ** -0.5),
        'gm_bs': gain(20, (L, GM_GROUPS, GM_CHUNK)),
        'w_att_out': nrm(21, (L, ATT_WIDTH, D), ATT_WIDTH ** -0.5),
        'w_gm_out': nrm(22, (L, GM_WIDTH, D), GM_WIDTH ** -0.5),
        'w_out': nrm(23, (L, D, D), D ** -0.5),
        'norm2_g': gain(24, (L, D)),
        'peer_w_q': nrm(25, (L, D, PEER_HEADS * PEER_DKEY), D ** -0.5),
        'peer_subkeys': nrm(26, (L, PEER_HEADS, 2, PEER_NKEYS, PEER_DHALF), PEER_DHALF ** -0.5),
        'peer_u': nrm(27, (L, PEER_EXPERTS, D), D ** -0.5),
        'peer_v': nrm(28, (L, PEER_EXPERTS, D), PEER_HEADS ** -0.5),
    }

def reference(x_prompt, x_sample, cache_k, cache_v, page_table, c_prompt, c_sample,
              w_ada, b_ada, norm1_g, w_in, q_norm_g, k_norm_g,
              lambda_q1, lambda_k1, lambda_q2, lambda_k2, subln_g,
              gm_v_norm_g, gm_ws, gm_bs, w_att_out, w_gm_out, w_out, norm2_g,
              peer_w_q, peer_subkeys, peer_u, peer_v):
    T_p = x_prompt.shape[1]
    T_s = x_sample.shape[1]
    past_len = page_table.shape[1] * cache_k.shape[2]
    pos_p = jnp.arange(T_p)
    pos_s = past_len + jnp.arange(T_s)
    k_pos_s = jnp.arange(past_len + T_s)
    yp, ys = x_prompt, x_sample
    kp_list, vp_list, ks_list, vs_list, gm_list = [], [], [], [], []
    for l in range(DEPTH):
        p = {
            'w_ada': w_ada[l], 'b_ada': b_ada[l], 'norm1_g': norm1_g[l], 'w_in': w_in[l],
            'q_norm_g': q_norm_g[l], 'k_norm_g': k_norm_g[l],
            'lambda_q1': lambda_q1[l], 'lambda_k1': lambda_k1[l],
            'lambda_q2': lambda_q2[l], 'lambda_k2': lambda_k2[l], 'subln_g': subln_g[l],
            'gm_v_norm_g': gm_v_norm_g[l], 'gm_ws': gm_ws[l], 'gm_bs': gm_bs[l],
            'w_att_out': w_att_out[l], 'w_gm_out': w_gm_out[l], 'w_out': w_out[l],
            'norm2_g': norm2_g[l], 'peer_w_q': peer_w_q[l], 'peer_subkeys': peer_subkeys[l],
            'peer_u': peer_u[l], 'peer_v': peer_v[l],
        }
        lam_init = lambda_init_fn(l)

        def attend_prompt(q, k, v, lam):
            B = q.shape[0]
            nq = T_p // Q_BLOCK
            qb = jnp.moveaxis(q.reshape(B, nq, Q_BLOCK, ATT_HEADS, 2, ATT_DH), 1, 0)
            pb = pos_p.reshape(nq, Q_BLOCK)
            o = lax.map(lambda qp: diff_attend(qp[0], k, v, qp[1], pos_p, lam), (qb, pb))
            return jnp.moveaxis(o, 0, 1).reshape(B, T_p, ATT_HEADS, ATT_VD)

        def attend_sample(q, k, v, lam):
            DB = q.shape[0]
            pk = cache_k[l][page_table].reshape(DB, past_len, ATT_HEADS, 2, ATT_DH)
            pv = cache_v[l][page_table].reshape(DB, past_len, ATT_HEADS, ATT_VD)
            k_all = jnp.concatenate([pk, k], axis=1)
            v_all = jnp.concatenate([pv, v], axis=1)
            return diff_attend(q, k_all, v_all, pos_s, k_pos_s, lam)

        yp, kp, vp, _ = decoder_layer(yp, c_prompt, pos_p, attend_prompt, lam_init, p)
        ys, ksm, vsm, gmv = decoder_layer(ys, c_sample, pos_s, attend_sample, lam_init, p)
        kp_list.append(kp)
        vp_list.append(vp)
        ks_list.append(ksm)
        vs_list.append(vsm)
        gm_list.append(gmv)
    new_k_prompt = jnp.stack(kp_list, axis=0)
    new_v_prompt = jnp.stack(vp_list, axis=0)
    new_k_sample = jnp.stack(ks_list, axis=0)
    new_v_sample = jnp.stack(vs_list, axis=0)
    new_gm_v_sample = jnp.stack(gm_list, axis=0)
    return (yp, ys, new_k_prompt, new_v_prompt, new_k_sample, new_v_sample, new_gm_v_sample)


_drawn_inputs = setup_inputs


def setup_inputs(seed=0):
    import zlib

    import numpy as np

    out = dict(_drawn_inputs(seed))
    spreads = {}
    factors = {'b_ada': 4.146,
     'norm1_g': 5.732,
     'q_norm_g': 30.674,
     'k_norm_g': 26.259,
     'lambda_q1': 6.926,
     'lambda_k1': 64.0,
     'lambda_q2': 6.849,
     'lambda_k2': 8.0,
     'subln_g': 64.0,
     'gm_v_norm_g': 36.136,
     'gm_bs': 36.574,
     'norm2_g': 64.0}
    for name, (base, spread) in spreads.items():
        noise = np.random.default_rng([zlib.crc32(name.encode()), seed]).standard_normal(out[name].shape)
        drawn = base * np.exp(spread * noise) if base else spread * noise
        out[name] = __import__('jax').numpy.asarray(drawn.astype(out[name].dtype))
    for name, factor in factors.items():
        out[name] = (out[name] * factor).astype(out[name].dtype)
    return out
```

```python
from contextlib import ExitStack

import concourse.bass as bass
from concourse import mybir

F32 = mybir.dt.float32
U32 = mybir.dt.uint32
I32 = mybir.dt.int32
ALU = mybir.AluOpType
ACT = mybir.ActivationFunctionType
AX = mybir.AxisListType

P = 128
D = 1024
KD = D // P
NP = 1024
PT = NP // P
NSEQ, NDEC = 8, 4
NS = NSEQ * NDEC
NT = NP + NS
TILES = PT + 1
PAST, PAGE = 2048, 128
NPAGES = PAST // PAGE
H, DH, VD = 8, 64, 128
ZW = 7168
ZQ, ZK, ZV, ZU, ZGV, ZGA, ZGB = [D * n for n in range(7)]
CB = 512
MODS = 6
EPS = 1e-6
GROUPS = 8
LAMBDA_INIT = 0.2
PH, NKEYS, TOPK = 8, 128, 16
SLOTS = PH * TOPK
NEG = -1e30


def rows_of(t):
    return P if t < PT else NS


def wait_if_any(eng, sem, value):
    if not isinstance(value, int) or value > 0:
        eng.wait_ge(sem, value)


def wait_apart(eng, sem, value, passed):
    if not isinstance(value, int) or value > 0:
        eng.wait_ge(sem, value)
        eng.sem_inc(passed, 1)


class Shared:
    pass


def adaln_phase(nc, g):
    NC = 1 + NSEQ
    WB = 2
    NB = MODS * D // CB
    with ExitStack() as ctx:
        sb = lambda name, shape, dt=F32: ctx.enter_context(nc.sbuf_tensor(name, shape, dt))
        c_rows = sb("c_rows", [NC, D])
        c_silu = sb("c_silu", [NC, D])
        cT = sb("cT", [P, KD, NC])
        bias = sb("ada_bias", [NC, MODS * D])
        gain = sb("ada_gain", [NC, 2, D])
        mod = sb("mod_rows", [NC, MODS * D])
        ident = sb("ident_a", [P, P])
        w = sb("w_ada_buf", [P, WB, KD, CB])
        lvec = sb("lambda_vectors", [P, 4, DH])
        lprod = sb("lambda_products", [P, 2, DH])
        ldot = sb("lambda_dots", [P, 2])
        ldif = sb("lambda_exp_difference", [P, 1])
        s_ld, s_le, s_lam = [g.sem("a_lambda_" + n) for n in ("dots", "exp", "done")]
        ps_t = ctx.enter_context(nc.psum_tensor("ps_cT", [P, CB], F32))
        ps_m = ctx.enter_context(nc.psum_tensor("ps_mod", [P, 2, CB], F32))
        s_in, s_silu, s_ct, s_ctc, s_mm, s_mod, s_out = [
            g.sem(n) for n in ("a_inputs", "a_silu", "a_cT_psum", "a_cT", "a_product", "a_mod", "a_stored")]
        s_w = [g.sem(f"a_weights{b}") for b in range(WB)]
        w_view = g.w_ada.rearrange("(k p) n -> p k n", p=P)
        with nc.Block() as block:
            @block.sync
            def _(sp):
                sp.dma_start(c_rows[0:1, :], g.c_prompt).then_inc(s_in, 16)
                sp.dma_start(c_rows[1:NC, :], g.c_sample).then_inc(s_in, 16)
                sp.dma_start(ident[:], g.ident).then_inc(s_in, 16)
                sp.dma_start(bias[:], g.b_ada.broadcast_to([NC, MODS * D])).then_inc(s_in, 16)
                sp.dma_start(gain[:, 0, :], g.norm1_g.broadcast_to([NC, D])).then_inc(s_in, 16)
                sp.dma_start(gain[:, 1, :], g.norm2_g.broadcast_to([NC, D])).then_inc(s_in, 16)
                for n, v in enumerate((g.lambda_q1, g.lambda_k1, g.lambda_q2, g.lambda_k2)):
                    sp.dma_start(lvec[:, n, :], v.broadcast_to([P, DH])).then_inc(s_in, 16)
                sp.wait_ge(s_mod, NB + 2)
                sp.dma_start(g.mod, mod[:]).then_inc(s_out, 16)
                sp.wait_ge(s_out, 16)

            @block.gpsimd
            def _(pool):
                for b in range(WB):
                    pool.dma_start(w[:, b], w_view[:, :, b * CB:(b + 1) * CB]).then_inc(s_w[b], 16)
                with pool.Fori(1, NB // WB) as i:
                    for b in range(WB):
                        pool.wait_ge(s_mm, i * WB + (b + 1 - WB))
                        pool.dma_start(w[:, b], w_view[:, :, bass.ds(i * (WB * CB) + b * CB, CB)]).then_inc(s_w[b], 16)

            @block.scalar
            def _(act):
                act.wait_ge(s_in, 160)
                nc.scalar.activation(c_silu[:], c_rows[:], ACT.Silu).then_inc(s_silu, 1)
                act.wait_ge(s_ld, 2)
                nc.scalar.activation(ldot[:], ldot[:], ACT.Exp).then_inc(s_le, 1)

            @block.tensor
            def _(pe):
                pe.wait_ge(s_in, 160)
                pe.wait_ge(s_silu, 1)
                for k in range(KD):
                    last = nc.tensor.transpose(ps_t[:, k * NC:(k + 1) * NC], c_silu[:, k * P:(k + 1) * P], ident[0:NC, 0:NC])
                last.then_inc(s_ct, 1)
                pe.wait_ge(s_ctc, 1)

                def block_product(b):
                    for k in range(KD):
                        last = nc.tensor.matmul(ps_m[0:NC, b, :], cT[:, k, :], w[:, b, k, :], start=k == 0, stop=k == KD - 1)
                    last.then_inc(s_mm, 1)
                for b in range(WB):
                    pe.wait_ge(s_w[b], 16)
                    block_product(b)
                with pe.Fori(1, NB // WB) as i:
                    for b in range(WB):
                        pe.wait_ge(s_w[b], i * 16 + 16)
                        pe.wait_ge(s_mod, i * WB + (b + 1 - WB))
                        block_product(b)

            @block.vector
            def _(dve):
                dve.wait_ge(s_ct, 1)
                nc.vector.tensor_copy(cT[:].rearrange("p k c -> p (k c)"), ps_t[:, 0:KD * NC]).then_inc(s_ctc, 1)
                dve.wait_ge(s_in, 160)
                with dve.Fori(0, NB // WB) as i:
                    for b in range(WB):
                        dve.wait_ge(s_mm, i * WB + (b + 1))
                        cols = bass.ds(i * (WB * CB) + b * CB, CB)
                        nc.vector.tensor_tensor(mod[:, cols], ps_m[0:NC, b, :], bias[:, cols], ALU.add).then_inc(s_mod, 1)
                for n in range(2):
                    nc.vector.tensor_tensor_reduce(lprod[:, n, :], lvec[:, 2 * n, :], lvec[:, 2 * n + 1, :], 1.0, 0.0,
                                                   ALU.mult, ALU.add, ldot[:, n:n + 1]).then_inc(s_ld, 1)
                dve.wait_ge(s_le, 1)
                nc.vector.tensor_tensor(ldif[:], ldot[:, 0:1], ldot[:, 1:2], ALU.subtract).then_inc(s_lam, 1)
                dve.wait_ge(s_lam, 1)
                nc.vector.tensor_scalar(g.lam[:], ldif[:], LAMBDA_INIT, None, ALU.add).then_inc(s_lam, 1)
                dve.wait_ge(s_mod, NB)
                for n in range(2):
                    part = mod[:, (3 * n + 1) * D:(3 * n + 2) * D]
                    nc.vector.scalar_tensor_tensor(out=part, in0=part, scalar=1.0, in1=gain[:, n, :],
                                                   op0=ALU.add, op1=ALU.mult).then_inc(s_mod, 1)


def projection_phase(nc, g):
    with nc.sbuf_tensor("hT", [P, KD, NT], F32) as hT, nc.sbuf_tensor("eps_b", [P, 1], F32) as eps:
        modulated_transposed(nc, g, hT, eps)
        z_blocks(nc, g, hT, eps)


def modulated_transposed(nc, g, hT, eps):
    with ExitStack() as ctx:
        sb = lambda name, shape, dt=F32: ctx.enter_context(nc.sbuf_tensor(name, shape, dt))
        ident = sb("ident_b", [P, P])
        x = sb("x_tile", [P, 2, D])
        h = sb("h_tile", [P, 2, D])
        modp = sb("mod_prompt", [P, 2, D])
        mods = sb("mod_sample", [NS, 2, D])
        ms = sb("mean_square", [P, 2, 1])
        rstd = sb("rstd_x", [P, 2, 1])
        ps_h = ctx.enter_context(nc.psum_tensor("ps_hT", [P, 2, D], F32))
        s_x = [g.sem(f"b_x{b}") for b in range(2)]
        s_in, s_sq, s_sqrt, s_rec, s_xn, s_xm, s_h, s_ht, s_htc = [
            g.sem("b_" + n) for n in ("inputs", "square", "sqrt", "rstd", "normed", "scaled", "h", "hT_psum", "hT")]
        x_dram = [g.x_prompt[t * P:(t + 1) * P, :] for t in range(PT)] + [g.x_sample]
        with nc.Block() as block:
            @block.sync
            def _(sp):
                sp.dma_start(ident[:], g.ident).then_inc(s_in, 16)
                for n in range(2):
                    sp.dma_start(modp[:, n, :], g.mod[0:1, n * D:(n + 1) * D].broadcast_to([P, D])).then_inc(s_in, 16)
                    for q in range(NSEQ):
                        sp.dma_start(mods[q * NDEC:(q + 1) * NDEC, n, :],
                                     g.mod[1 + q:2 + q, n * D:(n + 1) * D].broadcast_to([NDEC, D])).then_inc(s_in, 16)
                for t in range(TILES):
                    if t >= 2:
                        sp.wait_ge(s_xn, t - 1)
                    sp.dma_start(x[0:rows_of(t), t % 2, :], x_dram[t]).then_inc(s_x[t % 2], 16)

            @block.gpsimd
            def _(pool):
                nc.gpsimd.memset(eps[:], EPS).then_inc(s_in, 16)

            @block.scalar
            def _(act):
                act.wait_ge(s_in, 16 * (4 + 2 * NSEQ))
                for t in range(TILES):
                    r = rows_of(t)
                    act.wait_ge(s_x[t % 2], 16 * (t // 2 + 1))
                    if t >= 2:
                        act.wait_ge(s_ht, t - 1)
                    nc.scalar.activation(h[0:r, t % 2, :], x[0:r, t % 2, :], ACT.Square,
                                         accum_out=ms[0:r, t % 2, :]).then_inc(s_sq, 1)
                    act.wait_ge(s_sq, t + 1)
                    nc.scalar.activation(ms[0:r, t % 2, :], ms[0:r, t % 2, :], ACT.Sqrt, bias=eps[0:r, :],
                                         scale=1.0 / D).then_inc(s_sqrt, 1)

            @block.vector
            def _(dve):
                dve.wait_ge(s_in, 16 * (4 + 2 * NSEQ))

                def copy_hT(t):
                    r = rows_of(t)
                    dve.wait_ge(s_ht, t + 1)
                    nc.vector.tensor_copy(hT[:, :, t * P:t * P + r],
                                          ps_h[:, t % 2, :].rearrange("p (k c) -> p k c", c=P)[:, :, 0:r]).then_inc(s_htc, 1)
                for t in range(TILES):
                    r = rows_of(t)
                    m = modp if t < PT else mods
                    dve.wait_ge(s_sqrt, t + 1)
                    nc.vector.reciprocal(rstd[0:r, t % 2, :], ms[0:r, t % 2, :]).then_inc(s_rec, 1)
                    dve.wait_ge(s_rec, t + 1)
                    nc.vector.scalar_tensor_tensor(out=h[0:r, t % 2, :], in0=x[0:r, t % 2, :], scalar=rstd[0:r, t % 2, :],
                                                   in1=m[0:r, 1, :], op0=ALU.mult, op1=ALU.mult).then_inc(s_xn, 1)
                    dve.wait_ge(s_xn, t + 1)
                    nc.vector.tensor_tensor(h[0:r, t % 2, :], h[0:r, t % 2, :], m[0:r, 0, :], ALU.add).then_inc(s_h, 1)
                    if t >= 1:
                        copy_hT(t - 1)
                copy_hT(TILES - 1)

            @block.tensor
            def _(pe):
                pe.wait_ge(s_in, 16 * (4 + 2 * NSEQ))
                for t in range(TILES):
                    r = rows_of(t)
                    pe.wait_ge(s_h, t + 1)
                    if t >= 2:
                        pe.wait_ge(s_htc, t - 1)
                    for k in range(KD):
                        last = nc.tensor.transpose(ps_h[:, t % 2, k * P:k * P + r], h[0:r, t % 2, k * P:(k + 1) * P],
                                                   ident[0:r, 0:r])
                    last.then_inc(s_ht, 1)


def z_blocks(nc, g, hT, eps):
    RING = 6
    PAIRS = ZW // CB // 2
    STEPS = 2 * TILES
    assert STEPS % RING == 0
    NM = CB // DH
    NG = CB // P
    with ExitStack() as ctx:
        sb = lambda name, shape, dt=F32: ctx.enter_context(nc.sbuf_tensor(name, shape, dt))
        w = sb("w_in_buf", [P, 2, KD, CB])
        zs = sb("z_raw", [P, RING, CB])
        zo = sb("z_out", [P, RING, CB])
        sq = sb("z_square", [P, CB])
        t1 = sb("rope_cos_part", [P, CB])
        t2 = sb("rope_sin_part", [P, CB])
        ss = sb("z_sumsq", [P, NM])
        sd = sb("z_std", [P, NM])
        rs = sb("z_rstd", [P, NM])
        cs = sb("rope_tables", [P, TILES, 2, DH])
        gains = sb("qkv_gains", [P, 2, DH])
        vgain = sb("gate_v_gain", [P, P])
        ps_z = ctx.enter_context(nc.psum_tensor("ps_z", [P, RING, CB], F32))
        s_w = [g.sem(f"z_weights{b}") for b in range(2)]
        s_st = [g.sem(f"z_stored{j}") for j in range(RING)]
        LAPS = STEPS // RING
        s_in, s_z, s_zfree, s_zs, s_d, s_ss, s_std, s_zo = [
            g.sem("z_" + n) for n in ("consts", "product", "bank_free", "raw", "dve_chain", "sumsq", "std", "out_ready")]
        s_zoa = g.sem("z_out_ready_act")
        w_view = g.w_in.rearrange("(k p) n -> p k n", p=P)
        CHAIN_QK, CHAIN_GV = 8, 4
        NCONST = 16 * (TILES + 3)
        with nc.Block() as block:
            @block.gpsimd
            def _(pool):
                for b in range(2):
                    pool.dma_start(w[:, b], w_view[:, :, b * CB:(b + 1) * CB]).then_inc(s_w[b], 16)
                with pool.Fori(1, PAIRS) as i:
                    for b in range(2):
                        pool.wait_ge(s_z, i * STEPS + (b - 1) * TILES)
                        pool.dma_start(w[:, b], w_view[:, :, bass.ds(i * (2 * CB) + b * CB, CB)]).then_inc(s_w[b], 16)

            @block.tensor
            def _(pe):
                with pe.Fori(0, PAIRS) as i:
                    for b in range(2):
                        pe.wait_ge(s_w[b], i * 16 + 16)
                        for t in range(TILES):
                            r = rows_of(t)
                            n = b * TILES + t
                            pe.wait_ge(s_zfree, i * STEPS + (n + 1))
                            for k in range(KD):
                                last = nc.tensor.matmul(ps_z[0:r, n % RING, :], hT[:, k, t * P:t * P + r], w[:, b, k, :],
                                                        start=k == 0, stop=k == KD - 1)
                            last.then_inc(s_z, 1)

            kinds = [("rope", 0, 2), ("copy", 2, 3), ("gelu", 3, 4), ("gate_v", 4, 5), ("sigmoid", 5, 7)]

            @block.scalar
            def _(act):
                for _ in range(RING):
                    act.sem_inc(s_zfree, 1)
                act.wait_ge(s_in, NCONST)
                for kind, lo, hi in kinds:
                    with act.Fori(lo, hi) as i:
                        for n in range(STEPS):
                            r = rows_of(n % TILES)
                            act.wait_ge(s_z, i * STEPS + (n + 1))
                            src, j = ps_z[0:r, n % RING, :], n % RING
                            if kind in ("rope", "gate_v"):
                                f = ACT.Copy if kind == "rope" else ACT.Gelu
                                nc.scalar.activation(zs[0:r, j, :], src, f).then_inc(s_zs, 1)
                                act.wait_ge(s_zs, (i * STEPS + (n + 1)) if kind == "rope" else (i * STEPS + (n + 1 - 2 * STEPS)))
                                act.sem_inc(s_zfree, 1)
                                m, scale = (NM, 1.0 / DH) if kind == "rope" else (NG, 1.0 / P)
                                at = (n + 1) if kind == "rope" else (n + 1 - 2 * STEPS)
                                act.wait_ge(s_ss, i * STEPS + at)
                                nc.scalar.activation(sd[0:r, 0:m], ss[0:r, 0:m], ACT.Sqrt, bias=eps[0:r, :],
                                                     scale=scale).then_inc(s_std, 1)
                            else:
                                f = {"copy": ACT.Copy, "gelu": ACT.Gelu, "sigmoid": ACT.Sigmoid}[kind]
                                act.wait_ge(s_st[j], i * (16 * LAPS) + 16 * (n // RING))
                                nc.scalar.activation(zo[0:r, j, :], src, f).then_inc(s_zoa, 1)
                                off = 2 * STEPS if kind in ("copy", "gelu") else 3 * STEPS
                                act.wait_ge(s_zoa, i * STEPS + (n + 1 - off))
                                act.sem_inc(s_zfree, 1)

            @block.vector
            def _(dve):
                dve.wait_ge(s_in, NCONST)

                def step(kind, i, n, first):
                    t, j = n % TILES, n % RING
                    r = rows_of(t)
                    d_at = (lambda c: i * (STEPS * CHAIN_QK) + (n * CHAIN_QK + c)) if kind == "rope" else \
                        (lambda c: i * (STEPS * CHAIN_GV) + (2 * STEPS * CHAIN_QK + (n - 4 * STEPS) * CHAIN_GV + c))
                    at = (n + 1) if kind == "rope" else (n + 1 - 2 * STEPS)
                    m = NM if kind == "rope" else NG
                    wd = CB // m
                    z3 = zs[0:r, j, :].rearrange("p (m d) -> p m d", d=wd)
                    o3 = zo[0:r, j, :].rearrange("p (m d) -> p m d", d=wd)
                    q3 = sq[0:r, :].rearrange("p (m d) -> p m d", d=wd)
                    c = [0]

                    def link(ins):
                        c[0] += 1
                        ins.then_inc(s_d, 1)
                        dve.wait_ge(s_d, d_at(c[0]))
                    dve.wait_ge(s_zs, i * STEPS + at)
                    link(nc.vector.tensor_tensor(sq[0:r, :], zs[0:r, j, :], zs[0:r, j, :], ALU.mult))
                    nc.vector.tensor_reduce(ss[0:r, 0:m], q3, AX.X, ALU.add).then_inc(s_ss, 1)
                    dve.wait_ge(s_std, i * STEPS + at)
                    link(nc.vector.reciprocal(rs[0:r, 0:m], sd[0:r, 0:m]))
                    rb = rs[0:r, 0:m].unsqueeze(2).broadcast_to([r, m, wd])
                    link(nc.vector.tensor_tensor(z3, z3, rb, ALU.mult))
                    if not first:
                        dve.wait_ge(s_st[j], i * (16 * LAPS) + 16 * (n // RING))
                    if kind == "gate_v":
                        gb = vgain[0:r, :].unsqueeze(1).broadcast_to([r, m, wd])
                        link(nc.vector.tensor_tensor(o3, z3, gb, ALU.mult))
                    else:
                        gb = gains[0:r, n_gain[0], :].unsqueeze(1).broadcast_to([r, m, wd])
                        link(nc.vector.tensor_tensor(z3, z3, gb, ALU.mult))
                        hd = DH // 2
                        cb = cs[0:r, t, 0, :].unsqueeze(1).broadcast_to([r, m, DH])
                        a3 = t1[0:r, :].rearrange("p (m d) -> p m d", d=DH)
                        b3 = t2[0:r, :].rearrange("p (m d) -> p m d", d=DH)
                        link(nc.vector.tensor_tensor(a3, z3, cb, ALU.mult))
                        for lo, other in ((0, hd), (hd, 0)):
                            sn = cs[0:r, t, 1, lo:lo + hd].unsqueeze(1).broadcast_to([r, m, hd])
                            link(nc.vector.tensor_tensor(b3[:, :, lo:lo + hd], z3[:, :, other:other + hd], sn, ALU.mult))
                        link(nc.vector.tensor_tensor(zo[0:r, j, :], t1[0:r, :], t2[0:r, :], ALU.add))
                    dve.sem_inc(s_zo, 1)
                n_gain = [0]
                for n in range(STEPS):
                    step("rope", 0, n, n < RING)
                n_gain[0] = 1
                for n in range(STEPS):
                    step("rope", 1, n, False)
                with dve.Fori(4, 5) as i:
                    for n in range(STEPS):
                        step("gate_v", i, n, False)

            @block.sync
            def _(sp):
                for t in range(TILES):
                    sp.dma_start(cs[0:rows_of(t), t], g.rope[t * P:t * P + rows_of(t)]).then_inc(s_in, 16)
                sp.dma_start(gains[:, 0, :], g.q_norm_g.broadcast_to([P, DH])).then_inc(s_in, 16)
                sp.dma_start(gains[:, 1, :], g.k_norm_g.broadcast_to([P, DH])).then_inc(s_in, 16)
                sp.dma_start(vgain[:], g.gm_v_norm_g.broadcast_to([P, P])).then_inc(s_in, 16)
                for kind, lo, hi in kinds:
                    ready, off = {"rope": (s_zo, 0), "gate_v": (s_zo, 2), "copy": (s_zoa, 2), "gelu": (s_zoa, 2),
                                  "sigmoid": (s_zoa, 3)}[kind]
                    with sp.Fori(lo, hi) as i:
                      for n in range(STEPS):
                        b, t = divmod(n, TILES)
                        r = rows_of(t)
                        sp.wait_ge(ready, i * STEPS + (n + 1 - off * STEPS))
                        sp.dma_start(g.z[t * P:t * P + r, bass.ds(i * (2 * CB) + b * CB, CB)],
                                     zo[0:r, n % RING, :]).then_inc(s_st[n % RING], 16)
                for j in range(RING):
                    sp.wait_ge(s_st[j], 16 * PAIRS * LAPS)


SCALE = DH ** -0.5


def prompt_attention_phase(nc, g):
    with ExitStack() as ctx:
        sb = lambda name, shape, dt=F32: ctx.enter_context(nc.sbuf_tensor(name, shape, dt))
        ident, mask = sb("ident_c", [P, P]), sb("causal_mask", [P, P])
        qkv = sb("qkv_rows", [P, 2, 3, PT, P])
        qkT = sb("qkT", [P, 2, 2, NP])
        prob = sb("prob", [P, 2, 2, NP])
        diff = sb("diff_prob", [P, 2, NP])
        diffT = sb("diff_probT", [P, 2, NP])
        o = sb("att_rows", [P, 2, PT, P])
        nmax, nbias, rsum, rec, coef = [sb(n, [P, 2, 2]) for n in ("neg_max", "exp_bias", "row_sum", "row_rec", "map2_coef")]
        ps_s = ctx.enter_context(nc.psum_tensor("ps_scores", [P, 2, NP], F32))
        ps_t = ctx.enter_context(nc.psum_tensor("ps_turned", [P, NP], F32))
        ps_o = ctx.enter_context(nc.psum_tensor("ps_att", [P, 2, CB], F32))
        s_in = g.sem("c_consts")
        s_ld = [g.sem(f"c_qkv{b}") for b in range(2)]
        s_st = [g.sem(f"c_stored{b}") for b in range(2)]
        s_ofree = [g.sem(f"c_rows_free{b}") for b in range(2)]
        s_turn, s_turnc, s_s, s_nm, s_nb, s_e, s_rec, s_coef, s_p2, s_a, s_at, s_atc, s_o, s_oc = [
            g.sem("c_" + n) for n in ("qk_turned", "qkT", "scores", "neg_max", "exp_bias", "exp", "rec", "map2_coef",
                                      "map2_scaled", "diff", "diff_turned", "diffT", "att", "att_rows")]
        HEADS2 = 2 * PT
        with nc.Block() as block:
            @block.sync
            def _(sp):
                sp.dma_start(ident[:], g.ident).then_inc(s_in, 16)
                sp.dma_start(mask[:], g.mask).then_inc(s_in, 16)

                def load(h, par):
                    for n in range(3):
                        sp.dma_start(qkv[:, par, n], g.z[0:NP, bass.ds(h * P + n * D, P)]
                                     .rearrange("(t p) c -> p t c", p=P)).then_inc(s_ld[par], 16)
                load(0, 0)
                load(1, 1)

                def head(i, par, more):
                    sp.wait_ge(s_oc, i * HEADS2 + ((par + 1) * PT + 2))
                    sp.dma_start(g.att[0:NP, bass.ds(i * (2 * P) + par * P, P)].rearrange("(t p) c -> p t c", p=P),
                                 o[:, par]).then_inc(s_st[par], 16)
                    if more:
                        load(i * 2 + (2 + par), par)
                    sp.wait_ge(s_st[par], i * 16 + 16)
                    sp.sem_inc(s_ofree[par], 1)
                for par in range(2):
                    sp.sem_inc(s_ofree[par], 1)
                with sp.Fori(0, H // 2 - 1) as i:
                    for par in range(2):
                        head(i, par, True)
                for par in range(2):
                    head(H // 2 - 1, par, False)

            @block.tensor
            def _(pe):
                pe.wait_ge(s_in, 32)
                with pe.Fori(0, H // 2) as i:
                    for par in range(2):
                        pe.wait_ge(s_ld[par], i * 48 + 48)
                        for n in range(2):
                            if n == 0:
                                pe.wait_ge(s_atc, i * HEADS2 + (par * PT + 1))
                            else:
                                pe.wait_ge(s_turnc, i * 4 + (2 * par + 1))
                            for t in range(PT):
                                last = nc.tensor.transpose(ps_t[:, t * P:(t + 1) * P], qkv[:, par, n, t, :], ident[:])
                            last.then_inc(s_turn, 1)
                        pe.wait_ge(s_turnc, i * 4 + (2 * par + 2))

                        def scores(t):
                            step = par * PT + t
                            pe.wait_ge(s_e, i * (2 * HEADS2) + (2 * step + 2))
                            for m in range(2):
                                rows = slice(m * DH, (m + 1) * DH)
                                for c in range(0, (t + 1) * P, CB):
                                    w = min(CB, (t + 1) * P - c)
                                    edge = c + w == (t + 1) * P
                                    last = nc.tensor.matmul(ps_s[:, m, c:c + w], qkT[rows, par, 0, t * P:(t + 1) * P],
                                                            qkT[rows, par, 1, c:c + w], start=True, stop=not edge)
                                last = nc.tensor.matmul(ps_s[:, m, t * P:(t + 1) * P], ident[:], mask[:], start=False, stop=True)
                            last.then_inc(s_s, 1)
                        scores(0)
                        for t in range(PT):
                            step = par * PT + t
                            if t + 1 < PT:
                                scores(t + 1)
                            pe.wait_ge(s_a, i * HEADS2 + (step + 1))
                            if t > 0:
                                pe.wait_ge(s_atc, i * HEADS2 + (step + 1))
                            for c in range(t + 1):
                                last = nc.tensor.transpose(ps_t[:, c * P:(c + 1) * P], diff[:, t % 2, c * P:(c + 1) * P], ident[:])
                            last.then_inc(s_at, 1)
                            pe.wait_ge(s_atc, i * HEADS2 + (step + 2))
                            pe.wait_ge(s_oc, i * HEADS2 + (step + 1))
                            for c in range(t + 1):
                                last = nc.tensor.matmul(ps_o[:, t % 2, 0:P], diffT[:, t % 2, c * P:(c + 1) * P],
                                                        qkv[:, par, 2, c, :], start=c == 0, stop=c == t)
                            last.then_inc(s_o, 1)

            @block.scalar
            def _(act):
                act.sem_inc(s_e, 2)
                act.sem_inc(s_atc, 1)
                with act.Fori(0, H // 2) as i:
                    for par in range(2):
                        for n in range(2):
                            act.wait_ge(s_turn, i * 4 + (2 * par + n + 1))
                            nc.scalar.activation(qkT[:, par, n, :], ps_t[:], ACT.Copy).then_inc(s_turnc, 1)

                        def exps(t):
                            step = par * PT + t
                            n = (t + 1) * P
                            act.wait_ge(s_nb, i * HEADS2 + (step + 1))
                            for m in range(2):
                                nc.scalar.activation(prob[:, t % 2, m, 0:n], ps_s[:, m, 0:n], ACT.Exp, bias=nbias[:, t % 2, m:m + 1],
                                                     scale=SCALE, accum_out=rsum[:, t % 2, m:m + 1]).then_inc(s_e, 1)
                        exps(0)
                        for t in range(PT):
                            step = par * PT + t
                            if t + 1 < PT:
                                exps(t + 1)
                            n = (t + 1) * P
                            act.wait_ge(s_at, i * HEADS2 + (step + 1))
                            nc.scalar.activation(diffT[:, t % 2, 0:n], ps_t[:, 0:n], ACT.Copy).then_inc(s_atc, 1)

            @block.vector
            def _(dve):
                dve.sem_inc(s_oc, 2)

                def bias(i, par, t):
                    step, n, b = par * PT + t, (t + 1) * P, t % 2
                    dve.wait_ge(s_s, i * HEADS2 + (step + 1))
                    nc.vector.tensor_reduce(nmax[:, b, :], ps_s[:, :, 0:n], AX.X, ALU.max, negate=True).then_inc(s_nm, 1)
                    dve.wait_ge(s_nm, i * HEADS2 + (step + 1))
                    nc.vector.tensor_scalar(nbias[:, b, :], nmax[:, b, :], SCALE, None, ALU.mult).then_inc(s_nb, 1)

                def combine(i, par, t):
                    step, n, b = par * PT + t, (t + 1) * P, t % 2
                    dve.wait_ge(s_e, i * (2 * HEADS2) + (2 * step + 4))
                    nc.vector.reciprocal(rec[:, b, :], rsum[:, b, :]).then_inc(s_rec, 1)
                    dve.wait_ge(s_rec, i * HEADS2 + (step + 1))
                    nc.vector.tensor_scalar(coef[:, b, 0:1], rec[:, b, 1:2], g.lam[:, 0:1], None, ALU.mult).then_inc(s_coef, 1)
                    dve.wait_ge(s_coef, i * HEADS2 + (step + 1))
                    nc.vector.tensor_scalar(prob[:, b, 1, 0:n], prob[:, b, 1, 0:n], coef[:, b, 0:1], None, ALU.mult).then_inc(s_p2, 1)
                    dve.wait_ge(s_p2, i * HEADS2 + (step + 1))
                    nc.vector.scalar_tensor_tensor(out=diff[:, b, 0:n], in0=prob[:, b, 0, 0:n], scalar=rec[:, b, 0:1],
                                                   in1=prob[:, b, 1, 0:n], op0=ALU.mult, op1=ALU.subtract).then_inc(s_a, 1)

                def rows_out(i, par, t):
                    step = par * PT + t
                    dve.wait_ge(s_o, i * HEADS2 + (step + 1))
                    nc.vector.tensor_copy(o[:, par, t, :], ps_o[:, t % 2, 0:P]).then_inc(s_oc, 1)

                with dve.Fori(0, H // 2) as i:
                    for par in range(2):
                        bias(i, par, 0)
                        for t in range(PT):
                            combine(i, par, t)
                            if t + 1 < PT:
                                bias(i, par, t + 1)
                            if t == 1:
                                dve.wait_ge(s_ofree[par], i + 1)
                            if t > 0:
                                rows_out(i, par, t - 1)
                        rows_out(i, par, PT - 1)


def sample_attention_phase(nc, g):
    R2 = 2 * H * NDEC
    R1 = H * NDEC
    KR = 4
    GP = CB // PAGE
    NG = NPAGES // GP
    with ExitStack() as ctx:
        sb = lambda name, shape, dt=F32: ctx.enter_context(nc.sbuf_tensor(name, shape, dt))
        ident = sb("ident_d", [P, P])
        mask = sb("new_mask", [R2, NDEC])
        prow = sb("partition_number", [P, 1])
        rowidx = sb("page_rows", [P, NSEQ * NPAGES], U32)
        idx = sb("page_rows_now", [P, 2, NPAGES], U32)
        qkT = sb("qk_sampleT", [P, 2, H, NS])
        qsel = sb("q_by_rows", [P, 2, H * (R2 + NDEC)])
        kpage = sb("k_pages", [P, KR, D])
        vpage = sb("v_pages", [P, 2, NPAGES, D])
        vnew = sb("v_new", [NDEC, 2, D])
        kT = sb("kT_pages", [P, 2, H, CB])
        prob = sb("prob_sample", [R2, PAST + NDEC])
        stat = sb("softmax_stats", [R2, 8])
        sign = sb("map_sign", [R2, 1])
        pT = sb("probT", [P, CB])
        ptab = pT[:, 0:NSEQ * NPAGES].bitcast(I32)
        ptabf = pT[:, CB - NSEQ * NPAGES:CB]
        qk = prob[0:NS, 0:2 * D].rearrange("p (n c) -> p n c", n=2)
        aT = sb("diffT_sample", [P, NPAGES + 1, R1])
        o = sb("att_sample", [R1, D])
        ps_s = ctx.enter_context(nc.psum_tensor("ps_scores_d", [R2, PAST], F32))
        ps_t = ctx.enter_context(nc.psum_tensor("ps_turned_d", [P, 2, CB], F32))
        ps_o = ctx.enter_context(nc.psum_tensor("ps_att_d", [R1, D], F32))
        s_in, s_idx0, s_qkt, s_qktc = [g.sem("d_" + n) for n in ("inputs", "row_numbers", "qk_turned", "qkT")]
        s_idx, s_qsel, s_sg, s_sn, s_chain, s_nb, s_e, s_ps, s_pt, s_ptc, s_at, s_o, s_oc = [
            g.sem("d_" + n) for n in ("index_copied", "q_by_rows", "group_scores", "new_scores", "softmax_chain",
                                      "exp_bias", "exp", "prob_scaled", "prob_turned", "probT", "diffT", "att", "att_copied")]
        s_kt = [g.sem(f"d_k_turned{b}") for b in range(2)]
        s_ktc = [g.sem(f"d_k_copied{b}") for b in range(2)]
        s_k = [g.sem(f"d_k_page{j}") for j in range(KR)]
        s_v = [g.sem(f"d_v_pages{b}") for b in range(2)]
        s_vn = [g.sem(f"d_v_new{b}") for b in range(2)]
        s_ost = g.sem("d_stored")
        s_pass_pool, s_pass_pe = g.sem("d_pool_passed"), g.sem("d_tensor_passed")
        s_ofree = g.sem("d_rows_free")
        kc = g.cache_k
        vc = g.cache_v
        NIN = 5

        def nothing(s, par):
            pass

        def schedule(eng, turn_keys, join, softmax, finish):
            def around(s, par):
                turn_keys(s + 1, 1 - par)
                join(s, par)
                softmax(s + 1, 1 - par)
                finish(s, par)
            turn_keys(0, 0)
            softmax(0, 0)
            with eng.Fori(0, NSEQ // 2 - 1) as i:
                around(i * 2, 0)
                around(i * 2 + 1, 1)
            around(NSEQ - 2, 0)
            join(NSEQ - 1, 1)
            finish(NSEQ - 1, 1)

        with nc.Block() as block:
            @block.sync
            def _(sp):
                sp.dma_start(ident[:], g.ident).then_inc(s_in, 16)
                sp.dma_start(mask[:], g.new_mask).then_inc(s_in, 16)
                sp.dma_start(ptab, g.page_table.rearrange("a b -> (a b)").unsqueeze(0).broadcast_to([P, NSEQ * NPAGES])).then_inc(s_in, 16)
                sp.dma_start(prow[:], g.prow).then_inc(s_in, 16)
                sp.dma_start(qk, g.z[NP:NT, 0:2 * D].rearrange("t (n c) -> t n c", n=2)).then_inc(s_in, 16)

                def new_values(s, par):
                    sp.dma_start(vnew[:, par, :], g.z[bass.ds(s * NDEC + NP, NDEC), ZV:ZV + D]).then_inc(s_vn[par], 16)
                new_values(0, 0)
                new_values(1, 1)

                sp.sem_inc(s_ofree, 1)

                def store(s, par, more):
                    sp.wait_ge(s_oc, s + 2)
                    for h in range(H):
                        sp.dma_start(g.att[bass.ds(s * NDEC + NP, NDEC), h * VD:(h + 1) * VD],
                                     o[h * NDEC:(h + 1) * NDEC, h * VD:(h + 1) * VD]).then_inc(s_ost, 16)
                    sp.wait_ge(s_ost, s * (16 * H) + 16 * H)
                    sp.sem_inc(s_ofree, 1)
                    if more:
                        new_values(s + 2, par)
                with sp.Fori(0, NSEQ // 2 - 1) as i:
                    store(i * 2, 0, True)
                    store(i * 2 + 1, 1, True)
                store(NSEQ - 2, 0, False)
                store(NSEQ - 1, 1, False)

            @block.gpsimd
            def _(pool):
                pool.wait_ge(s_idx0, 5)

                def load_v(s, par, pg):
                    pool.indirect_dma_start(vpage[:, par, pg, :], None, vc,
                                            bass.IndirectOffsetOnAxis(ap=idx[:, par, pg:pg + 1], axis=0)).then_inc(s_v[par], 16)

                def kstage(s, par):
                    if not isinstance(s, int) or s > 1:
                        pool.wait_ge(s_o, s + 1)
                    nc.gpsimd.tensor_copy(idx[:, par, :], rowidx[:, bass.ds(s * NPAGES, NPAGES)]).then_inc(s_idx, 1)
                    wait_apart(pool, s_idx, s + 1, s_pass_pool)
                    for pg in range(NPAGES):
                        j = pg % KR
                        wait_apart(pool, s_kt[1], s * NPAGES + (pg + 1 - KR), s_pass_pool)
                        pool.indirect_dma_start(kpage[:, j, :], None, kc,
                                                bass.IndirectOffsetOnAxis(ap=idx[:, par, pg:pg + 1], axis=0)).then_inc(s_k[j], 16)
                        load_v(s, par, pg)
                schedule(pool, kstage, nothing, nothing, nothing)

            @block.tensor
            def _(pe):
                pe.sem_inc(s_o, 2)
                pe.wait_ge(s_in, 16 * NIN)
                for n in range(2):
                    for h in range(H):
                        last = nc.tensor.transpose(ps_t[:, n, h * NS:(h + 1) * NS], qk[:, n, h * P:(h + 1) * P], ident[0:NS, 0:NS])
                    last.then_inc(s_qkt, 1)
                pe.wait_ge(s_qktc, 2)
                KU = NPAGES

                def kstage(s, par):
                    pe.wait_ge(s_qsel, s + 1)
                    for pg in range(NPAGES):
                        j, grp = pg % KR, pg // GP
                        pe.wait_ge(s_k[j], s * (16 * NPAGES // KR) + 16 * (pg // KR + 1))
                        if pg == 0:
                            wait_if_any(pe, s_e, s * 2)
                        for b in range(2):
                            wait_if_any(pe, s_ktc[b], s * KU + pg)
                            for q in range(4):
                                h = 4 * b + q
                                last = nc.tensor.transpose(ps_t[:, b, q * P:(q + 1) * P], kpage[:, j, h * P:(h + 1) * P], ident[:])
                            last.then_inc(s_kt[b], 1)
                        if pg % GP == GP - 1:
                            for b in range(2):
                                pe.wait_ge(s_ktc[b], s * KU + (pg + 1))
                            for h in range(H):
                                last = nc.tensor.matmul(ps_s[:, grp * CB:(grp + 1) * CB], qsel[:, par, h * R2:(h + 1) * R2],
                                                        kT[:, grp % 2, h, :], start=h == 0, stop=h == H - 1)
                            last.then_inc(s_sg, 1)
                    for h in range(H):
                        nc.tensor.matmul(ps_t[0:R2, 0, 0:NDEC], qsel[:, par, h * R2:(h + 1) * R2],
                                         qkT[:, 1, h, bass.ds(s * NDEC, NDEC)], start=h == 0, stop=False)
                    nc.tensor.matmul(ps_t[0:R2, 0, 0:NDEC], ident[0:R2, 0:R2], mask[:], start=False, stop=True).then_inc(s_sn, 1)

                def pvstage(s, par):
                    wait_apart(pe, s_ps, s + 1, s_pass_pe)
                    for u in range(2):
                        if u:
                            wait_apart(pe, s_ptc, s * 3 + u, s_pass_pe)
                        for q in range(8):
                            pg = 8 * u + q
                            last = nc.tensor.transpose(ps_t[:, 1, q * R2:(q + 1) * R2], prob[:, pg * PAGE:(pg + 1) * PAGE],
                                                       ident[0:R2, 0:R2])
                        last.then_inc(s_pt, 1)
                    wait_apart(pe, s_ptc, s * 3 + 2, s_pass_pe)
                    nc.tensor.transpose(ps_t[0:NDEC, 1, 0:R2], prob[:, PAST:PAST + NDEC], ident[0:R2, 0:R2]).then_inc(s_pt, 1)
                    pe.wait_ge(s_v[par], (s - par) * (8 * NPAGES) + 16 * NPAGES)
                    pe.wait_ge(s_vn[par], (s - par) * 8 + 16)
                    pe.wait_ge(s_at, s * 3 + 3)
                    pe.wait_ge(s_oc, s + 1)
                    for c in range(2):
                        cols = slice(c * CB, (c + 1) * CB)
                        for pg in range(NPAGES):
                            nc.tensor.matmul(ps_o[:, cols], aT[:, pg, :], vpage[:, par, pg, cols], start=pg == 0, stop=False)
                        last = nc.tensor.matmul(ps_o[:, cols], aT[0:NDEC, NPAGES, :], vnew[:, par, cols], start=False, stop=True)
                    last.then_inc(s_o, 1)
                schedule(pe, kstage, nothing, nothing, pvstage)

            @block.vector
            def _(dve):
                dve.sem_inc(s_oc, 1)
                nc.vector.memset(qsel[:], 0.0).then_inc(s_idx0, 1)
                nc.vector.memset(sign[0:R1, :], 1.0).then_inc(s_idx0, 1)
                nc.vector.tensor_scalar(sign[R1:R2, :], g.lam[R1:R2, 0:1], -1.0, None, ALU.mult).then_inc(s_idx0, 1)
                dve.wait_ge(s_in, 16 * NIN)
                nc.vector.tensor_copy(ptabf, ptab).then_inc(s_idx0, 1)
                dve.wait_ge(s_idx0, 4)
                nc.vector.tensor_scalar(rowidx[:], ptabf, float(PAGE), prow[:, 0:1], ALU.mult, ALU.add).then_inc(s_idx0, 1)
                dve.wait_ge(s_idx0, 5)
                for n in range(2):
                    dve.wait_ge(s_qkt, n + 1)
                    nc.vector.tensor_copy(qkT[:, n].rearrange("p h t -> p (h t)"), ps_t[:, n, 0:H * NS]).then_inc(s_qktc, 1)
                dve.wait_ge(s_qktc, 2)

                def prepare(s, par):
                    spread = qsel[:, par, :].rearrange("p (h c) -> p h c", h=H)
                    for m in range(2):
                        rows = slice(m * DH, (m + 1) * DH)
                        last = nc.vector.tensor_copy(spread[rows, :, m * R1:m * R1 + NDEC], qkT[rows, 0, :, bass.ds(s * NDEC, NDEC)])
                    last.then_inc(s_qsel, 1)
                prepare(0, 0)
                prepare(1, 1)
                CH = 6

                def kstage(s, par):
                    for pg in range(NPAGES):
                        dve.wait_ge(s_kt[0], s * NPAGES + (pg + 1))
                        if pg % GP == 0:
                            wait_if_any(dve, s_sg, s * NG + (pg // GP - 1))
                        nc.vector.tensor_copy(kT[:, (pg // GP) % 2, 0:4, (pg % GP) * P:(pg % GP + 1) * P],
                                              ps_t[:, 0, :].rearrange("p (h c) -> p h c", h=4)).then_inc(s_ktc[0], 1)

                def softmax(s, par):
                    c = [0]

                    def link(ins):
                        c[0] += 1
                        ins.then_inc(s_chain, 1)
                        dve.wait_ge(s_chain, s * CH + c[0])
                    dve.wait_ge(s_sg, s * NG + NG)
                    link(nc.vector.tensor_reduce(stat[:, 0:1], ps_s[:], AX.X, ALU.max))
                    dve.wait_ge(s_sn, s + 1)
                    link(nc.vector.tensor_reduce(stat[:, 1:2], ps_t[0:R2, 0, 0:NDEC], AX.X, ALU.max))
                    link(nc.vector.tensor_reduce(stat[:, 2:3], stat[:, 0:2], AX.X, ALU.max, negate=True))
                    nc.vector.tensor_scalar(stat[:, 3:4], stat[:, 2:3], SCALE, None, ALU.mult).then_inc(s_nb, 1)
                    dve.wait_ge(s_e, s * 2 + 2)
                    link(nc.vector.tensor_tensor(stat[:, 6:7], stat[:, 4:5], stat[:, 5:6], ALU.add))
                    link(nc.vector.reciprocal(stat[:, 7:8], stat[:, 6:7]))
                    link(nc.vector.tensor_tensor(stat[:, 6:7], stat[:, 7:8], sign[:], ALU.mult))
                    nc.vector.tensor_scalar(prob[:], prob[:], stat[:, 6:7], None, ALU.mult).then_inc(s_ps, 1)

                def join(s, par):
                    for u in range(3):
                        dve.wait_ge(s_ptc, s * 3 + (u + 1))
                        if u == 0:
                            dve.wait_ge(s_o, s + 2)
                        if u < 2:
                            v = pT[:, :].rearrange("p (g m r) -> p g m r", m=2, r=R1)
                            nc.vector.tensor_tensor(aT[:, 8 * u:8 * u + 8, :], v[:, :, 0, :], v[:, :, 1, :], ALU.add).then_inc(s_at, 1)
                        else:
                            nc.vector.tensor_tensor(aT[0:NDEC, NPAGES, :], pT[0:NDEC, 0:R1], pT[0:NDEC, R1:R2], ALU.add).then_inc(s_at, 1)

                def finish(s, par):
                    dve.wait_ge(s_ofree, s + 1)
                    dve.wait_ge(s_o, s + 3)
                    nc.vector.tensor_copy(o[:], ps_o[:]).then_inc(s_oc, 1)
                    prepare_next(s, par)

                def prepare_next(s, par):
                    if not (isinstance(s, int) and s >= NSEQ - 2):
                        prepare(s + 2, par)
                schedule(dve, kstage, join, softmax, finish)

            @block.scalar
            def _(act):
                def kstage(s, par):
                    for pg in range(NPAGES):
                        act.wait_ge(s_kt[1], s * NPAGES + (pg + 1))
                        if pg % GP == 0:
                            wait_if_any(act, s_sg, s * NG + (pg // GP - 1))
                        nc.scalar.activation(kT[:, (pg // GP) % 2, 4:8, (pg % GP) * P:(pg % GP + 1) * P],
                                             ps_t[:, 1, :].rearrange("p (h c) -> p h c", h=4), ACT.Copy).then_inc(s_ktc[1], 1)

                def softmax(s, par):
                    act.wait_ge(s_nb, s + 1)
                    wait_if_any(act, s_pt, s * 3)
                    nc.scalar.activation(prob[:, 0:PAST], ps_s[:], ACT.Exp, bias=stat[:, 3:4], scale=SCALE,
                                         accum_out=stat[:, 4:5]).then_inc(s_e, 1)
                    nc.scalar.activation(prob[:, PAST:PAST + NDEC], ps_t[0:R2, 0, 0:NDEC], ACT.Exp, bias=stat[:, 3:4], scale=SCALE,
                                         accum_out=stat[:, 5:6]).then_inc(s_e, 1)

                def pvstage(s, par):
                    for u in range(3):
                        act.wait_ge(s_pt, s * 3 + (u + 1))
                        if u:
                            act.wait_ge(s_at, s * 3 + u)
                        if u < 2:
                            nc.scalar.activation(pT[:], ps_t[:, 1, :], ACT.Copy).then_inc(s_ptc, 1)
                        else:
                            nc.scalar.activation(pT[0:NDEC, 0:R2], ps_t[0:NDEC, 1, 0:R2], ACT.Copy).then_inc(s_ptc, 1)
                schedule(act, kstage, pvstage, softmax, nothing)


def mix_phase(nc, g):
    with ExitStack() as ctx:
        sb = lambda name, shape, dt=F32: ctx.enter_context(nc.sbuf_tensor(name, shape, dt))
        w_att, w_gm, w_o = [sb(n, [P, KD, D]) for n in ("w_att", "w_gm", "w_o")]
        ident, lower = sb("ident_e", [P, P]), sb("lower_T", [P, P])
        ws_rows = sb("ws_rows", [P, GROUPS, P])
        wsT = sb("wsT", [P, GROUPS, P])
        wsT_s = sb("wsT_sample", [NS, GROUPS, NS])
        bias, bias_s = sb("gate_bias", [P, GROUPS]), sb("gate_bias_sample", [NS, GROUPS])
        again = sb("subln_gain", [P, VD])
        modp, mods = sb("modp_e", [P, 3, D]), sb("mods_e", [NS, 3, D])
        att, u, v, x, ga, gb = [sb(n, [P, 2, D]) for n in ("att_in", "u_in", "v_in", "x_in", "ga_in", "gb_in")]
        sq = sb("square_e", [P, D])
        aT, sT, mT = [sb(n, [P, KD, P]) for n in ("aT_e", "sT_e", "mT_e")]
        ss, sd, rs = [sb(n, [P, GROUPS]) for n in ("ss_e", "sd_e", "rs_e")]
        ms, rx = sb("ms_e", [P, 1]), sb("rx_e", [P, 1])
        eps = sb("eps_e", [P, 1])
        ps_g, ps_t, ps_a, ps_b = [ctx.enter_context(nc.psum_tensor(n, [P, D], F32)) for n in ("ps_g", "ps_te", "ps_ae", "ps_be")]
        s_in, s_w0, s_ws, s_wsm, s_again = [g.sem("e_" + n) for n in ("inputs", "weights", "ws_turned", "ws_masked", "gain")]
        s_ld = [g.sem(f"e_rows{b}") for b in range(2)]
        s_st = [g.sem(f"e_stored{b}") for b in range(2)]
        s_sqa, s_ss, s_sd, s_rs, s_an, s_a, s_gt, s_so, s_t, s_tc, s_pa, s_pb, s_gm, s_m, s_w, s_gx, s_x2, s_ms, s_sx, s_rx, s_hn, s_h2 = [
            g.sem("e_" + n) for n in ("att_square", "att_sumsq", "att_std", "att_rstd", "att_normed", "a", "gated", "s_out",
                                      "turned", "turned_copied", "product_a", "product_b", "gate_products", "mix_in", "product_o",
                                      "gated_mix", "x2", "mean_square", "std", "rstd", "normed", "h2")]
        s_zero = g.sem("e_zeroed")
        NIN = 16 * (5 + 3 + 3 * NSEQ + (NDEC + 1) * NSEQ)

        def schedule(eng, prepare, products, finish):
            prepare(0, 0)

            def around(t, par):
                products(t, par)
                prepare(t + 1, 1 - par)
                finish(t, par)
            with eng.Fori(0, PT // 2 - 1) as i:
                around(i * 2, 0)
                around(i * 2 + 1, 1)
            around(PT - 2, 0)
            around(PT - 1, 1)
            products(PT, 0)
            finish(PT, 0)

        def rows(t):
            return NS if isinstance(t, int) and t == PT else P

        def use_a(t):
            return 1 if isinstance(t, int) and t == 0 else t * 3

        def use_m(t):
            return t * 3 + (3 if isinstance(t, int) and t == PT else 5)

        def nothing(t, par):
            pass
        with nc.Block() as block:
            @block.sync
            def _(sp):
                sp.dma_start(ws_rows[:], g.gm_ws.rearrange("g i j -> i g j")).then_inc(s_in, 16)
                sp.dma_start(ident[:], g.ident).then_inc(s_in, 16)
                sp.dma_start(lower[:], g.lower_T).then_inc(s_in, 16)
                sp.dma_start(again[:], g.subln_g.broadcast_to([P, VD])).then_inc(s_in, 16)
                sp.dma_start(bias[:], g.gm_bs.rearrange("g i -> i g"), allow_slow_non_contiguous=True).then_inc(s_in, 16)
                for n in range(3):
                    cols = slice((2 + n) * D, (3 + n) * D)
                    sp.dma_start(modp[:, n, :], g.mod[0:1, cols].broadcast_to([P, D])).then_inc(s_in, 16)
                    for q in range(NSEQ):
                        sp.dma_start(mods[q * NDEC:(q + 1) * NDEC, n, :],
                                     g.mod[1 + q:2 + q, cols].broadcast_to([NDEC, D])).then_inc(s_in, 16)
                sp.wait_ge(s_zero, 2)
                for q in range(NSEQ):
                    b = slice(q * NDEC, (q + 1) * NDEC)
                    for i in range(NDEC):
                        sp.dma_start(wsT_s[b, :, q * NDEC + i], g.gm_ws[:, i, 0:NDEC].rearrange("g j -> j g"),
                                     allow_slow_non_contiguous=True).then_inc(s_in, 16)
                    sp.dma_start(bias_s[b, :], g.gm_bs[:, 0:NDEC].rearrange("g i -> i g"),
                                 allow_slow_non_contiguous=True).then_inc(s_in, 16)

                def load(t, par):
                    r = rows(t)
                    src = lambda a, c: a[t * P:t * P + r, c:c + D] if isinstance(t, int) else a[bass.ds(t * P, P), c:c + D]
                    for dst, a, c in ((att, g.att, 0), (v, g.z, ZGV), (u, g.z, ZU), (ga, g.z, ZGA), (gb, g.z, ZGB)):
                        sp.dma_start(dst[0:r, par, :], src(a, c)).then_inc(s_ld[par], 16)
                    xs = g.x_sample if isinstance(t, int) and t == PT else src(g.x_prompt, 0)
                    sp.dma_start(x[0:r, par, :], xs).then_inc(s_ld[par], 16)

                def store(t, par):
                    r = rows(t)
                    dst = lambda a: a[t * P:t * P + r, :] if isinstance(t, int) else a[bass.ds(t * P, P), :]
                    sp.wait_ge(s_h2, t + 1)
                    sp.dma_start(dst(g.x2), x[0:r, par, :]).then_inc(s_st[par], 16)
                    sp.dma_start(dst(g.h2), ga[0:r, par, :]).then_inc(s_st[par], 16)
                    sp.wait_ge(s_st[par], (t - par) * 16 + 32)
                load(0, 0)
                for n, (dst, src) in enumerate(((w_att, g.w_att_out), (w_gm, g.w_gm_out), (w_o, g.w_out))):
                    sp.dma_start(dst[:], src.rearrange("(k p) n -> p k n", p=P)).then_inc(s_w0, 16)
                load(1, 1)
                with sp.Fori(0, PT // 2 - 1) as i:
                    for par in range(2):
                        store(i * 2 + par, par)
                        load(i * 2 + (par + 2), par)
                store(PT - 2, 0)
                load(PT, 0)
                store(PT - 1, 1)
                store(PT, 0)

            @block.gpsimd
            def _(pool):
                nc.gpsimd.memset(wsT_s[:], 0.0).then_inc(s_zero, 1)
                nc.gpsimd.memset(eps[:], EPS).then_inc(s_zero, 1)

            @block.tensor
            def _(pe):
                pe.wait_ge(s_in, NIN)
                for q in range(GROUPS):
                    last = nc.tensor.transpose(ps_g[:, q * P:(q + 1) * P], ws_rows[:, q, :], ident[:])
                last.then_inc(s_ws, 1)
                pe.wait_ge(s_wsm, 2)

                def turn(dst_r, src, count):
                    for k in range(KD):
                        last = nc.tensor.transpose(ps_t[:, k * P:k * P + dst_r], src[:, k * P:(k + 1) * P], ident[0:dst_r, 0:dst_r])
                    last.then_inc(s_t, 1)

                def product(ps, r, lT, w, sem):
                    for c in range(0, D, CB):
                        for k in range(KD):
                            last = nc.tensor.matmul(ps[0:r, c:c + CB], lT[:, k, 0:r], w[:, k, c:c + CB], start=k == 0, stop=k == KD - 1)
                    last.then_inc(sem, 1)

                def prepare(t, par):
                    r = rows(t)
                    pe.wait_ge(s_ld[par], (t - par) * 48 + 96)
                    wait_if_any(pe, s_x2, t)
                    for q in range(GROUPS):
                        lhs = wsT[:, q, :] if r == P else wsT_s[:, q, :]
                        last = nc.tensor.matmul(ps_g[0:r, q * P:(q + 1) * P], lhs, v[0:r, par, q * P:(q + 1) * P], start=True, stop=True)
                    last.then_inc(s_gt, 1)
                    pe.wait_ge(s_a, t + 1)
                    wait_if_any(pe, s_tc, use_a(t) - 1)
                    turn(r, att[0:r, par, :], None)
                    pe.wait_ge(s_so, t + 1)
                    pe.wait_ge(s_tc, use_a(t))
                    turn(r, u[0:r, par, :], None)

                def products(t, par):
                    r = rows(t)
                    pe.wait_ge(s_tc, t * 3 + 2)
                    product(ps_a, r, aT, w_att, s_pa)
                    product(ps_b, r, sT, w_gm, s_pb)

                def finish(t, par):
                    r = rows(t)
                    at = use_m(t)
                    pe.wait_ge(s_m, t + 1)
                    pe.wait_ge(s_tc, at - 1)
                    turn(r, ga[0:r, par, :], None)
                    pe.wait_ge(s_tc, at)
                    product(ps_g, r, mT, w_o, s_w)
                pe.wait_ge(s_w0, 48)
                schedule(pe, prepare, products, finish)

            @block.scalar
            def _(act):
                act.wait_ge(s_in, NIN)
                act.wait_ge(s_zero, 2)

                def copy_turned(dst, r, at):
                    act.wait_ge(s_t, at)
                    nc.scalar.activation(dst[:, :, 0:r], ps_t[:].rearrange("p (k c) -> p k c", c=P)[:, :, 0:r], ACT.Copy).then_inc(s_tc, 1)

                def prepare(t, par):
                    r = rows(t)
                    act.wait_ge(s_ld[par], (t - par) * 48 + 96)
                    nc.scalar.activation(sq[0:r, :], att[0:r, par, :], ACT.Square).then_inc(s_sqa, 1)
                    act.wait_ge(s_ss, t + 1)
                    nc.scalar.activation(sd[0:r, :], ss[0:r, :], ACT.Sqrt, bias=eps[0:r, :], scale=1.0 / VD).then_inc(s_sd, 1)
                    wait_if_any(act, s_pa, t)
                    copy_turned(aT, r, use_a(t))
                    wait_if_any(act, s_pb, t)
                    copy_turned(sT, r, use_a(t) + 1)

                def finish(t, par):
                    r = rows(t)
                    copy_turned(mT, r, use_m(t))
                    act.wait_ge(s_x2, t + 2)
                    nc.scalar.activation(sq[0:r, :], x[0:r, par, :], ACT.Square, accum_out=ms[0:r, :]).then_inc(s_ms, 1)
                    act.wait_ge(s_ms, t + 1)
                    nc.scalar.activation(ms[0:r, :], ms[0:r, :], ACT.Sqrt, bias=eps[0:r, :], scale=1.0 / D).then_inc(s_sx, 1)
                schedule(act, prepare, nothing, finish)

            @block.vector
            def _(dve):
                dve.sem_inc(s_x2, 1)
                dve.wait_ge(s_in, NIN)
                dve.wait_ge(s_ws, 1)
                lowb = lower[:].unsqueeze(1).broadcast_to([P, GROUPS, P])
                nc.vector.tensor_tensor(wsT[:], ps_g[:].rearrange("p (g c) -> p g c", c=P), lowb, ALU.mult).then_inc(s_wsm, 1)
                lows = lower[0:NS, 0:NS].unsqueeze(1).broadcast_to([NS, GROUPS, NS])
                nc.vector.tensor_tensor(wsT_s[:], wsT_s[:], lows, ALU.mult).then_inc(s_wsm, 1)
                nc.vector.tensor_scalar(again[:], again[:], 1.0 - LAMBDA_INIT, None, ALU.mult).then_inc(s_again, 1)
                dve.wait_ge(s_again, 1)

                def normed_attention(t, par):
                    r = rows(t)
                    dve.wait_ge(s_sqa, t + 1)
                    nc.vector.tensor_reduce(ss[0:r, :], sq[0:r, :].rearrange("p (h c) -> p h c", c=VD), AX.X, ALU.add).then_inc(s_ss, 1)
                    dve.wait_ge(s_sd, t + 1)
                    nc.vector.reciprocal(rs[0:r, :], sd[0:r, :]).then_inc(s_rs, 1)
                    dve.wait_ge(s_rs, t + 1)
                    a3 = att[0:r, par, :].rearrange("p (h c) -> p h c", c=VD)
                    nc.vector.tensor_tensor(a3, a3, rs[0:r, :].unsqueeze(2).broadcast_to([r, H, VD]), ALU.mult).then_inc(s_an, 1)
                    dve.wait_ge(s_an, t + 1)
                    nc.vector.tensor_tensor(a3, a3, again[0:r, :].unsqueeze(1).broadcast_to([r, H, VD]), ALU.mult).then_inc(s_a, 1)

                def gated(t, par):
                    r = rows(t)
                    dve.wait_ge(s_gt, t + 1)
                    b = bias if r == P else bias_s
                    for q in range(GROUPS):
                        cols = slice(q * P, (q + 1) * P)
                        last = nc.vector.scalar_tensor_tensor(out=u[0:r, par, cols], in0=ps_g[0:r, cols], scalar=b[0:r, q:q + 1],
                                                              in1=u[0:r, par, cols], op0=ALU.add, op1=ALU.mult)
                    last.then_inc(s_so, 1)

                def mix_input(t, par):
                    r = rows(t)
                    dve.wait_ge(s_pa, t + 1)
                    nc.vector.tensor_tensor(ga[0:r, par, :], ga[0:r, par, :], ps_a[0:r, :], ALU.mult)
                    dve.wait_ge(s_pb, t + 1)
                    nc.vector.tensor_tensor(gb[0:r, par, :], gb[0:r, par, :], ps_b[0:r, :], ALU.mult).then_inc(s_gm, 1)
                    dve.wait_ge(s_gm, t + 1)
                    nc.vector.tensor_tensor(ga[0:r, par, :], ga[0:r, par, :], gb[0:r, par, :], ALU.add).then_inc(s_m, 1)

                def prepare(t, par):
                    if isinstance(t, int) and t == 0:
                        normed_attention(t, par)
                        gated(t, par)
                    else:
                        gated(t, par)

                def products(t, par):
                    if not (isinstance(t, int) and t == PT):
                        normed_attention(t + 1, 1 - par)
                    mix_input(t, par)

                def finish(t, par):
                    r = rows(t)
                    m = modp if r == P else mods
                    dve.wait_ge(s_w, t + 1)
                    nc.vector.tensor_tensor(gb[0:r, par, :], ps_g[0:r, :], m[0:r, 0, :], ALU.mult).then_inc(s_gx, 1)
                    dve.wait_ge(s_gx, t + 1)
                    nc.vector.tensor_tensor(x[0:r, par, :], x[0:r, par, :], gb[0:r, par, :], ALU.add).then_inc(s_x2, 1)
                    dve.wait_ge(s_sx, t + 1)
                    nc.vector.reciprocal(rx[0:r, :], ms[0:r, :]).then_inc(s_rx, 1)
                    dve.wait_ge(s_rx, t + 1)
                    nc.vector.scalar_tensor_tensor(out=ga[0:r, par, :], in0=x[0:r, par, :], scalar=rx[0:r, :], in1=m[0:r, 2, :],
                                                   op0=ALU.mult, op1=ALU.mult).then_inc(s_hn, 1)
                    dve.wait_ge(s_hn, t + 1)
                    nc.vector.tensor_tensor(ga[0:r, par, :], ga[0:r, par, :], m[0:r, 1, :], ALU.add).then_inc(s_h2, 1)
                schedule(dve, prepare, products, finish)


def routing_phase(nc, g):
    HP = 2 * PH
    QW = HP * P
    LOWEST = -3.4e38
    with ExitStack() as ctx:
        sb = lambda name, shape, dt=F32: ctx.enter_context(nc.sbuf_tensor(name, shape, dt))
        ident, iota = sb("ident_f", [P, P]), sb("iota16", [P, TOPK])
        wq = sb("w_query", [P, KD, QW])
        keys = sb("subkeys", [P, HP, P])
        keysT = sb("subkeysT", [P, HP, P])
        h2 = sb("h2_rows", [P, 2, D])
        h2T = sb("h2T", [P, KD, P])
        q = sb("query", [P, QW])
        qT = sb("queryT", [P, HP, P])
        sc = sb("scores", [P, HP, NKEYS])
        rest = sb("scores_rest", [P, HP, NKEYS])
        top = sb("half_top", [P, HP, TOPK])
        topi, topf = sb("half_top_i", [P, HP, TOPK], U32), sb("half_top_f", [P, HP, TOPK])
        best, besti = sb("best", [P, PH, TOPK]), sb("best_i", [P, PH, TOPK], U32)
        part, partf = sb("best_part", [P, 2, SLOTS], U32), sb("best_part_f", [P, 2, SLOTS])
        key = sb("best_key", [P, 2, SLOTS])
        total, rec = sb("gate_sum", [P, PH]), sb("gate_rec", [P, PH])
        ps_t = ctx.enter_context(nc.psum_tensor("ps_tf", [P, D], F32))
        ps_q = ctx.enter_context(nc.psum_tensor("ps_qf", [P, D], F32))
        ps_s = ctx.enter_context(nc.psum_tensor("ps_sf", [P, QW], F32))
        s_in, s_kt, s_ktc, s_ht, s_htc, s_q, s_qc, s_qt, s_qtc, s_s, s_sc, s_ch, s_df, s_ex = [
            g.sem("f_" + n) for n in ("inputs", "keys_turned", "keysT", "h2_turned", "h2T", "query_half", "query_copied",
                                      "query_turned", "queryT", "scores", "scores_copied", "chain", "gate_difference", "gate_exp")]
        s_ld = [g.sem(f"f_rows{b}") for b in range(2)]
        s_rec, s_gate, s_pass = g.sem("f_gate_rec"), g.sem("f_gates"), g.sem("f_vector_passed")

        def rows(t):
            return NS if isinstance(t, int) and t == PT else P

        def tiles(eng, body):
            with eng.Fori(0, PT // 2) as i:
                body(i * 2, 0)
                body(i * 2 + 1, 1)
            body(PT, 0)
        with nc.Block() as block:
            @block.sync
            def _(sp):
                sp.dma_start(keys[:], g.subkeys.rearrange("n k d -> k n d")).then_inc(s_in, 16)
                sp.dma_start(ident[:], g.ident).then_inc(s_in, 16)
                sp.dma_start(iota[:], g.iota16.broadcast_to([P, TOPK])).then_inc(s_in, 16)
                sp.dma_start(wq[:], g.peer_w_q.rearrange("(k p) n -> p k n", p=P)).then_inc(s_in, 16)

                def load(t, par):
                    r = rows(t)
                    src = g.h2[t * P:t * P + r, :] if isinstance(t, int) else g.h2[bass.ds(t * P, P), :]
                    sp.dma_start(h2[0:r, par, :], src).then_inc(s_ld[par], 16)
                load(0, 0)
                load(1, 1)
                with sp.Fori(0, PT // 2 - 1) as i:
                    for par in range(2):
                        sp.wait_ge(s_ht, i * 2 + (par + 1))
                        load(i * 2 + (par + 2), par)
                sp.wait_ge(s_ht, PT - 1)
                load(PT, 0)

            @block.tensor
            def _(pe):
                pe.wait_ge(s_in, 64)
                for n in range(2):
                    if n:
                        pe.wait_ge(s_ktc, 1)
                    for k in range(KD):
                        last = nc.tensor.transpose(ps_t[:, k * P:(k + 1) * P], keys[:, n * KD + k, :], ident[:])
                    last.then_inc(s_kt, 1)
                pe.wait_ge(s_ktc, 2)

                def body(t, par):
                    r = rows(t)
                    pe.wait_ge(s_ld[par], (t - par) * 8 + 16)
                    wait_if_any(pe, s_qtc, t * 2 + 2)
                    for k in range(KD):
                        last = nc.tensor.transpose(ps_t[:, k * P:k * P + r], h2[0:r, par, k * P:(k + 1) * P], ident[0:r, 0:r])
                    last.then_inc(s_ht, 1)
                    pe.wait_ge(s_htc, t + 1)
                    for n in range(2):
                        pe.wait_ge(s_qc, t * 2 + (n + 1))
                        for c in range(0, D, CB):
                            for k in range(KD):
                                last = nc.tensor.matmul(ps_q[0:r, c:c + CB], h2T[:, k, 0:r], wq[:, k, n * D + c:n * D + c + CB],
                                                        start=k == 0, stop=k == KD - 1)
                        last.then_inc(s_q, 1)
                    for n in range(2):
                        pe.wait_ge(s_qc, t * 2 + (n + 2))
                        if n:
                            pe.wait_ge(s_qtc, t * 2 + 3)
                        for k in range(KD):
                            last = nc.tensor.transpose(ps_t[:, k * P:k * P + r], q[0:r, (n * KD + k) * P:(n * KD + k + 1) * P], ident[0:r, 0:r])
                        last.then_inc(s_qt, 1)
                    pe.wait_ge(s_qtc, t * 2 + 4)
                    pe.wait_ge(s_sc, t + 1)
                    for n in range(HP):
                        last = nc.tensor.matmul(ps_s[0:r, n * P:(n + 1) * P], qT[:, n, 0:r], keysT[:, n, :], start=True, stop=True)
                    last.then_inc(s_s, 1)
                tiles(pe, body)

            @block.scalar
            def _(act):
                act.sem_inc(s_qtc, 2)
                act.sem_inc(s_qc, 1)
                act.sem_inc(s_sc, 1)
                for n in range(2):
                    act.wait_ge(s_kt, n + 1)
                    nc.scalar.activation(keysT[:, n * KD:(n + 1) * KD, :].rearrange("p k c -> p (k c)"), ps_t[:], ACT.Copy).then_inc(s_ktc, 1)
                turned = ps_t[:].rearrange("p (k c) -> p k c", c=P)

                def body(t, par):
                    r = rows(t)
                    act.wait_ge(s_ht, t + 1)
                    nc.scalar.activation(h2T[:, :, 0:r], turned[:, :, 0:r], ACT.Copy).then_inc(s_htc, 1)
                    for n in range(2):
                        act.wait_ge(s_q, t * 2 + (n + 1))
                        nc.scalar.activation(q[0:r, n * D:(n + 1) * D], ps_q[0:r, :], ACT.Copy).then_inc(s_qc, 1)
                    for n in range(2):
                        act.wait_ge(s_qt, t * 2 + (n + 1))
                        nc.scalar.activation(qT[:, n * KD:(n + 1) * KD, 0:r], turned[:, :, 0:r], ACT.Copy).then_inc(s_qtc, 1)
                    act.wait_ge(s_s, t + 1)
                    act.wait_ge(s_df, t + 1)
                    nc.scalar.activation(sc[0:r].rearrange("p n c -> p (n c)"), ps_s[0:r, :], ACT.Copy).then_inc(s_sc, 1)
                    act.wait_ge(s_df, t + 2)
                    nc.scalar.activation(best[0:r], best[0:r], ACT.Exp).then_inc(s_ex, 1)
                tiles(act, body)

            @block.vector
            def _(dve):
                dve.sem_inc(s_df, 1)
                dve.wait_ge(s_in, 64)
                CH = 20

                def body(t, par):
                    r = rows(t)
                    c = [0]

                    def link(ins):
                        c[0] += 1
                        ins.then_inc(s_ch, 1)
                        wait_apart(dve, s_ch, t * CH + c[0], s_pass)
                    a8, b8 = slice(0, 8), slice(8, 16)
                    wait_apart(dve, s_sc, t + 2, s_pass)
                    each = lambda n, f: [f(k) for k in range(n)][-1]
                    link(each(HP, lambda k: nc.vector.max(top[0:r, k, a8], sc[0:r, k, :])))
                    link(each(HP, lambda k: nc.vector.match_replace(out=rest[0:r, k, :], in_to_replace=top[0:r, k, a8],
                                                                    in_values=sc[0:r, k, :], imm_value=LOWEST)))
                    link(each(HP, lambda k: nc.vector.max(top[0:r, k, b8], rest[0:r, k, :])))
                    each(HP, lambda k: nc.vector.max_index(topi[0:r, k, a8], top[0:r, k, a8], sc[0:r, k, :]))
                    link(each(HP, lambda k: nc.vector.max_index(topi[0:r, k, b8], top[0:r, k, b8], rest[0:r, k, :])))
                    link(nc.vector.tensor_copy(topf[0:r], topi[0:r]))
                    half = top[0:r].rearrange("p (h m) k -> p h m k", m=2)
                    cand = sc[0:r].rearrange("p n c -> p (n c)").rearrange("p (h a b) -> p h a b", h=PH, a=TOPK)
                    link(nc.vector.tensor_tensor(cand, half[:, :, 0, :].unsqueeze(3).broadcast_to([r, PH, TOPK, TOPK]),
                                                 half[:, :, 1, :].unsqueeze(2).broadcast_to([r, PH, TOPK, TOPK]), ALU.add))
                    cf = sc[0:r].rearrange("p (h m) c -> p h (m c)", m=2)
                    rf = rest[0:r].rearrange("p (h m) c -> p h (m c)", m=2)
                    link(each(PH, lambda k: nc.vector.max(best[0:r, k, a8], cf[:, k, :])))
                    link(each(PH, lambda k: nc.vector.match_replace(out=rf[:, k, :], in_to_replace=best[0:r, k, a8],
                                                                    in_values=cf[:, k, :], imm_value=LOWEST)))
                    link(each(PH, lambda k: nc.vector.max(best[0:r, k, b8], rf[:, k, :])))
                    each(PH, lambda k: nc.vector.max_index(besti[0:r, k, a8], best[0:r, k, a8], cf[:, k, :]))
                    link(each(PH, lambda k: nc.vector.max_index(besti[0:r, k, b8], best[0:r, k, b8], rf[:, k, :])))
                    bi = besti[0:r].rearrange("p h k -> p (h k)")
                    nc.vector.tensor_scalar(part[0:r, 0, :], bi, 4, None, ALU.logical_shift_right)
                    link(nc.vector.tensor_scalar(part[0:r, 1, :], bi, TOPK - 1, None, ALU.bitwise_and))
                    link(nc.vector.tensor_copy(partf[0:r], part[0:r]))
                    tf = topf[0:r].rearrange("p (h m) k -> p h m k", m=2)
                    hot = cand
                    pick = rest[0:r].rearrange("p n c -> p (n c)").rearrange("p (h a b) -> p h a b", h=PH, a=TOPK)
                    io = iota[0:r].unsqueeze(1).broadcast_to([r, SLOTS, TOPK])
                    hot3 = sc[0:r].rearrange("p n c -> p (n c)").rearrange("p (s b) -> p s b", b=TOPK)
                    pick3 = rest[0:r].rearrange("p n c -> p (n c)").rearrange("p (s b) -> p s b", b=TOPK)
                    for m in range(2):
                        link(nc.vector.tensor_tensor(hot3, partf[0:r, m, :].unsqueeze(2).broadcast_to([r, SLOTS, TOPK]), io, ALU.is_equal))
                        link(nc.vector.tensor_tensor(pick, hot, tf[:, :, m, :].unsqueeze(2).broadcast_to([r, PH, TOPK, TOPK]), ALU.mult))
                        link(nc.vector.tensor_reduce(key[0:r, m, :], pick3, AX.X, ALU.add))
                    tile = (lambda a: a[0:r, t, :]) if isinstance(t, int) else (lambda a: a[0:r, bass.ds(t, 1), :])
                    flat = lambda x: x if isinstance(t, int) else x.unsqueeze(1)
                    nc.vector.scalar_tensor_tensor(out=tile(g.idx), in0=flat(key[0:r, 0, :]), scalar=float(NKEYS), in1=flat(key[0:r, 1, :]),
                                                   op0=ALU.mult, op1=ALU.add)
                    link(nc.vector.tensor_copy(rec[0:r, :], best[0:r, :, 0]))
                    nc.vector.tensor_tensor(best[0:r], best[0:r], rec[0:r, :].unsqueeze(2).broadcast_to([r, PH, TOPK]),
                                            ALU.subtract).then_inc(s_df, 1)
                    dve.wait_ge(s_ex, t + 1)
                    link(nc.vector.tensor_reduce(total[0:r, :], best[0:r], AX.X, ALU.add))
                    assert c[0] == CH, c
                    nc.vector.reciprocal(rec[0:r, :], total[0:r, :]).then_inc(s_rec, 1)
                    dve.wait_ge(s_rec, t + 1)
                    if isinstance(t, int):
                        dst = g.gate[0:r, t, :].rearrange("p (h k) -> p h k", k=TOPK)
                    else:
                        dst = g.gate[0:r, bass.ds(t, 1), :].rearrange("p o (h k) -> p (o h) k", k=TOPK)
                    nc.vector.tensor_tensor(dst, best[0:r], rec[0:r, :].unsqueeze(2).broadcast_to([r, PH, TOPK]), ALU.mult).then_inc(s_gate, 1)
                tiles(dve, body)


def expert_phase(nc, g):
    R = 16
    CH = 16
    NCH = SLOTS // CH
    HALF = SLOTS // 2
    ND = 8
    QS = P // NS
    KS = SLOTS // QS
    with ExitStack() as ctx:
        sb = lambda name, shape, dt=F32: ctx.enter_context(nc.sbuf_tensor(name, shape, dt))
        ident, ident4 = sb("ident_g", [P, P]), sb("ident_4", [P, NS])
        ur, vr = sb("u_rows", [P, R, D]), sb("v_rows", [P, R, D])
        h2n, h2c = sb("h2_next", [P, D]), sb("h2_now", [P, D])
        x2 = sb("x2_rows", [P, D])
        y = sb("y_rows", [P, D])
        g2p, g2s = sb("gate2_prompt", [P, D]), sb("gate2_sample", [NS, D])
        idx = sb("idx_now", [P, 2, HALF], U32)
        idx_s, gate_s = sb("idx_sample", [P, KS], U32), sb("gate_sample", [P, KS])
        a, ge, w = sb("a_now", [P, SLOTS]), sb("gelu_now", [P, SLOTS]), sb("w_now", [P, SLOTS])
        diag = sb("diag", [P, ND, P])
        ps_y = ctx.enter_context(nc.psum_tensor("ps_y", [P, D], F32))
        s_in, s_hc, s_u, s_ge, s_w, s_dg, s_v, s_gy, s_y, s_yfree, s_pk = [
            g.sem("g_" + n) for n in ("inputs", "h2_now", "dots", "gelu", "weights", "diagonal", "added", "gated", "y",
                                      "y_free", "sample_packed")]
        s_h, s_x, s_st = [g.sem("g_" + n) for n in ("h2_loaded", "x2_loaded", "y_stored")]
        s_ix = [g.sem(f"g_index{n}") for n in range(2)]
        s_ur = [g.sem(f"g_u_rows{j}") for j in range(R)]
        s_vr = [g.sem(f"g_v_rows{j}") for j in range(R)]
        s_pass = g.sem("g_pool_passed")
        LAPS = SLOTS // R

        def tiles(eng, body):
            with eng.Fori(0, PT) as t:
                body(t, SLOTS, P)
            body(PT, KS, NS)
        with nc.Block() as block:
            @block.sync
            def _(sp):
                sp.dma_start(ident[:], g.ident).then_inc(s_in, 16)
                sp.dma_start(ident4[:], g.ident4).then_inc(s_in, 16)
                cols = slice(5 * D, 6 * D)
                sp.dma_start(g2p[:], g.mod[0:1, cols].broadcast_to([P, D])).then_inc(s_in, 16)
                for q in range(NSEQ):
                    sp.dma_start(g2s[q * NDEC:(q + 1) * NDEC, :], g.mod[1 + q:2 + q, cols].broadcast_to([NDEC, D])).then_inc(s_in, 16)
                sp.dma_start(h2n[:], g.h2[0:P, :]).then_inc(s_h, 16)
                sp.sem_inc(s_yfree, 1)

                def y_rows(t, dst):
                    sp.wait_ge(s_y, t + 1)
                    sp.dma_start(dst, y[:]).then_inc(s_st, 16)
                    sp.wait_ge(s_st, t * 16 + 16)
                    sp.sem_inc(s_yfree, 1)
                with sp.Fori(0, PT - 1) as t:
                    sp.dma_start(x2[:], g.x2[bass.ds(t * P, P), :]).then_inc(s_x, 16)
                    sp.wait_ge(s_hc, t + 1)
                    sp.dma_start(h2n[:], g.h2[bass.ds(t * P + P, P), :]).then_inc(s_h, 16)
                    y_rows(t, g.y_p[bass.ds(t * P, P), :])
                sp.dma_start(x2[:], g.x2[NP - P:NP, :]).then_inc(s_x, 16)
                sp.wait_ge(s_hc, PT)
                for n in range(QS):
                    sp.dma_start(h2n[n * NS:(n + 1) * NS, :], g.h2[NP:NT, :]).then_inc(s_h, 16)
                y_rows(PT - 1, g.y_p[NP - P:NP, :])
                sp.dma_start(x2[0:NS, :], g.x2[NP:NT, :]).then_inc(s_x, 16)
                sp.wait_ge(s_y, PT + 1)
                sp.dma_start(g.y_s, y[0:NS, :]).then_inc(s_st, 16)
                sp.wait_ge(s_st, 16 * (PT + 1))

            @block.gpsimd
            def _(pool):
                def body(t, slots, r):
                    def gather(ring, sems, table, s, freed, ahead):
                        col = idx[:, s // HALF, s % HALF:s % HALF + 1] if slots == SLOTS else idx_s[:, s:s + 1]
                        wait_apart(pool, freed, t * SLOTS + (s + 1 - R + ahead), s_pass)
                        pool.indirect_dma_start(ring[:, s % R, :], None, table,
                                                bass.IndirectOffsetOnAxis(ap=col, axis=0)).then_inc(sems[s % R], 16)
                    for s in range(slots + CH):
                        if slots == SLOTS and s in (0, 2 * CH):
                            n = 0 if s == 0 else 1
                            pool.wait_ge(s_v, t * SLOTS + (1 if n == 0 else HALF))
                            nc.gpsimd.tensor_copy(idx[:, n, :], g.idx[:, bass.ds(t, 1), n * HALF:(n + 1) * HALF]
                                                  .rearrange("p o s -> p (o s)")).then_inc(s_ix[n], 1)
                            wait_apart(pool, s_ix[n], t + 1, s_pass)
                        if s < slots:
                            gather(ur, s_ur, g.peer_u, s, s_u, R)
                        if s >= CH:
                            gather(vr, s_vr, g.peer_v, s - CH, s_v, HALF)

                wait_apart(pool, s_pk, 2 * QS, s_pass)
                tiles(pool, body)

            @block.vector
            def _(dve):
                dve.sem_inc(s_u, R)
                dve.sem_inc(s_gy, 1)
                dve.wait_ge(s_in, 16 * (3 + NSEQ))
                for n in range(QS):
                    nc.vector.tensor_copy(idx_s[n * NS:(n + 1) * NS, :], g.idx[0:NS, PT, n * KS:(n + 1) * KS]).then_inc(s_pk, 1)
                    nc.vector.tensor_copy(gate_s[n * NS:(n + 1) * NS, :], g.gate[0:NS, PT, n * KS:(n + 1) * KS]).then_inc(s_pk, 1)
                dve.wait_ge(s_pk, 2 * QS)

                def body(t, slots, r):
                    dve.wait_ge(s_h, t * 16 + (16 if slots == SLOTS else 16 * QS))
                    nc.vector.tensor_copy(h2c[:], h2n[:]).then_inc(s_hc, 1)
                    dve.wait_ge(s_hc, t + 1)
                    for c in range(slots // CH):
                        for s in range(c * CH, (c + 1) * CH):
                            dve.wait_ge(s_ur[s % R], t * (16 * LAPS) + 16 * (s // R + 1))
                            nc.vector.tensor_tensor_reduce(ur[:, s % R, :], ur[:, s % R, :], h2c[:], 1.0, 0.0, ALU.mult, ALU.add,
                                                           a[:, s:s + 1]).then_inc(s_u, 1)
                        cols = slice(c * CH, (c + 1) * CH)
                        dve.wait_ge(s_ge, t * NCH + (c + 1))
                        if slots == SLOTS:
                            gt = g.gate[:, bass.ds(t, 1), cols].rearrange("p o s -> p (o s)")
                        else:
                            gt = gate_s[:, cols]
                        nc.vector.tensor_tensor(w[:, cols], ge[:, cols], gt, ALU.mult).then_inc(s_w, 1)
                    dve.wait_ge(s_v, t * SLOTS + (slots + HALF))
                    dve.wait_ge(s_x, t * 16 + 16)
                    dve.wait_ge(s_yfree, t + 1)
                    m = g2p if slots == SLOTS else g2s
                    nc.vector.tensor_tensor(y[0:r, :], ps_y[0:r, :], m[0:r, :], ALU.mult).then_inc(s_gy, 1)
                    dve.wait_ge(s_gy, t + 2)
                    nc.vector.tensor_tensor(y[0:r, :], y[0:r, :], x2[0:r, :], ALU.add).then_inc(s_y, 1)
                tiles(dve, body)

            @block.scalar
            def _(act):
                act.wait_ge(s_in, 16 * (3 + NSEQ))

                def body(t, slots, r):
                    base = ident[:, 0:P] if slots == SLOTS else ident4[:]
                    for c in range(slots // CH):
                        cols = slice(c * CH, (c + 1) * CH)
                        act.wait_ge(s_u, t * SLOTS + ((c + 1) * CH + R))
                        nc.scalar.activation(ge[:, cols], a[:, cols], ACT.Gelu).then_inc(s_ge, 1)
                        act.wait_ge(s_w, t * NCH + (c + 1))
                        for s in range(c * CH, (c + 1) * CH):
                            act.wait_ge(s_v, t * SLOTS + (s + 1 - ND + HALF))
                            nc.scalar.activation(diag[:, s % ND, 0:r], base, ACT.Copy, scale=w[:, s:s + 1]).then_inc(s_dg, 1)
                tiles(act, body)

            @block.tensor
            def _(pe):
                pe.sem_inc(s_v, HALF)

                def body(t, slots, r):
                    for s in range(slots):
                        if s == 0:
                            pe.wait_ge(s_gy, t + 1)
                        pe.wait_ge(s_vr[s % R], t * (16 * LAPS) + 16 * (s // R + 1))
                        pe.wait_ge(s_dg, t * SLOTS + (s + 1))
                        for c in range(0, D, CB):
                            last = nc.tensor.matmul(ps_y[0:r, c:c + CB], diag[:, s % ND, 0:r], vr[:, s % R, c:c + CB],
                                                    start=s == 0, stop=s == slots - 1)
                        last.then_inc(s_v, 1)
                tiles(pe, body)


def output_phase(nc, g):
    s = g.sem("outputs_copied")
    with nc.Block() as block:
        @block.sync
        def _(sp):
            sp.dma_start(g.o_kp, g.z[0:NP, ZK:ZK + D]).then_inc(s, 16)
            sp.dma_start(g.o_vp, g.z[0:NP, ZV:ZV + D]).then_inc(s, 16)
            sp.dma_start(g.o_ks, g.z[NP:NT, ZK:ZK + D]).then_inc(s, 16)
            sp.dma_start(g.o_vs, g.z[NP:NT, ZV:ZV + D]).then_inc(s, 16)
            sp.dma_start(g.o_gv, g.z[NP:NT, ZGV:ZGV + D]).then_inc(s, 16)
            sp.wait_ge(s, 80)


def build(nc, ins, outs):
    g = Shared()
    with ExitStack() as ctx:
        used = []

        def sem(name):
            used.append(nc.alloc_semaphore(name=name))
            return used[-1]

        def run(phase):
            phase(nc, g)
            nc.clear_and_free_semaphores(used)
            nc.all_engine_barrier()
            used.clear()
        g.sem = sem
        g.c_prompt = ins["c_prompt"]
        g.c_sample = ins["c_sample"]
        g.page_table = ins["page_table"]
        g.ident = ins["ident"]
        g.rope = ins["rope"]
        g.mask = ins["mask"]
        g.new_mask = ins["new_mask"]
        g.prow = ins["prow"]
        g.b_ada = ins["b_ada"]
        g.norm1_g = ins["norm1_g"]
        g.norm2_g = ins["norm2_g"]
        g.q_norm_g = ins["q_norm_g"]
        g.k_norm_g = ins["k_norm_g"]
        g.subln_g = ins["subln_g"]
        g.gm_v_norm_g = ins["gm_v_norm_g"]
        g.lambda_q1 = ins["lambda_q1"]
        g.lambda_k1 = ins["lambda_k1"]
        g.lambda_q2 = ins["lambda_q2"]
        g.lambda_k2 = ins["lambda_k2"]
        g.lower_T = ins["lower_T"]
        g.ident4 = ins["ident4"]
        g.iota16 = ins["iota16"]
        g.w_ada = ins["w_ada"].rearrange("a p n -> (a p) n")
        g.w_in = ins["w_in"].rearrange("a p n -> (a p) n")
        g.w_att_out = ins["w_att_out"].rearrange("a p n -> (a p) n")
        g.w_gm_out = ins["w_gm_out"].rearrange("a p n -> (a p) n")
        g.w_out = ins["w_out"].rearrange("a p n -> (a p) n")
        g.peer_w_q = ins["peer_w_q"].rearrange("a p n -> (a p) n")
        g.peer_u = ins["peer_u"].rearrange("a p n -> (a p) n")
        g.peer_v = ins["peer_v"].rearrange("a p n -> (a p) n")
        g.x_prompt = ins["x_prompt"].rearrange("b t d -> (b t) d")
        g.x_sample = ins["x_sample"].rearrange("b t d -> (b t) d")
        g.y_p = outs[0].rearrange("b t d -> (b t) d")
        g.y_s = outs[1].rearrange("b t d -> (b t) d")
        g.o_kp = outs[2].rearrange("a b t h m d -> (a b t) (h m d)")
        g.o_vp = outs[3].rearrange("a b t h d -> (a b t) (h d)")
        g.o_ks = outs[4].rearrange("a b t h m d -> (a b t) (h m d)")
        g.o_vs = outs[5].rearrange("a b t h d -> (a b t) (h d)")
        g.o_gv = outs[6].rearrange("a b t d -> (a b t) d")
        g.mod = nc.dram_tensor("scratch_mod", [1 + NSEQ, MODS * D], F32, kind="Internal").ap()
        g.z = nc.dram_tensor("scratch_z", [NT, ZW], F32, kind="Internal").ap()
        g.att = nc.dram_tensor("scratch_att", [NT, D], F32, kind="Internal").ap()
        g.x2 = nc.dram_tensor("scratch_x2", [NT, D], F32, kind="Internal").ap()
        g.h2 = nc.dram_tensor("scratch_h2", [NT, D], F32, kind="Internal").ap()
        g.gm_ws = ins["gm_ws"].rearrange("a g i j -> (a g) i j")
        g.gm_bs = ins["gm_bs"].rearrange("a g i -> (a g) i")
        g.subkeys = ins["peer_subkeys"].rearrange("a h m k d -> (a h m) k d")
        g.lam = ctx.enter_context(nc.sbuf_tensor("lambda", [P, 1], F32))
        g.cache_k = ins["cache_k"].rearrange("a n p h m d -> (a n p) (h m d)")
        g.cache_v = ins["cache_v"].rearrange("a n p h d -> (a n p) (h d)")
        run(adaln_phase)
        run(projection_phase)
        run(prompt_attention_phase)
        run(sample_attention_phase)
        run(mix_phase)
        g.idx = ctx.enter_context(nc.sbuf_tensor("expert_numbers", [P, TILES, SLOTS], U32))
        g.gate = ctx.enter_context(nc.sbuf_tensor("expert_gates", [P, TILES, SLOTS], F32))
        run(routing_phase)
        run(expert_phase)
        run(output_phase)


_INS = ['x_prompt', 'x_sample', 'cache_k', 'cache_v', 'page_table', 'c_prompt', 'c_sample', 'w_ada', 'b_ada', 'norm1_g',
        'w_in', 'q_norm_g', 'k_norm_g', 'lambda_q1', 'lambda_k1', 'lambda_q2', 'lambda_k2', 'subln_g', 'gm_v_norm_g',
        'gm_ws', 'gm_bs', 'w_att_out', 'w_gm_out', 'w_out', 'norm2_g', 'peer_w_q', 'peer_subkeys', 'peer_u', 'peer_v']
_OUTS = [(1, 1024, 1024), (8, 4, 1024), (1, 1, 1024, 8, 2, 64), (1, 1, 1024, 8, 128), (1, 8, 4, 8, 2, 64),
         (1, 8, 4, 8, 128), (1, 8, 4, 1024)]


def _constants():
    import numpy as np
    f = np.float32
    pos = np.concatenate([np.arange(NP), PAST + np.tile(np.arange(NDEC), NSEQ)]).astype(f)
    inv = (f(1.0) / np.power(f(10000.0), np.arange(0, DH, 2, dtype=f) / f(DH))).astype(f)
    ang = (pos[:, None] * inv[None, :]).astype(f)
    cos, sin = np.cos(ang).astype(f), np.sin(ang).astype(f)
    rope = np.stack([np.concatenate([cos, cos], 1), np.concatenate([-sin, sin], 1)], 1)
    upper = np.triu(np.full((P, P), NEG, f), 1)
    new_mask = np.tile(upper[0:NDEC, 0:NDEC], (2 * H, 1))
    return {"ident": np.eye(P, dtype=f), "rope": np.ascontiguousarray(rope), "mask": upper, "new_mask": new_mask,
            "lower_T": np.triu(np.ones((P, P), f)), "ident4": np.tile(np.eye(NS, dtype=f), (P // NS, 1)),
            "iota16": np.arange(TOPK, dtype=f)[None, :], "prow": np.arange(P, dtype=f)[:, None]}


def kernel(**inputs):
    import numpy as _np
    import concourse.bacc as _bacc
    from concourse.bass_utils import run_bass_kernel_spmd as _run

    nc = _bacc.Bacc("TRN2", target_bir_lowering=False, num_devices=1)
    arrays, args = {}, {}
    named = {n: inputs[n] for n in _INS}
    named.update(_constants())
    for name, a in named.items():
        a = _np.ascontiguousarray(a)
        arrays[f"in_{name}"] = a
        args[name] = nc.dram_tensor(f"in_{name}", a.shape, mybir.dt.from_np(a.dtype), kind="ExternalInput").ap()
    outs = [nc.dram_tensor(f"out_{i}", shape, F32, kind="ExternalOutput").ap() for i, shape in enumerate(_OUTS)]
    build(nc, args, outs)
    r = _run(nc, [arrays], core_ids=[0])
    return tuple(r.results[0][f"out_{i}"] for i in range(len(_OUTS)))
```

```python
from contextlib import ExitStack

import concourse.bass as bass
from concourse import mybir

F32 = mybir.dt.float32
F32R = mybir.dt.float32r
U32 = mybir.dt.uint32
I32 = mybir.dt.int32
ALU = mybir.AluOpType
ACT = mybir.ActivationFunctionType
AX = mybir.AxisListType

P = 128
D = 1024
KD = D // P
NP = 1024
PT = NP // P
NSEQ, NDEC = 8, 4
NS = NSEQ * NDEC
NT = NP + NS
TILES = PT + 1
PAST, PAGE = 2048, 128
NPAGES = PAST // PAGE
H, DH, VD = 8, 64, 128
ZW = 7168
ZQ, ZK, ZV, ZU, ZGV, ZGA, ZGB = [D * n for n in range(7)]
CB = 512
MODS = 6
EPS = 1e-6
GROUPS = 8
LAMBDA_INIT = 0.2
PH, NKEYS, TOPK = 8, 128, 16
SLOTS = PH * TOPK
NEG = -1e30


def rows_of(t):
    return P if t < PT else NS


def wait_if_any(eng, sem, value):
    if not isinstance(value, int) or value > 0:
        eng.wait_ge(sem, value)


def wait_apart(eng, sem, value, passed):
    if not isinstance(value, int) or value > 0:
        eng.wait_ge(sem, value)
        eng.sem_inc(passed, 1)


class Shared:
    pass


def adaln_phase(nc, g):
    NC = 1 + NSEQ
    WB = 2
    NB = MODS * D // CB
    with ExitStack() as ctx:
        sb = lambda name, shape, dt=F32: ctx.enter_context(nc.sbuf_tensor(name, shape, dt))
        c_rows = sb("c_rows", [NC, D])
        c_silu = sb("c_silu", [NC, D])
        cT = sb("cT", [P, KD, NC])
        bias = sb("ada_bias", [NC, MODS * D])
        gain = sb("ada_gain", [NC, 2, D])
        mod = sb("mod_rows", [NC, MODS * D])
        ident = sb("ident_a", [P, P])
        w = sb("w_ada_buf", [P, WB, KD, CB])
        lvec = sb("lambda_vectors", [P, 4, DH])
        lprod = sb("lambda_products", [P, 2, DH])
        ldot = sb("lambda_dots", [P, 2])
        ldif = sb("lambda_exp_difference", [P, 1])
        s_ld, s_le, s_lam = [g.sem("a_lambda_" + n) for n in ("dots", "exp", "done")]
        ps_t = ctx.enter_context(nc.psum_tensor("ps_cT", [P, CB], F32))
        ps_m = ctx.enter_context(nc.psum_tensor("ps_mod", [P, 2, CB], F32))
        s_in, s_silu, s_ct, s_ctc, s_mm, s_mod, s_out = [
            g.sem(n) for n in ("a_inputs", "a_silu", "a_cT_psum", "a_cT", "a_product", "a_mod", "a_stored")]
        s_c = g.sem("a_conditioning")
        s_w = [g.sem(f"a_weights{b}") for b in range(WB)]
        w_view = g.w_ada.rearrange("(k p) n -> p k n", p=P)
        with nc.Block() as block:
            @block.sync
            def _(sp):
                sp.dma_start(c_rows[0:1, :], g.c_prompt).then_inc(s_c, 16)
                sp.dma_start(c_rows[1:NC, :], g.c_sample).then_inc(s_c, 16)
                sp.dma_start(ident[:], g.ident).then_inc(s_c, 16)
                sp.dma_start(bias[:], g.b_ada.broadcast_to([NC, MODS * D])).then_inc(s_in, 16)
                sp.dma_start(gain[:, 0, :], g.norm1_g.broadcast_to([NC, D])).then_inc(s_in, 16)
                sp.dma_start(gain[:, 1, :], g.norm2_g.broadcast_to([NC, D])).then_inc(s_in, 16)
                for n, v in enumerate((g.lambda_q1, g.lambda_k1, g.lambda_q2, g.lambda_k2)):
                    sp.dma_start(lvec[:, n, :], v.broadcast_to([P, DH])).then_inc(s_in, 16)
                sp.wait_ge(s_mod, NB + 2)
                sp.dma_start(g.mod, mod[:]).then_inc(s_out, 16)
                sp.wait_ge(s_out, 16)

            @block.gpsimd
            def _(pool):
                for b in range(WB):
                    pool.dma_start(w[:, b], w_view[:, :, b * CB:(b + 1) * CB]).then_inc(s_w[b], 16)
                with pool.Fori(1, NB // WB) as i:
                    for b in range(WB):
                        pool.wait_ge(s_mm, i * WB + (b + 1 - WB))
                        pool.dma_start(w[:, b], w_view[:, :, bass.ds(i * (WB * CB) + b * CB, CB)]).then_inc(s_w[b], 16)

            @block.scalar
            def _(act):
                act.wait_ge(s_c, 48)
                nc.scalar.activation(c_silu[:], c_rows[:], ACT.Silu).then_inc(s_silu, 1)
                act.wait_ge(s_ld, 2)
                nc.scalar.activation(ldot[:], ldot[:], ACT.Exp).then_inc(s_le, 1)

            @block.tensor
            def _(pe):
                pe.wait_ge(s_c, 48)
                pe.wait_ge(s_silu, 1)
                for k in range(KD):
                    last = nc.tensor.transpose(ps_t[:, k * NC:(k + 1) * NC], c_silu[:, k * P:(k + 1) * P], ident[0:NC, 0:NC])
                last.then_inc(s_ct, 1)
                pe.wait_ge(s_ctc, 1)

                def block_product(b):
                    for k in range(KD):
                        last = nc.tensor.matmul(ps_m[0:NC, b, :], cT[:, k, :], w[:, b, k, :], start=k == 0, stop=k == KD - 1)
                    last.then_inc(s_mm, 1)
                for b in range(WB):
                    pe.wait_ge(s_w[b], 16)
                    block_product(b)
                with pe.Fori(1, NB // WB) as i:
                    for b in range(WB):
                        pe.wait_ge(s_w[b], i * 16 + 16)
                        pe.wait_ge(s_mod, i * WB + (b + 1 - WB))
                        block_product(b)

            @block.vector
            def _(dve):
                dve.wait_ge(s_ct, 1)
                nc.vector.tensor_copy(cT[:].rearrange("p k c -> p (k c)"), ps_t[:, 0:KD * NC]).then_inc(s_ctc, 1)
                dve.wait_ge(s_in, 112)
                with dve.Fori(0, NB // WB) as i:
                    for b in range(WB):
                        dve.wait_ge(s_mm, i * WB + (b + 1))
                        cols = bass.ds(i * (WB * CB) + b * CB, CB)
                        nc.vector.tensor_tensor(mod[:, cols], ps_m[0:NC, b, :], bias[:, cols], ALU.add).then_inc(s_mod, 1)
                for n in range(2):
                    nc.vector.tensor_tensor_reduce(lprod[:, n, :], lvec[:, 2 * n, :], lvec[:, 2 * n + 1, :], 1.0, 0.0,
                                                   ALU.mult, ALU.add, ldot[:, n:n + 1]).then_inc(s_ld, 1)
                dve.wait_ge(s_le, 1)
                nc.vector.tensor_tensor(ldif[:], ldot[:, 0:1], ldot[:, 1:2], ALU.subtract).then_inc(s_lam, 1)
                dve.wait_ge(s_lam, 1)
                nc.vector.tensor_scalar(g.lam[:], ldif[:], LAMBDA_INIT, None, ALU.add).then_inc(s_lam, 1)
                dve.wait_ge(s_mod, NB)
                for n in range(2):
                    part = mod[:, (3 * n + 1) * D:(3 * n + 2) * D]
                    nc.vector.scalar_tensor_tensor(out=part, in0=part, scalar=1.0, in1=gain[:, n, :],
                                                   op0=ALU.add, op1=ALU.mult).then_inc(s_mod, 1)


def projection_phase(nc, g):
    with ExitStack() as ctx:
        sb = lambda name, shape, dt=F32: ctx.enter_context(nc.sbuf_tensor(name, shape, dt))
        hT = sb("hT_high", [P, KD, NT], F32R), sb("hT_low", [P, KD, NT], F32R)
        w = sb("w_in_high", [P, 2, KD, CB], F32R), sb("w_in_low", [P, 2, KD, CB], F32R)
        w_raw = sb("w_in_buf", [P, KD, CB])
        eps = sb("eps_b", [P, 1])
        modulated_transposed(nc, g, hT, w, w_raw, eps)
        z_blocks(nc, g, hT, w, w_raw, eps)


def modulated_transposed(nc, g, hT, w, w_raw, eps):
    with ExitStack() as ctx:
        sb = lambda name, shape, dt=F32: ctx.enter_context(nc.sbuf_tensor(name, shape, dt))
        ident = sb("ident_b", [P, P])
        x = sb("x_tile", [P, 2, D])
        h = sb("h_tile", [P, 2, D])
        modp = sb("mod_prompt", [P, 2, D])
        mods = sb("mod_sample", [NS, 2, D])
        ms = sb("mean_square", [P, 2, 1])
        rstd = sb("rstd_x", [P, 2, 1])
        ps_h = ctx.enter_context(nc.psum_tensor("ps_hT", [P, 2, D], F32))
        s_x = [g.sem(f"b_x{b}") for b in range(2)]
        s_eps, s_ms, s_w, s_high, s_low, s_hth = [g.sem("b_" + n) for n in ("eps", "mod_sample", "weights", "w_high", "w_low", "hT_high")]
        w_view = g.w_in.rearrange("(k p) n -> p k n", p=P)
        s_in, s_sq, s_sqrt, s_rec, s_xn, s_xm, s_h, s_ht, s_htc = [
            g.sem("b_" + n) for n in ("inputs", "square", "sqrt", "rstd", "normed", "scaled", "h", "hT_psum", "hT")]
        x_dram = [g.x_prompt[t * P:(t + 1) * P, :] for t in range(PT)] + [g.x_sample]
        with nc.Block() as block:
            @block.sync
            def _(sp):
                for t in range(TILES):
                    if t == 1:
                        sp.dma_start(ident[:], g.ident).then_inc(s_in, 16)
                        for n in (1, 0):
                            sp.dma_start(modp[:, n, :], g.mod[0:1, n * D:(n + 1) * D].broadcast_to([P, D])).then_inc(s_in, 16)
                    if t == 2:
                        for n in range(2):
                            for q in range(NSEQ):
                                sp.dma_start(mods[q * NDEC:(q + 1) * NDEC, n, :],
                                             g.mod[1 + q:2 + q, n * D:(n + 1) * D].broadcast_to([NDEC, D])).then_inc(s_ms, 16)
                    if t >= 2:
                        sp.wait_ge(s_xn, t - 1)
                    sp.dma_start(x[0:rows_of(t), t % 2, :], x_dram[t]).then_inc(s_x[t % 2], 16)

            @block.gpsimd
            def _(pool):
                nc.gpsimd.memset(eps[:], EPS).then_inc(s_eps, 1)
                pool.dma_start(w_raw[:], w_view[:, :, 0:CB]).then_inc(s_w, 16)
                pool.wait_ge(s_w, 16)
                nc.gpsimd.tensor_copy(w[0][:, 0], w_raw[:]).then_inc(s_high, 1)
                pool.wait_ge(s_high, 1)
                nc.gpsimd.tensor_tensor(w[1][:, 0], w_raw[:], w[0][:, 0].bitcast(F32), ALU.subtract).then_inc(s_low, 1)
                pool.wait_ge(s_low, 1)
                pool.dma_start(w_raw[:], w_view[:, :, CB:2 * CB]).then_inc(s_w, 16)
                pool.wait_ge(s_w, 32)

            @block.scalar
            def _(act):
                act.wait_ge(s_eps, 1)

                def high_hT(t):
                    r = rows_of(t)
                    act.wait_ge(s_ht, t + 1)
                    nc.scalar.activation(hT[0][:, :, t * P:t * P + r],
                                         ps_h[:, t % 2, :].rearrange("p (k c) -> p k c", c=P)[:, :, 0:r], ACT.Copy).then_inc(s_hth, 1)
                for t in range(TILES):
                    r = rows_of(t)
                    act.wait_ge(s_x[t % 2], 16 * (t // 2 + 1))
                    if t >= 2:
                        act.wait_ge(s_ht, t - 1)
                    nc.scalar.activation(h[0:r, t % 2, :], x[0:r, t % 2, :], ACT.Square,
                                         accum_out=ms[0:r, t % 2, :]).then_inc(s_sq, 1)
                    act.wait_ge(s_sq, t + 1)
                    nc.scalar.activation(ms[0:r, t % 2, :], ms[0:r, t % 2, :], ACT.Sqrt, bias=eps[0:r, :],
                                         scale=1.0 / D).then_inc(s_sqrt, 1)
                    if t >= 1:
                        high_hT(t - 1)
                high_hT(TILES - 1)

            @block.vector
            def _(dve):
                dve.wait_ge(s_in, 48)

                def low_hT(t):
                    r = rows_of(t)
                    cols = slice(t * P, t * P + r)
                    dve.wait_ge(s_hth, t + 1)
                    nc.vector.tensor_tensor(hT[1][:, :, cols], ps_h[:, t % 2, :].rearrange("p (k c) -> p k c", c=P)[:, :, 0:r],
                                            hT[0][:, :, cols].bitcast(F32), ALU.subtract).then_inc(s_htc, 1)
                for t in range(TILES):
                    r = rows_of(t)
                    m = modp if t < PT else mods
                    if t == PT:
                        dve.wait_ge(s_ms, 16 * 2 * NSEQ)
                    dve.wait_ge(s_sqrt, t + 1)
                    nc.vector.reciprocal(rstd[0:r, t % 2, :], ms[0:r, t % 2, :]).then_inc(s_rec, 1)
                    dve.wait_ge(s_rec, t + 1)
                    nc.vector.scalar_tensor_tensor(out=h[0:r, t % 2, :], in0=x[0:r, t % 2, :], scalar=rstd[0:r, t % 2, :],
                                                   in1=m[0:r, 1, :], op0=ALU.mult, op1=ALU.mult).then_inc(s_xn, 1)
                    dve.wait_ge(s_xn, t + 1)
                    nc.vector.tensor_tensor(h[0:r, t % 2, :], h[0:r, t % 2, :], m[0:r, 0, :], ALU.add).then_inc(s_h, 1)
                    if t >= 1:
                        low_hT(t - 1)
                low_hT(TILES - 1)

            @block.tensor
            def _(pe):
                pe.wait_ge(s_in, 48)
                for t in range(TILES):
                    r = rows_of(t)
                    pe.wait_ge(s_h, t + 1)
                    if t >= 2:
                        pe.wait_ge(s_htc, t - 1)
                    for k in range(KD):
                        last = nc.tensor.transpose(ps_h[:, t % 2, k * P:k * P + r], h[0:r, t % 2, k * P:(k + 1) * P],
                                                   ident[0:r, 0:r])
                    last.then_inc(s_ht, 1)


def z_blocks(nc, g, hT, w, w_raw, eps):
    RING = 6
    PAIRS = ZW // CB // 2
    STEPS = 2 * TILES
    assert STEPS % RING == 0
    NM = CB // DH
    NG = CB // P
    with ExitStack() as ctx:
        sb = lambda name, shape, dt=F32: ctx.enter_context(nc.sbuf_tensor(name, shape, dt))
        zs = sb("z_raw", [P, RING, CB])
        zo = sb("z_out", [P, RING, CB])
        sq = sb("z_square", [P, CB])
        t1 = sb("rope_cos_part", [P, CB])
        t2 = sb("rope_sin_part", [P, CB])
        ss = sb("z_sumsq", [P, NM])
        sd = sb("z_std", [P, NM])
        rs = sb("z_rstd", [P, NM])
        cs = sb("rope_tables", [P, TILES, 2, DH])
        gains = sb("qkv_gains", [P, 2, DH])
        vgain = sb("gate_v_gain", [P, P])
        ps_z = ctx.enter_context(nc.psum_tensor("ps_z", [P, RING, CB], F32))
        s_raw, s_high, s_w, s_pass = [g.sem("z_" + n) for n in ("weights_loaded", "w_high", "w_split", "pool_passed")]
        s_st = [g.sem(f"z_stored{j}") for j in range(RING)]
        LAPS = STEPS // RING
        s_in, s_z, s_zfree, s_zs, s_d, s_ss, s_std, s_zo = [
            g.sem("z_" + n) for n in ("consts", "product", "bank_free", "raw", "dve_chain", "sumsq", "std", "out_ready")]
        s_zoa = g.sem("z_out_ready_act")
        w_view = g.w_in.rearrange("(k p) n -> p k n", p=P)
        CHAIN_QK, CHAIN_GV = 8, 4
        NCONST = 16 * (TILES + 3)
        with nc.Block() as block:
            @block.gpsimd
            def _(pool):
                pool.sem_inc(s_w, 1)

                def split(b, highs, blocks):
                    nc.gpsimd.tensor_copy(w[0][:, b], w_raw[:]).then_inc(s_high, 1)
                    pool.wait_ge(s_high, highs)
                    nc.gpsimd.tensor_tensor(w[1][:, b], w_raw[:], w[0][:, b].bitcast(F32), ALU.subtract).then_inc(s_w, 1)
                    pool.wait_ge(s_w, blocks)
                split(1, 1, 2)
                with pool.Fori(1, PAIRS) as i:
                    for b in range(2):
                        pool.dma_start(w_raw[:], w_view[:, :, bass.ds(i * (2 * CB) + b * CB, CB)]).then_inc(s_raw, 16)
                        pool.wait_ge(s_raw, i * 32 + (16 * b - 16))
                        wait_apart(pool, s_z, i * STEPS + (b - 1) * TILES, s_pass)
                        split(b, i * 2 + b, i * 2 + (b + 1))

            @block.tensor
            def _(pe):
                with pe.Fori(0, PAIRS) as i:
                    for b in range(2):
                        pe.wait_ge(s_w, i * 2 + (b + 1))
                        for t in range(TILES):
                            r = rows_of(t)
                            n = b * TILES + t
                            pe.wait_ge(s_zfree, i * STEPS + (n + 1))
                            for k in range(KD):
                                for lhs, rhs in ((0, 0), (0, 1), (1, 0)):
                                    last = nc.tensor.matmul(ps_z[0:r, n % RING, :], hT[lhs][:, k, t * P:t * P + r],
                                                            w[rhs][:, b, k, :], start=k == 0 and (lhs, rhs) == (0, 0),
                                                            stop=k == KD - 1 and lhs == 1)
                            last.then_inc(s_z, 1)

            kinds = [("rope", 0, 2), ("copy", 2, 3), ("gelu", 3, 4), ("gate_v", 4, 5), ("sigmoid", 5, 7)]

            @block.scalar
            def _(act):
                for _ in range(RING):
                    act.sem_inc(s_zfree, 1)
                act.wait_ge(s_in, NCONST)
                for kind, lo, hi in kinds:
                    with act.Fori(lo, hi) as i:
                        for n in range(STEPS):
                            r = rows_of(n % TILES)
                            act.wait_ge(s_z, i * STEPS + (n + 1))
                            src, j = ps_z[0:r, n % RING, :], n % RING
                            if kind in ("rope", "gate_v"):
                                f = ACT.Copy if kind == "rope" else ACT.Gelu
                                nc.scalar.activation(zs[0:r, j, :], src, f).then_inc(s_zs, 1)
                                act.wait_ge(s_zs, (i * STEPS + (n + 1)) if kind == "rope" else (i * STEPS + (n + 1 - 2 * STEPS)))
                                act.sem_inc(s_zfree, 1)
                                m, scale = (NM, 1.0 / DH) if kind == "rope" else (NG, 1.0 / P)
                                at = (n + 1) if kind == "rope" else (n + 1 - 2 * STEPS)
                                act.wait_ge(s_ss, i * STEPS + at)
                                nc.scalar.activation(sd[0:r, 0:m], ss[0:r, 0:m], ACT.Sqrt, bias=eps[0:r, :],
                                                     scale=scale).then_inc(s_std, 1)
                            else:
                                f = {"copy": ACT.Copy, "gelu": ACT.Gelu, "sigmoid": ACT.Sigmoid}[kind]
                                act.wait_ge(s_st[j], i * (16 * LAPS) + 16 * (n // RING))
                                nc.scalar.activation(zo[0:r, j, :], src, f).then_inc(s_zoa, 1)
                                off = 2 * STEPS if kind in ("copy", "gelu") else 3 * STEPS
                                act.wait_ge(s_zoa, i * STEPS + (n + 1 - off))
                                act.sem_inc(s_zfree, 1)

            @block.vector
            def _(dve):
                dve.wait_ge(s_in, NCONST)

                def step(kind, i, n, gain=None, first=False):
                    t, j = n % TILES, n % RING
                    r = rows_of(t)
                    d_at = (lambda c: i * (STEPS * CHAIN_QK) + (n * CHAIN_QK + c)) if kind == "rope" else \
                        (lambda c: i * (STEPS * CHAIN_GV) + (2 * STEPS * CHAIN_QK + (n - 4 * STEPS) * CHAIN_GV + c))
                    at = (n + 1) if kind == "rope" else (n + 1 - 2 * STEPS)
                    m = NM if kind == "rope" else NG
                    wd = CB // m
                    z3 = zs[0:r, j, :].rearrange("p (m d) -> p m d", d=wd)
                    o3 = zo[0:r, j, :].rearrange("p (m d) -> p m d", d=wd)
                    q3 = sq[0:r, :].rearrange("p (m d) -> p m d", d=wd)
                    c = [0]

                    def link(ins):
                        c[0] += 1
                        ins.then_inc(s_d, 1)
                        dve.wait_ge(s_d, d_at(c[0]))
                    dve.wait_ge(s_zs, i * STEPS + at)
                    link(nc.vector.tensor_tensor(sq[0:r, :], zs[0:r, j, :], zs[0:r, j, :], ALU.mult))
                    nc.vector.tensor_reduce(ss[0:r, 0:m], q3, AX.X, ALU.add).then_inc(s_ss, 1)
                    dve.wait_ge(s_std, i * STEPS + at)
                    link(nc.vector.reciprocal(rs[0:r, 0:m], sd[0:r, 0:m]))
                    rb = rs[0:r, 0:m].unsqueeze(2).broadcast_to([r, m, wd])
                    link(nc.vector.tensor_tensor(z3, z3, rb, ALU.mult))
                    if not first:
                        dve.wait_ge(s_st[j], i * (16 * LAPS) + 16 * (n // RING))
                    if kind == "gate_v":
                        gb = vgain[0:r, :].unsqueeze(1).broadcast_to([r, m, wd])
                        link(nc.vector.tensor_tensor(o3, z3, gb, ALU.mult))
                    else:
                        gb = gains[0:r, gain, :].unsqueeze(1).broadcast_to([r, m, wd])
                        link(nc.vector.tensor_tensor(z3, z3, gb, ALU.mult))
                        hd = DH // 2
                        cb = cs[0:r, t, 0, :].unsqueeze(1).broadcast_to([r, m, DH])
                        a3 = t1[0:r, :].rearrange("p (m d) -> p m d", d=DH)
                        b3 = t2[0:r, :].rearrange("p (m d) -> p m d", d=DH)
                        link(nc.vector.tensor_tensor(a3, z3, cb, ALU.mult))
                        for lo, other in ((0, hd), (hd, 0)):
                            sn = cs[0:r, t, 1, lo:lo + hd].unsqueeze(1).broadcast_to([r, m, hd])
                            link(nc.vector.tensor_tensor(b3[:, :, lo:lo + hd], z3[:, :, other:other + hd], sn, ALU.mult))
                        link(nc.vector.tensor_tensor(zo[0:r, j, :], t1[0:r, :], t2[0:r, :], ALU.add))
                    dve.sem_inc(s_zo, 1)
                for pair in range(2):
                    for n in range(STEPS):
                        step("rope", pair, n, gain=pair, first=pair == 0 and n < RING)
                with dve.Fori(4, 5) as i:
                    for n in range(STEPS):
                        step("gate_v", i, n)

            @block.sync
            def _(sp):
                for t in range(TILES):
                    sp.dma_start(cs[0:rows_of(t), t], g.rope[t * P:t * P + rows_of(t)]).then_inc(s_in, 16)
                sp.dma_start(gains[:, 0, :], g.q_norm_g.broadcast_to([P, DH])).then_inc(s_in, 16)
                sp.dma_start(gains[:, 1, :], g.k_norm_g.broadcast_to([P, DH])).then_inc(s_in, 16)
                sp.dma_start(vgain[:], g.gm_v_norm_g.broadcast_to([P, P])).then_inc(s_in, 16)
                for kind, lo, hi in kinds:
                    ready, off = {"rope": (s_zo, 0), "gate_v": (s_zo, 2), "copy": (s_zoa, 2), "gelu": (s_zoa, 2),
                                  "sigmoid": (s_zoa, 3)}[kind]
                    with sp.Fori(lo, hi) as i:
                        for n in range(STEPS):
                            b, t = divmod(n, TILES)
                            r = rows_of(t)
                            sp.wait_ge(ready, i * STEPS + (n + 1 - off * STEPS))
                            sp.dma_start(g.z[t * P:t * P + r, bass.ds(i * (2 * CB) + b * CB, CB)],
                                         zo[0:r, n % RING, :]).then_inc(s_st[n % RING], 16)
                for j in range(RING):
                    sp.wait_ge(s_st[j], 16 * PAIRS * LAPS)


SCALE = DH ** -0.5


def prompt_attention_phase(nc, g):
    RR = 4
    with ExitStack() as ctx:
        sb = lambda name, shape, dt=F32: ctx.enter_context(nc.sbuf_tensor(name, shape, dt))
        ident, mask = sb("ident_c", [P, P]), sb("causal_mask", [P, P])
        qkv = sb("qkv_rows", [P, 2, 3, PT, P])
        qT = sb("qT", [P, 2, 2, NP])
        kT = sb("kT", [P, 2, NP])
        prob = sb("prob", [P, 2, 2, NP])
        diff = sb("diff_prob", [P, 2, NP])
        diffT = sb("diff_probT", [P, 2, NP])
        o = sb("att_rows", [P, 2, PT, P])
        nmax, nbias, rsum = [sb(n, [P, 2, 2]) for n in ("neg_max", "exp_bias", "row_sum")]
        rec, coef = sb("row_rec", [P, RR, 2]), sb("map2_coef", [P, RR])
        ps_s = ctx.enter_context(nc.psum_tensor("ps_scores", [P, 2, NP], F32))
        ps_t = ctx.enter_context(nc.psum_tensor("ps_turned", [P, NP], F32))
        ps_o = ctx.enter_context(nc.psum_tensor("ps_att", [P, 2, CB], F32))
        s_in, s_res = g.sem("c_consts"), g.sem("c_results_copied")
        s_ld = [g.sem(f"c_qkv{b}") for b in range(2)]
        s_st = [g.sem(f"c_stored{b}") for b in range(2)]
        s_ofree = [g.sem(f"c_rows_free{b}") for b in range(2)]
        s_s = [g.sem(f"c_scores{m}") for m in range(2)]
        s_nm = [g.sem(f"c_neg_max{m}") for m in range(2)]
        s_nb = [g.sem(f"c_exp_bias{m}") for m in range(2)]
        s_e = [g.sem(f"c_exp{m}") for m in range(2)]
        s_turn, s_kTc, s_qTc, s_z, s_rec, s_coef, s_a, s_at, s_atc, s_o, s_oc = [
            g.sem("c_" + n) for n in ("qk_turned", "kT", "qT", "zeroed", "rec", "map2_coef",
                                      "diff", "diff_turned", "diffT", "att", "att_rows")]
        HEADS2 = 2 * PT

        def heads(eng, head):
            with eng.Fori(0, H // 2 - 1) as i:
                head(i, 0, True)
                head(i, 1, True)
            head(H // 2 - 1, 0, True)
            head(H // 2 - 1, 1, False)
        with nc.Block() as block:
            @block.sync
            def _(sp):
                sp.dma_start(ident[:], g.ident).then_inc(s_in, 16)
                sp.dma_start(mask[:], g.mask).then_inc(s_in, 16)

                def results():
                    for dst, rows, c in ((g.o_kp, slice(0, NP), ZK), (g.o_vp, slice(0, NP), ZV), (g.o_ks, slice(NP, NT), ZK),
                                         (g.o_vs, slice(NP, NT), ZV), (g.o_gv, slice(NP, NT), ZGV)):
                        sp.dma_start(dst, g.z[rows, c:c + D]).then_inc(s_res, 16)

                def load(h, par):
                    for n in range(3):
                        sp.dma_start(qkv[:, par, n], g.z[0:NP, bass.ds(h * P + n * D, P)]
                                     .rearrange("(t p) c -> p t c", p=P)).then_inc(s_ld[par], 16)
                load(0, 0)
                load(1, 1)
                results()

                def head(i, par, more):
                    sp.wait_ge(s_oc, i * HEADS2 + ((par + 1) * PT + 2))
                    sp.dma_start(g.att[0:NP, bass.ds(i * (2 * P) + par * P, P)].rearrange("(t p) c -> p t c", p=P),
                                 o[:, par]).then_inc(s_st[par], 16)
                    if more:
                        load(i * 2 + (2 + par), par)
                    sp.wait_ge(s_st[par], i * 16 + 16)
                    sp.sem_inc(s_ofree[par], 1)
                for par in range(2):
                    sp.sem_inc(s_ofree[par], 1)
                with sp.Fori(0, H // 2 - 1) as i:
                    for par in range(2):
                        head(i, par, True)
                for par in range(2):
                    head(H // 2 - 1, par, False)
                sp.wait_ge(s_res, 16 * 5)

            @block.tensor
            def _(pe):
                pe.wait_ge(s_in, 32)

                def turn_qk(h, par):
                    pe.wait_ge(s_ld[par], (h - par) * 24 + 48)
                    for n, m in ((1, 0), (0, 1)):
                        pe.wait_ge(s_e[m], h * PT + 1)
                        for t in range(PT):
                            last = nc.tensor.transpose(ps_s[:, m, t * P:(t + 1) * P], qkv[:, par, n, t, :], ident[:])
                        last.then_inc(s_turn, 1)

                def head(i, par, more):
                    pe.wait_ge(s_kTc, i * 2 + (par + 1))
                    pe.wait_ge(s_qTc, i * 4 + (2 * par + 2))

                    def scores(t):
                        step = par * PT + t
                        for m in range(2):
                            pe.wait_ge(s_e[m], i * HEADS2 + (step + 1))
                            for c in range(0, (t + 1) * P, CB):
                                w = min(CB, (t + 1) * P - c)
                                edge = c + w == (t + 1) * P
                                last = nc.tensor.matmul(ps_s[:, m, c:c + w], qT[:, par, m, t * P:(t + 1) * P],
                                                        kT[:, par, c:c + w], start=True, stop=not edge)
                            last = nc.tensor.matmul(ps_s[:, m, t * P:(t + 1) * P], ident[:], mask[:], start=False, stop=True)
                            last.then_inc(s_s[m], 1)

                    def values(t):
                        step = par * PT + t
                        pe.wait_ge(s_atc, i * HEADS2 + (step + 2))
                        pe.wait_ge(s_oc, i * HEADS2 + (step + 1))
                        for c in range(t + 1):
                            last = nc.tensor.matmul(ps_o[:, t % 2, 0:P], diffT[:, t % 2, c * P:(c + 1) * P],
                                                    qkv[:, par, 2, c, :], start=c == 0, stop=c == t)
                        last.then_inc(s_o, 1)
                    scores(0)
                    for t in range(PT):
                        step = par * PT + t
                        if t + 1 < PT:
                            scores(t + 1)
                        elif more:
                            turn_qk(i * 2 + (par + 1), 1 - par)
                        pe.wait_ge(s_a, i * HEADS2 + (step + 1))
                        if t > 0:
                            pe.wait_ge(s_atc, i * HEADS2 + (step + 1))
                        for c in range(t + 1):
                            last = nc.tensor.transpose(ps_t[:, c * P:(c + 1) * P], diff[:, t % 2, c * P:(c + 1) * P], ident[:])
                        last.then_inc(s_at, 1)
                        if t > 0:
                            values(t - 1)
                    values(PT - 1)
                turn_qk(0, 0)
                heads(pe, head)

            @block.scalar
            def _(act):
                for m in range(2):
                    act.sem_inc(s_e[m], 1)
                act.sem_inc(s_atc, 1)

                def copy_kT(h, par):
                    act.wait_ge(s_turn, h * 2 + 1)
                    nc.scalar.activation(kT[:, par, :], ps_s[:, 0, :], ACT.Copy).then_inc(s_kTc, 1)

                def head(i, par, more):
                    def exps(t):
                        step = par * PT + t
                        n = (t + 1) * P
                        for m in range(2):
                            act.wait_ge(s_nb[m], i * HEADS2 + (step + 1))
                            nc.scalar.activation(prob[:, t % 2, m, 0:n], ps_s[:, m, 0:n], ACT.Exp, bias=nbias[:, t % 2, m:m + 1],
                                                 scale=SCALE, accum_out=rsum[:, t % 2, m:m + 1]).then_inc(s_e[m], 1)
                    exps(0)
                    for t in range(PT):
                        step = par * PT + t
                        if t + 1 < PT:
                            exps(t + 1)
                        elif more:
                            copy_kT(i * 2 + (par + 1), 1 - par)
                        n = (t + 1) * P
                        act.wait_ge(s_at, i * HEADS2 + (step + 1))
                        nc.scalar.activation(diffT[:, t % 2, 0:n], ps_t[:, 0:n], ACT.Copy).then_inc(s_atc, 1)
                copy_kT(0, 0)
                heads(act, head)

            @block.vector
            def _(dve):
                dve.sem_inc(s_oc, 2)
                nc.vector.memset(qT[:], 0.0).then_inc(s_z, 1)
                dve.wait_ge(s_z, 1)

                def bias(i, par, t):
                    step, n, b = par * PT + t, (t + 1) * P, t % 2
                    for m in range(2):
                        dve.wait_ge(s_s[m], i * HEADS2 + (step + 1))
                        nc.vector.tensor_reduce(nmax[:, b, m:m + 1], ps_s[:, m, 0:n], AX.X, ALU.max, negate=True).then_inc(s_nm[m], 1)
                        dve.wait_ge(s_nm[m], i * HEADS2 + (step + 1))
                        nc.vector.tensor_scalar(nbias[:, b, m:m + 1], nmax[:, b, m:m + 1], SCALE, None, ALU.mult).then_inc(s_nb[m], 1)

                def combine(i, par, t):
                    step, n, b = par * PT + t, (t + 1) * P, t % 2
                    for m in range(2):
                        dve.wait_ge(s_e[m], i * HEADS2 + (step + 2))
                    nc.vector.reciprocal(rec[:, t % RR, :], rsum[:, b, :]).then_inc(s_rec, 1)
                    dve.wait_ge(s_rec, i * HEADS2 + (step + 1))
                    nc.vector.scalar_tensor_tensor(out=coef[:, t % RR:t % RR + 1], in0=rsum[:, b, 0:1], scalar=g.lam[:, 0:1],
                                                   in1=rec[:, t % RR, 1:2], op0=ALU.mult, op1=ALU.mult).then_inc(s_coef, 1)
                    dve.wait_ge(s_coef, i * HEADS2 + (step + 1))
                    nc.vector.scalar_tensor_tensor(out=diff[:, b, 0:n], in0=prob[:, b, 1, 0:n], scalar=coef[:, t % RR:t % RR + 1],
                                                   in1=prob[:, b, 0, 0:n], op0=ALU.mult, op1=ALU.subtract).then_inc(s_a, 1)

                def rows_out(i, par, t):
                    step = par * PT + t
                    dve.wait_ge(s_o, i * HEADS2 + (step + 1))
                    nc.vector.tensor_scalar(o[:, par, t, :], ps_o[:, t % 2, 0:P], rec[:, t % RR, 0:1], -1.0,
                                            ALU.mult, ALU.mult).then_inc(s_oc, 1)

                def copy_qT(h, par):
                    dve.wait_ge(s_turn, h * 2 + 2)
                    for m in range(2):
                        rows = slice(m * DH, (m + 1) * DH)
                        nc.vector.tensor_copy(qT[rows, par, m, :], ps_s[rows, 1, :]).then_inc(s_qTc, 1)

                def head(i, par, more):
                    bias(i, par, 0)
                    for t in range(PT):
                        combine(i, par, t)
                        if t + 1 < PT:
                            bias(i, par, t + 1)
                        elif more:
                            copy_qT(i * 2 + (par + 1), 1 - par)
                        if t == 1:
                            dve.wait_ge(s_ofree[par], i + 1)
                        if t > 1:
                            rows_out(i, par, t - 2)
                    rows_out(i, par, PT - 2)
                    rows_out(i, par, PT - 1)
                copy_qT(0, 0)
                heads(dve, head)


def sample_attention_phase(nc, g):
    R2 = 2 * H * NDEC
    R1 = H * NDEC
    KR = 4
    GP = CB // PAGE
    NG = NPAGES // GP
    with ExitStack() as ctx:
        sb = lambda name, shape, dt=F32: ctx.enter_context(nc.sbuf_tensor(name, shape, dt))
        ident = sb("ident_d", [P, P])
        mask = sb("new_mask", [R2, NDEC])
        prow = sb("partition_number", [P, 1])
        rowidx = sb("page_rows", [P, NSEQ * NPAGES], U32)
        idxk, idxv = sb("k_rows_now", [P, 2, NPAGES], U32), sb("v_rows_now", [P, 2, NPAGES], U32)
        qkT = sb("qk_sampleT", [P, 2, H, NS])
        qsel = sb("q_by_rows", [P, 2, H * (R2 + NDEC)])
        kpage = sb("k_pages", [P, KR, D])
        vpage = sb("v_pages", [P, 2, NPAGES, D])
        vnew = sb("v_new", [NDEC, 2, D])
        kT = sb("kT_pages", [P, 2, H, CB])
        prob = sb("prob_sample", [R2, PAST + NDEC])
        stat = sb("softmax_stats", [R2, 8])
        sign = sb("map_sign", [R2, 1])
        pT = sb("probT", [P, CB])
        ptab = pT[:, 0:NSEQ * NPAGES].bitcast(I32)
        ptabf = pT[:, CB - NSEQ * NPAGES:CB]
        qk = prob[0:NS, 0:2 * D].rearrange("p (n c) -> p n c", n=2)
        aT = sb("diffT_sample", [P, NPAGES + 1, R1])
        o = sb("att_sample", [R1, D])
        ps_s = ctx.enter_context(nc.psum_tensor("ps_scores_d", [R2, PAST], F32))
        ps_t = ctx.enter_context(nc.psum_tensor("ps_turned_d", [P, 2, CB], F32))
        ps_o = ctx.enter_context(nc.psum_tensor("ps_att_d", [R1, D], F32))
        s_in, s_idx0, s_qkt, s_qktc = [g.sem("d_" + n) for n in ("inputs", "row_numbers", "qk_turned", "qkT")]
        s_idx, s_qsel, s_sg, s_sn, s_chain, s_nb, s_e, s_ps, s_pt, s_ptc, s_at, s_o, s_oc = [
            g.sem("d_" + n) for n in ("index_copied", "q_by_rows", "group_scores", "new_scores", "softmax_chain",
                                      "exp_bias", "exp", "prob_scaled", "prob_turned", "probT", "diffT", "att", "att_copied")]
        s_kt = [g.sem(f"d_k_turned{b}") for b in range(2)]
        s_ktc = [g.sem(f"d_k_copied{b}") for b in range(2)]
        s_k = [g.sem(f"d_k_page{j}") for j in range(KR)]
        s_v = [g.sem(f"d_v_pages{b}") for b in range(2)]
        s_vn = [g.sem(f"d_v_new{b}") for b in range(2)]
        s_ost = g.sem("d_stored")
        s_pass_pool, s_pass_pe = g.sem("d_pool_passed"), g.sem("d_tensor_passed")
        s_ofree = g.sem("d_rows_free")
        kc = g.cache_k
        vc = g.cache_v
        NIN = 5

        with nc.Block() as block:
            @block.sync
            def _(sp):
                sp.dma_start(ident[:], g.ident).then_inc(s_in, 16)
                sp.dma_start(mask[:], g.new_mask).then_inc(s_in, 16)
                sp.dma_start(ptab, g.page_table.rearrange("a b -> (a b)").unsqueeze(0).broadcast_to([P, NSEQ * NPAGES])).then_inc(s_in, 16)
                sp.dma_start(prow[:], g.prow).then_inc(s_in, 16)
                sp.dma_start(qk, g.z[NP:NT, 0:2 * D].rearrange("t (n c) -> t n c", n=2)).then_inc(s_in, 16)

                def new_values(s, par):
                    sp.dma_start(vnew[:, par, :], g.z[bass.ds(s * NDEC + NP, NDEC), ZV:ZV + D]).then_inc(s_vn[par], 16)
                new_values(0, 0)
                new_values(1, 1)

                sp.sem_inc(s_ofree, 1)

                def store(s, par, more):
                    sp.wait_ge(s_oc, s + 2)
                    for h in range(H):
                        sp.dma_start(g.att[bass.ds(s * NDEC + NP, NDEC), h * VD:(h + 1) * VD],
                                     o[h * NDEC:(h + 1) * NDEC, h * VD:(h + 1) * VD]).then_inc(s_ost, 16)
                    sp.wait_ge(s_ost, s * (16 * H) + 16 * H)
                    sp.sem_inc(s_ofree, 1)
                    if more:
                        new_values(s + 2, par)
                with sp.Fori(0, NSEQ // 2 - 1) as i:
                    store(i * 2, 0, True)
                    store(i * 2 + 1, 1, True)
                store(NSEQ - 2, 0, False)
                store(NSEQ - 1, 1, False)

            @block.gpsimd
            def _(pool):
                pool.wait_ge(s_idx0, 5)

                def numbers(dst, s, par):
                    nc.gpsimd.tensor_copy(dst[:, par, :], rowidx[:, bass.ds(s * NPAGES, NPAGES)]).then_inc(s_idx, 1)

                def load_k(s, par, pg):
                    wait_apart(pool, s_kt[1], s * NPAGES + (pg + 1 - KR), s_pass_pool)
                    pool.indirect_dma_start(kpage[:, pg % KR, :], None, kc,
                                            bass.IndirectOffsetOnAxis(ap=idxk[:, par, pg:pg + 1], axis=0)).then_inc(s_k[pg % KR], 16)

                def load_v(s, par, pg):
                    pool.indirect_dma_start(vpage[:, par, pg, :], None, vc,
                                            bass.IndirectOffsetOnAxis(ap=idxv[:, par, pg:pg + 1], axis=0)).then_inc(s_v[par], 16)

                def load(s, par):
                    numbers(idxk, s, par)
                    wait_apart(pool, s_idx, s * 2 + 1, s_pass_pool)
                    for pg in range(KR):
                        load_k(s, par, pg)
                    if not isinstance(s, int) or s > 1:
                        wait_apart(pool, s_o, s + 1, s_pass_pool)
                    numbers(idxv, s, par)
                    wait_apart(pool, s_idx, s * 2 + 2, s_pass_pool)
                    for pg in range(KR, NPAGES):
                        load_k(s, par, pg)
                        if pg >= 2 * KR:
                            load_v(s, par, pg - 2 * KR)
                    for pg in range(NPAGES - 2 * KR, NPAGES):
                        load_v(s, par, pg)
                load(0, 0)
                with pool.Fori(0, NSEQ // 2 - 1) as i:
                    load(i * 2 + 1, 1)
                    load(i * 2 + 2, 0)
                load(NSEQ - 1, 1)

            @block.tensor
            def _(pe):
                pe.sem_inc(s_o, 2)
                pe.wait_ge(s_in, 16 * NIN)
                for n in range(2):
                    for h in range(H):
                        last = nc.tensor.transpose(ps_t[:, n, h * NS:(h + 1) * NS], qk[:, n, h * P:(h + 1) * P], ident[0:NS, 0:NS])
                    last.then_inc(s_qkt, 1)
                pe.wait_ge(s_qktc, 2)
                KU = NPAGES

                def group_scores(s, par, grp, h):
                    if h == 0:
                        if grp == 0:
                            pe.wait_ge(s_qsel, s + 1)
                        for b in range(2):
                            pe.wait_ge(s_ktc[b], s * KU + (grp + 1) * GP)
                    last = nc.tensor.matmul(ps_s[:, grp * CB:(grp + 1) * CB], qsel[:, par, h * R2:(h + 1) * R2],
                                            kT[:, grp % 2, h, :], start=h == 0, stop=h == H - 1)
                    if h == H - 1:
                        last.then_inc(s_sg, 1)

                def pages(s, par):
                    for pg in range(NPAGES):
                        j, grp = pg % KR, pg // GP
                        pe.wait_ge(s_k[j], s * (16 * NPAGES // KR) + 16 * (pg // KR + 1))
                        if pg == 0:
                            wait_if_any(pe, s_e, s * 2)
                        for b in range(2):
                            wait_if_any(pe, s_ktc[b], s * KU + pg)
                            for q in range(4):
                                h = 4 * b + q
                                last = nc.tensor.transpose(ps_t[:, b, q * P:(q + 1) * P], kpage[:, j, h * P:(h + 1) * P], ident[:])
                            last.then_inc(s_kt[b], 1)
                        if grp:
                            for h in range(2 * (pg % GP), 2 * (pg % GP) + 2):
                                group_scores(s, par, grp - 1, h)

                def last_scores(s, par, between=None):
                    for h in range(H):
                        group_scores(s, par, NG - 1, h)
                        if between and h in (0, 3, 6):
                            between(h // 3)
                    for h in range(H):
                        nc.tensor.matmul(ps_t[0:R2, 0, 0:NDEC], qsel[:, par, h * R2:(h + 1) * R2],
                                         qkT[:, 1, h, bass.ds(s * NDEC, NDEC)], start=h == 0, stop=False)
                    nc.tensor.matmul(ps_t[0:R2, 0, 0:NDEC], ident[0:R2, 0:R2], mask[:], start=False, stop=True).then_inc(s_sn, 1)

                def turn_probabilities(s, u):
                    if u == 0:
                        wait_apart(pe, s_ps, s + 1, s_pass_pe)
                    else:
                        wait_apart(pe, s_ptc, s * 3 + u, s_pass_pe)
                    if u < 2:
                        for q in range(8):
                            pg = 8 * u + q
                            last = nc.tensor.transpose(ps_t[:, 1, q * R2:(q + 1) * R2], prob[:, pg * PAGE:(pg + 1) * PAGE],
                                                       ident[0:R2, 0:R2])
                    else:
                        last = nc.tensor.transpose(ps_t[0:NDEC, 1, 0:R2], prob[:, PAST:PAST + NDEC], ident[0:R2, 0:R2])
                    last.then_inc(s_pt, 1)

                def values(s, par):
                    pe.wait_ge(s_v[par], (s - par) * (8 * NPAGES) + 16 * NPAGES)
                    pe.wait_ge(s_vn[par], (s - par) * 8 + 16)
                    pe.wait_ge(s_at, s * 3 + 3)
                    pe.wait_ge(s_oc, s + 1)
                    for c in range(2):
                        cols = slice(c * CB, (c + 1) * CB)
                        for pg in range(NPAGES):
                            nc.tensor.matmul(ps_o[:, cols], aT[:, pg, :], vpage[:, par, pg, cols], start=pg == 0, stop=False)
                        last = nc.tensor.matmul(ps_o[:, cols], aT[0:NDEC, NPAGES, :], vnew[:, par, cols], start=False, stop=True)
                    last.then_inc(s_o, 1)

                def around(s, par):
                    pages(s + 1, 1 - par)
                    last_scores(s + 1, 1 - par, lambda u: turn_probabilities(s, u))
                    values(s, par)
                pages(0, 0)
                last_scores(0, 0)
                with pe.Fori(0, NSEQ // 2 - 1) as i:
                    around(i * 2, 0)
                    around(i * 2 + 1, 1)
                around(NSEQ - 2, 0)
                for u in range(3):
                    turn_probabilities(NSEQ - 1, u)
                values(NSEQ - 1, 1)

            @block.vector
            def _(dve):
                dve.sem_inc(s_oc, 1)
                nc.vector.memset(qsel[:], 0.0).then_inc(s_idx0, 1)
                nc.vector.memset(sign[0:R1, :], 1.0).then_inc(s_idx0, 1)
                nc.vector.tensor_scalar(sign[R1:R2, :], g.lam[R1:R2, 0:1], -1.0, None, ALU.mult).then_inc(s_idx0, 1)
                dve.wait_ge(s_in, 16 * NIN)
                nc.vector.tensor_copy(ptabf, ptab).then_inc(s_idx0, 1)
                dve.wait_ge(s_idx0, 4)
                nc.vector.tensor_scalar(rowidx[:], ptabf, float(PAGE), prow[:, 0:1], ALU.mult, ALU.add).then_inc(s_idx0, 1)
                dve.wait_ge(s_idx0, 5)
                for n in range(2):
                    dve.wait_ge(s_qkt, n + 1)
                    nc.vector.tensor_copy(qkT[:, n].rearrange("p h t -> p (h t)"), ps_t[:, n, 0:H * NS]).then_inc(s_qktc, 1)
                dve.wait_ge(s_qktc, 2)

                def prepare(s, par):
                    spread = qsel[:, par, :].rearrange("p (h c) -> p h c", h=H)
                    for m in range(2):
                        rows = slice(m * DH, (m + 1) * DH)
                        last = nc.vector.tensor_copy(spread[rows, :, m * R1:m * R1 + NDEC], qkT[rows, 0, :, bass.ds(s * NDEC, NDEC)])
                    last.then_inc(s_qsel, 1)
                prepare(0, 0)
                prepare(1, 1)
                CH = 6

                def keys(s, par, between=None):
                    for pg in range(NPAGES):
                        dve.wait_ge(s_kt[0], s * NPAGES + (pg + 1))
                        if pg % GP == 0:
                            wait_if_any(dve, s_sg, s * NG + (pg // GP - 1))
                        nc.vector.tensor_copy(kT[:, (pg // GP) % 2, 0:4, (pg % GP) * P:(pg % GP + 1) * P],
                                              ps_t[:, 0, :].rearrange("p (h c) -> p h c", h=4)).then_inc(s_ktc[0], 1)
                        if between and pg == GP:
                            between()

                def softmax(s, par):
                    c = [0]

                    def link(ins):
                        c[0] += 1
                        ins.then_inc(s_chain, 1)
                        dve.wait_ge(s_chain, s * CH + c[0])
                    dve.wait_ge(s_sg, s * NG + NG)
                    link(nc.vector.tensor_reduce(stat[:, 0:1], ps_s[:], AX.X, ALU.max))
                    dve.wait_ge(s_sn, s + 1)
                    link(nc.vector.tensor_reduce(stat[:, 1:2], ps_t[0:R2, 0, 0:NDEC], AX.X, ALU.max))
                    link(nc.vector.tensor_reduce(stat[:, 2:3], stat[:, 0:2], AX.X, ALU.max, negate=True))
                    nc.vector.tensor_scalar(stat[:, 3:4], stat[:, 2:3], SCALE, None, ALU.mult).then_inc(s_nb, 1)
                    dve.wait_ge(s_e, s * 2 + 2)
                    link(nc.vector.tensor_tensor(stat[:, 6:7], stat[:, 4:5], stat[:, 5:6], ALU.add))
                    link(nc.vector.reciprocal(stat[:, 7:8], stat[:, 6:7]))
                    link(nc.vector.tensor_tensor(stat[:, 6:7], stat[:, 7:8], sign[:], ALU.mult))
                    nc.vector.tensor_scalar(prob[:], prob[:], stat[:, 6:7], None, ALU.mult).then_inc(s_ps, 1)

                def join(s, par):
                    for u in range(3):
                        dve.wait_ge(s_ptc, s * 3 + (u + 1))
                        if u == 0:
                            dve.wait_ge(s_o, s + 2)
                        if u < 2:
                            v = pT[:, :].rearrange("p (g m r) -> p g m r", m=2, r=R1)
                            nc.vector.tensor_tensor(aT[:, 8 * u:8 * u + 8, :], v[:, :, 0, :], v[:, :, 1, :], ALU.add).then_inc(s_at, 1)
                        else:
                            nc.vector.tensor_tensor(aT[0:NDEC, NPAGES, :], pT[0:NDEC, 0:R1], pT[0:NDEC, R1:R2], ALU.add).then_inc(s_at, 1)

                def output(s):
                    dve.wait_ge(s_ofree, s + 1)
                    dve.wait_ge(s_o, s + 3)
                    nc.vector.tensor_copy(o[:], ps_o[:]).then_inc(s_oc, 1)

                def around(s, par, first=False, more=True):
                    keys(s + 1, 1 - par, None if first else lambda: output(s - 1))
                    join(s, par)
                    softmax(s + 1, 1 - par)
                    if more:
                        prepare(s + 2, par)
                keys(0, 0)
                softmax(0, 0)
                around(0, 0, first=True)
                with dve.Fori(0, NSEQ // 2 - 2) as i:
                    around(i * 2 + 1, 1)
                    around(i * 2 + 2, 0)
                around(NSEQ - 3, 1)
                around(NSEQ - 2, 0, more=False)
                join(NSEQ - 1, 1)
                output(NSEQ - 2)
                output(NSEQ - 1)

            @block.scalar
            def _(act):
                def copy_keys(s, par):
                    for pg in range(NPAGES):
                        act.wait_ge(s_kt[1], s * NPAGES + (pg + 1))
                        if pg % GP == 0:
                            wait_if_any(act, s_sg, s * NG + (pg // GP - 1))
                        nc.scalar.activation(kT[:, (pg // GP) % 2, 4:8, (pg % GP) * P:(pg % GP + 1) * P],
                                             ps_t[:, 1, :].rearrange("p (h c) -> p h c", h=4), ACT.Copy).then_inc(s_ktc[1], 1)

                def softmax(s, par):
                    act.wait_ge(s_nb, s + 1)
                    wait_if_any(act, s_pt, s * 3)
                    nc.scalar.activation(prob[:, 0:PAST], ps_s[:], ACT.Exp, bias=stat[:, 3:4], scale=SCALE,
                                         accum_out=stat[:, 4:5]).then_inc(s_e, 1)
                    nc.scalar.activation(prob[:, PAST:PAST + NDEC], ps_t[0:R2, 0, 0:NDEC], ACT.Exp, bias=stat[:, 3:4], scale=SCALE,
                                         accum_out=stat[:, 5:6]).then_inc(s_e, 1)

                def copy_probabilities(s, par):
                    for u in range(3):
                        act.wait_ge(s_pt, s * 3 + (u + 1))
                        if u:
                            act.wait_ge(s_at, s * 3 + u)
                        if u < 2:
                            nc.scalar.activation(pT[:], ps_t[:, 1, :], ACT.Copy).then_inc(s_ptc, 1)
                        else:
                            nc.scalar.activation(pT[0:NDEC, 0:R2], ps_t[0:NDEC, 1, 0:R2], ACT.Copy).then_inc(s_ptc, 1)

                def around(s, par):
                    copy_keys(s + 1, 1 - par)
                    copy_probabilities(s, par)
                    softmax(s + 1, 1 - par)
                copy_keys(0, 0)
                softmax(0, 0)
                with act.Fori(0, NSEQ // 2 - 1) as i:
                    around(i * 2, 0)
                    around(i * 2 + 1, 1)
                around(NSEQ - 2, 0)
                copy_probabilities(NSEQ - 1, 1)


def mix_phase(nc, g):
    with ExitStack() as ctx:
        sb = lambda name, shape, dt=F32: ctx.enter_context(nc.sbuf_tensor(name, shape, dt))
        w_att, w_gm, w_o = [sb(n, [P, KD, D]) for n in ("w_att", "w_gm", "w_o")]
        ident, lower = sb("ident_e", [P, P]), sb("lower_T", [P, P])
        ws_rows = sb("ws_rows", [P, GROUPS, P])
        wsT = sb("wsT", [P, GROUPS, P])
        wsT_s = sb("wsT_sample", [NS, GROUPS, NS])
        bias, bias_s = sb("gate_bias", [P, GROUPS]), sb("gate_bias_sample", [NS, GROUPS])
        again = sb("subln_gain", [P, VD])
        modp, mods = sb("modp_e", [P, 3, D]), sb("mods_e", [NS, 3, D])
        att, u, v, x, ga, gb = [sb(n, [P, 2, D]) for n in ("att_in", "u_in", "v_in", "x_in", "ga_in", "gb_in")]
        sq = sb("square_e", [P, D])
        aT, sT, mT = [sb(n, [P, KD, P]) for n in ("aT_e", "sT_e", "mT_e")]
        ss, sd, rs = [sb(n, [P, GROUPS]) for n in ("ss_e", "sd_e", "rs_e")]
        ms, rx = sb("ms_e", [P, 1]), sb("rx_e", [P, 1])
        eps = sb("eps_e", [P, 1])
        ps_g, ps_t, ps_a, ps_b = [ctx.enter_context(nc.psum_tensor(n, [P, D], F32)) for n in ("ps_g", "ps_te", "ps_ae", "ps_be")]
        s_in, s_ins, s_ws, s_wsm, s_wss, s_again = [g.sem("e_" + n) for n in (
            "inputs", "sample_inputs", "ws_turned", "ws_masked", "ws_sample_masked", "gain")]
        s_w0 = [g.sem("e_weights_" + n) for n in ("att", "gm", "out")]
        s_ld = [g.sem(f"e_operands{b}") for b in range(2)]
        s_lg = [g.sem(f"e_gates_and_x{b}") for b in range(2)]
        s_sp, s_ma = g.sem("e_sync_passed"), g.sem("e_product_a_used")
        s_st = [g.sem(f"e_stored{b}") for b in range(2)]
        s_sqa, s_ss, s_sd, s_rs, s_an, s_a, s_gt, s_so, s_t, s_tc, s_pa, s_pb, s_gm, s_m, s_w, s_gx, s_x2, s_ms, s_sx, s_rx, s_hn, s_h2 = [
            g.sem("e_" + n) for n in ("att_square", "att_sumsq", "att_std", "att_rstd", "att_normed", "a", "gated", "s_out",
                                      "turned", "turned_copied", "product_a", "product_b", "gate_products", "mix_in", "product_o",
                                      "gated_mix", "x2", "mean_square", "std", "rstd", "normed", "h2")]
        s_zero = g.sem("e_zeroed")
        NIN, NSAMPLE = 16 * (5 + 3), 16 * (3 + NDEC + 1) * NSEQ

        def tiles(eng, around, last):
            with eng.Fori(0, PT // 2 - 1) as i:
                around(i * 2, 0)
                around(i * 2 + 1, 1)
            around(PT - 2, 0)
            around(PT - 1, 1)
            last(PT, 0)

        def rows(t):
            return NS if isinstance(t, int) and t == PT else P

        def use_a(t):
            return 1 if isinstance(t, int) and t == 0 else t * 3

        def use_m(t):
            return t * 3 + (3 if isinstance(t, int) and t == PT else 5)

        with nc.Block() as block:
            @block.sync
            def _(sp):
                sp.dma_start(ws_rows[:], g.gm_ws.rearrange("g i j -> i g j")).then_inc(s_in, 16)
                sp.dma_start(ident[:], g.ident).then_inc(s_in, 16)
                sp.dma_start(lower[:], g.lower_T).then_inc(s_in, 16)
                sp.dma_start(again[:], g.subln_g.broadcast_to([P, VD])).then_inc(s_in, 16)
                sp.dma_start(bias[:], g.gm_bs.rearrange("g i -> i g"), allow_slow_non_contiguous=True).then_inc(s_in, 16)
                for n in range(3):
                    sp.dma_start(modp[:, n, :], g.mod[0:1, (2 + n) * D:(3 + n) * D].broadcast_to([P, D])).then_inc(s_in, 16)

                def sample_inputs():
                    sp.wait_ge(s_zero, 2)
                    for q in range(NSEQ):
                        b = slice(q * NDEC, (q + 1) * NDEC)
                        for n in range(3):
                            sp.dma_start(mods[b, n, :], g.mod[1 + q:2 + q, (2 + n) * D:(3 + n) * D].broadcast_to([NDEC, D])).then_inc(s_ins, 16)
                        for i in range(NDEC):
                            sp.dma_start(wsT_s[b, :, q * NDEC + i], g.gm_ws[:, i, 0:NDEC].rearrange("g j -> j g"),
                                         allow_slow_non_contiguous=True).then_inc(s_ins, 16)
                        sp.dma_start(bias_s[b, :], g.gm_bs[:, 0:NDEC].rearrange("g i -> i g"),
                                     allow_slow_non_contiguous=True).then_inc(s_ins, 16)

                def rows_at(a, t, c=0):
                    r = rows(t)
                    return a[t * P:t * P + r, c:c + D] if isinstance(t, int) else a[bass.ds(t * P, P), c:c + D]

                def load_operands(t, par):
                    for dst, a, c in ((v, g.z, ZGV), (att, g.att, 0), (u, g.z, ZU)):
                        sp.dma_start(dst[0:rows(t), par, :], rows_at(a, t, c)).then_inc(s_ld[par], 16)

                def load_gates(t, par):
                    for dst, a, c in ((ga, g.z, ZGA), (gb, g.z, ZGB)):
                        sp.dma_start(dst[0:rows(t), par, :], rows_at(a, t, c)).then_inc(s_lg[par], 16)
                    xs = g.x_sample if isinstance(t, int) and t == PT else rows_at(g.x_prompt, t)
                    sp.dma_start(x[0:rows(t), par, :], xs).then_inc(s_lg[par], 16)

                def store(t, par):
                    r = rows(t)
                    dst = lambda a: a[t * P:t * P + r, :] if isinstance(t, int) else a[bass.ds(t * P, P), :]
                    wait_apart(sp, s_h2, t + 1, s_sp)
                    sp.dma_start(dst(g.x2), x[0:r, par, :]).then_inc(s_st[par], 16)
                    sp.dma_start(dst(g.h2), ga[0:r, par, :]).then_inc(s_st[par], 16)
                    wait_apart(sp, s_st[par], (t - par) * 16 + 32, s_sp)
                def load_weights(n):
                    dst, src = ((w_att, g.w_att_out), (w_gm, g.w_gm_out), (w_o, g.w_out))[n]
                    sp.dma_start(dst[:], src.rearrange("(k p) n -> p k n", p=P)).then_inc(s_w0[n], 16)
                load_operands(0, 0)
                load_weights(0)
                load_operands(1, 1)
                load_weights(1)
                load_gates(0, 0)
                load_weights(2)
                load_gates(1, 1)
                sample_inputs()

                def around(t, par):
                    if not (isinstance(t, int) and t == PT - 1):
                        wait_apart(sp, s_tc, t * 3 + 2, s_sp)
                        load_operands(t + 2, par)
                    store(t, par)
                    if not (isinstance(t, int) and t == PT - 1):
                        load_gates(t + 2, par)
                tiles(sp, around, store)

            @block.gpsimd
            def _(pool):
                nc.gpsimd.memset(wsT_s[:], 0.0).then_inc(s_zero, 1)
                nc.gpsimd.memset(eps[:], EPS).then_inc(s_zero, 1)
                pool.wait_ge(s_in, NIN)
                pool.wait_ge(s_ins, NSAMPLE)
                lows = lower[0:NS, 0:NS].unsqueeze(1).broadcast_to([NS, GROUPS, NS])
                nc.gpsimd.tensor_tensor(wsT_s[:], wsT_s[:], lows, ALU.mult).then_inc(s_wss, 1)

            @block.tensor
            def _(pe):
                pe.wait_ge(s_in, NIN)
                for q in range(GROUPS):
                    last = nc.tensor.transpose(ps_g[:, q * P:(q + 1) * P], ws_rows[:, q, :], ident[:])
                last.then_inc(s_ws, 1)
                pe.wait_ge(s_wsm, 1)

                def turn(bank, r, src):
                    for k in range(KD):
                        last = nc.tensor.transpose(bank[:, k * P:k * P + r], src[:, k * P:(k + 1) * P], ident[0:r, 0:r])
                    last.then_inc(s_t, 1)

                def product(ps, r, lT, w, sem):
                    for c in range(0, D, CB):
                        for k in range(KD):
                            last = nc.tensor.matmul(ps[0:r, c:c + CB], lT[:, k, 0:r], w[:, k, c:c + CB], start=k == 0, stop=k == KD - 1)
                    last.then_inc(sem, 1)

                def gate_products(t, par):
                    r = rows(t)
                    pe.wait_ge(s_ld[par], (t - par) * 24 + 48)
                    if r == NS:
                        pe.wait_ge(s_wss, 1)
                    wait_if_any(pe, s_gx, t - 1)
                    for q in range(GROUPS):
                        lhs = wsT[:, q, :] if r == P else wsT_s[:, q, :]
                        last = nc.tensor.matmul(ps_g[0:r, q * P:(q + 1) * P], lhs, v[0:r, par, q * P:(q + 1) * P], start=True, stop=True)
                    last.then_inc(s_gt, 1)

                def turn_operands(t, par):
                    r = rows(t)
                    pe.wait_ge(s_a, t + 1)
                    turn(ps_t, r, att[0:r, par, :])
                    wait_if_any(pe, s_ma, t)
                    pe.wait_ge(s_so, t + 1)
                    turn(ps_a, r, u[0:r, par, :])

                def products(t, par, between):
                    r = rows(t)
                    pe.wait_ge(s_tc, t * 3 + 2)
                    pe.wait_ge(s_w0[0], 16)
                    product(ps_a, r, aT, w_att, s_pa)
                    between()
                    pe.wait_ge(s_w0[1], 16)
                    product(ps_b, r, sT, w_gm, s_pb)

                def finish(t, par):
                    r = rows(t)
                    at = use_m(t)
                    pe.wait_ge(s_m, t + 1)
                    pe.wait_ge(s_tc, t * 3 + (2 if r == NS else 3))
                    turn(ps_t, r, ga[0:r, par, :])
                    pe.wait_ge(s_tc, at)
                    pe.wait_ge(s_w0[2], 16)
                    product(ps_g, r, mT, w_o, s_w)

                def around(t, par):
                    products(t, par, lambda: gate_products(t + 1, 1 - par))
                    turn_operands(t + 1, 1 - par)
                    finish(t, par)

                def last(t, par):
                    products(t, par, lambda: None)
                    finish(t, par)
                gate_products(0, 0)
                turn_operands(0, 0)
                tiles(pe, around, last)

            @block.scalar
            def _(act):
                act.wait_ge(s_in, NIN)
                act.wait_ge(s_zero, 2)

                def copy_turned(dst, bank, r, at):
                    act.wait_ge(s_t, at)
                    nc.scalar.activation(dst[:, :, 0:r], bank[:].rearrange("p (k c) -> p k c", c=P)[:, :, 0:r], ACT.Copy).then_inc(s_tc, 1)

                def prepare(t, par):
                    r = rows(t)
                    act.wait_ge(s_ld[par], (t - par) * 24 + 48)
                    nc.scalar.activation(sq[0:r, :], att[0:r, par, :], ACT.Square).then_inc(s_sqa, 1)
                    act.wait_ge(s_ss, t + 1)
                    nc.scalar.activation(sd[0:r, :], ss[0:r, :], ACT.Sqrt, bias=eps[0:r, :], scale=1.0 / VD).then_inc(s_sd, 1)
                    wait_if_any(act, s_pa, t)
                    copy_turned(aT, ps_t, r, use_a(t))
                    wait_if_any(act, s_pb, t)
                    copy_turned(sT, ps_a, r, use_a(t) + 1)

                def finish(t, par):
                    r = rows(t)
                    copy_turned(mT, ps_t, r, use_m(t))
                    act.wait_ge(s_x2, t + 2)
                    nc.scalar.activation(sq[0:r, :], x[0:r, par, :], ACT.Square, accum_out=ms[0:r, :]).then_inc(s_ms, 1)
                    act.wait_ge(s_ms, t + 1)
                    nc.scalar.activation(ms[0:r, :], ms[0:r, :], ACT.Sqrt, bias=eps[0:r, :], scale=1.0 / D).then_inc(s_sx, 1)

                def around(t, par):
                    prepare(t + 1, 1 - par)
                    finish(t, par)
                prepare(0, 0)
                tiles(act, around, finish)

            @block.vector
            def _(dve):
                dve.sem_inc(s_x2, 1)
                dve.wait_ge(s_in, NIN)
                dve.wait_ge(s_ws, 1)
                lowb = lower[:].unsqueeze(1).broadcast_to([P, GROUPS, P])
                nc.vector.tensor_tensor(wsT[:], ps_g[:].rearrange("p (g c) -> p g c", c=P), lowb, ALU.mult).then_inc(s_wsm, 1)
                nc.vector.tensor_scalar(again[:], again[:], 1.0 - LAMBDA_INIT, None, ALU.mult).then_inc(s_again, 1)
                dve.wait_ge(s_again, 1)

                def normed_attention(t, par):
                    r = rows(t)
                    dve.wait_ge(s_sqa, t + 1)
                    nc.vector.tensor_reduce(ss[0:r, :], sq[0:r, :].rearrange("p (h c) -> p h c", c=VD), AX.X, ALU.add).then_inc(s_ss, 1)
                    dve.wait_ge(s_sd, t + 1)
                    nc.vector.reciprocal(rs[0:r, :], sd[0:r, :]).then_inc(s_rs, 1)
                    dve.wait_ge(s_rs, t + 1)
                    a3 = att[0:r, par, :].rearrange("p (h c) -> p h c", c=VD)
                    nc.vector.tensor_tensor(a3, a3, rs[0:r, :].unsqueeze(2).broadcast_to([r, H, VD]), ALU.mult).then_inc(s_an, 1)
                    dve.wait_ge(s_an, t + 1)
                    nc.vector.tensor_tensor(a3, a3, again[0:r, :].unsqueeze(1).broadcast_to([r, H, VD]), ALU.mult).then_inc(s_a, 1)

                def gated(t, par):
                    r = rows(t)
                    dve.wait_ge(s_gt, t + 1)
                    if r == NS:
                        dve.wait_ge(s_ins, NSAMPLE)
                    b = bias if r == P else bias_s
                    for q in range(GROUPS):
                        cols = slice(q * P, (q + 1) * P)
                        last = nc.vector.scalar_tensor_tensor(out=u[0:r, par, cols], in0=ps_g[0:r, cols], scalar=b[0:r, q:q + 1],
                                                              in1=u[0:r, par, cols], op0=ALU.add, op1=ALU.mult)
                    last.then_inc(s_so, 1)

                def mix_a(t, par):
                    r = rows(t)
                    dve.wait_ge(s_lg[par], (t - par) * 24 + 48)
                    dve.wait_ge(s_pa, t + 1)
                    nc.vector.tensor_tensor(ga[0:r, par, :], ga[0:r, par, :], ps_a[0:r, :], ALU.mult).then_inc(s_ma, 1)

                def mix_b(t, par):
                    r = rows(t)
                    dve.wait_ge(s_pb, t + 1)
                    nc.vector.tensor_tensor(gb[0:r, par, :], gb[0:r, par, :], ps_b[0:r, :], ALU.mult).then_inc(s_gm, 1)
                    dve.wait_ge(s_gm, t + 1)
                    nc.vector.tensor_tensor(ga[0:r, par, :], ga[0:r, par, :], gb[0:r, par, :], ALU.add).then_inc(s_m, 1)

                def finish(t, par):
                    r = rows(t)
                    m = modp if r == P else mods
                    dve.wait_ge(s_w, t + 1)
                    nc.vector.tensor_tensor(gb[0:r, par, :], ps_g[0:r, :], m[0:r, 0, :], ALU.mult).then_inc(s_gx, 1)
                    dve.wait_ge(s_gx, t + 1)
                    nc.vector.tensor_tensor(x[0:r, par, :], x[0:r, par, :], gb[0:r, par, :], ALU.add).then_inc(s_x2, 1)
                    dve.wait_ge(s_sx, t + 1)
                    nc.vector.reciprocal(rx[0:r, :], ms[0:r, :]).then_inc(s_rx, 1)
                    dve.wait_ge(s_rx, t + 1)
                    nc.vector.scalar_tensor_tensor(out=ga[0:r, par, :], in0=x[0:r, par, :], scalar=rx[0:r, :], in1=m[0:r, 2, :],
                                                   op0=ALU.mult, op1=ALU.mult).then_inc(s_hn, 1)
                    dve.wait_ge(s_hn, t + 1)
                    nc.vector.tensor_tensor(ga[0:r, par, :], ga[0:r, par, :], m[0:r, 1, :], ALU.add).then_inc(s_h2, 1)

                def around(t, par):
                    normed_attention(t + 1, 1 - par)
                    mix_a(t, par)
                    gated(t + 1, 1 - par)
                    mix_b(t, par)
                    finish(t, par)

                def last(t, par):
                    mix_a(t, par)
                    mix_b(t, par)
                    finish(t, par)
                normed_attention(0, 0)
                gated(0, 0)
                tiles(dve, around, last)


def peer_phase(nc, g):
    HP = 2 * PH
    QW = HP * P
    LOWEST = -3.4e38
    R = 8
    CH = 16
    NCH = SLOTS // CH
    HALF = SLOTS // 2
    ND = 8
    QS = P // NS
    KS = SLOTS // QS
    LAPS = SLOTS // R
    with ExitStack() as ctx:
        sb = lambda name, shape, dt=F32: ctx.enter_context(nc.sbuf_tensor(name, shape, dt))
        ident, ident4, iota = sb("ident_f", [P, P]), sb("ident_4", [P, NS]), sb("iota16", [P, TOPK])
        wq = sb("w_query", [P, KD, QW])
        keysT = sb("subkeysT", [P, HP, P])
        h2n, h2c = sb("h2_next", [P, D]), sb("h2_now", [P, D])
        h2T = sb("h2T", [P, KD, P])
        sc = sb("query_then_scores", [P, HP, NKEYS])
        q = sc[:].rearrange("p n c -> p (n c)")
        qT = sb("queryT", [P, HP, P])
        rest = sb("scores_rest", [P, HP, NKEYS])
        keys = rest
        top = sb("half_top", [P, HP, TOPK])
        topi, topf = sb("half_top_i", [P, HP, TOPK], U32), sb("half_top_f", [P, HP, TOPK])
        best, besti = sb("best", [P, PH, TOPK]), sb("best_i", [P, PH, TOPK], U32)
        part, partf = sb("best_part", [P, 2, SLOTS], U32), sb("best_part_f", [P, 2, SLOTS])
        key = sb("best_key", [P, 2, SLOTS])
        total, rec = sb("gate_sum", [P, PH]), sb("gate_rec", [P, PH])
        gate = sb("gates", [P, PH, TOPK])
        idx_next, idx = sb("experts_next", [P, SLOTS], U32), sb("experts_now", [P, 2, HALF], U32)
        idx_s, gate_s = sb("experts_sample", [P, KS], U32), sb("gates_sample", [P, KS])
        ur, vr = sb("u_rows", [P, R, D]), sb("v_rows", [P, R, D])
        xy = sb("x2_then_y", [P, D])
        g2p, g2s = sb("gate2_prompt", [P, D]), sb("gate2_sample", [NS, D])
        a, ge, w = sb("a_now", [P, SLOTS]), sb("gelu_now", [P, SLOTS]), sb("w_now", [P, SLOTS])
        diag = sb("diag", [P, ND, P])
        ps_y, ps_t, ps_a, ps_b = [ctx.enter_context(nc.psum_tensor(n, [P, D], F32)) for n in ("ps_y", "ps_T", "ps_A", "ps_B")]
        s_in, s_kt, s_ktc, s_ht, s_htc, s_q, s_qc, s_qt, s_qtc, s_s, s_sc, s_ch, s_df, s_ex, s_rec, s_idx, s_gate, s_pv = [
            g.sem("f_" + n) for n in ("inputs", "keys_turned", "keysT", "h2_turned", "h2T", "query_half", "query_copied",
                                      "query_turned", "queryT", "scores", "scores_copied", "chain", "gate_difference",
                                      "gate_exp", "gate_rec", "experts", "gates", "vector_passed")]
        s_hc, s_u, s_ge, s_w, s_dg, s_v, s_gy, s_y, s_pk, s_pp, s_sp = [
            g.sem("g_" + n) for n in ("h2_now", "dots", "gelu", "weights", "diagonal", "added", "gated", "y",
                                      "sample_packed", "pool_passed", "sync_passed")]
        s_h, s_x, s_st = [g.sem(n) for n in ("g_h2_loaded", "g_x2_loaded", "g_y_stored")]
        s_key = g.sem("f_subkeys")
        s_wq = [g.sem(f"f_query_weights{n}") for n in range(2)]
        s_ix = [g.sem(f"g_experts_now{n}") for n in range(2)]
        s_ur = [g.sem(f"g_u_rows{j}") for j in range(R)]
        s_vr = [g.sem(f"g_v_rows{j}") for j in range(R)]
        NIN = 16 * (3 + NSEQ)

        def rows(f):
            return NS if isinstance(f, int) and f == PT else P

        def tiles(eng, body):
            with eng.Fori(0, PT - 1) as t:
                body(t, t + 1)
            body(PT - 1, PT)

        with nc.Block() as block:
            @block.sync
            def _(sp):
                sp.dma_start(keys[:], g.subkeys.rearrange("n k d -> k n d")).then_inc(s_key, 16)
                sp.dma_start(ident[:], g.ident).then_inc(s_key, 16)
                sp.dma_start(h2n[:], g.h2[0:P, :]).then_inc(s_h, 16)
                for n in range(2):
                    sp.dma_start(wq[:, :, n * D:(n + 1) * D],
                                 g.peer_w_q[:, n * D:(n + 1) * D].rearrange("(k p) n -> p k n", p=P)).then_inc(s_wq[n], 16)
                sp.dma_start(iota[:], g.iota16.broadcast_to([P, TOPK])).then_inc(s_in, 16)
                sp.dma_start(ident4[:], g.ident4).then_inc(s_in, 16)
                cols = slice(5 * D, 6 * D)
                sp.dma_start(g2p[:], g.mod[0:1, cols].broadcast_to([P, D])).then_inc(s_in, 16)
                for n in range(NSEQ):
                    sp.dma_start(g2s[n * NDEC:(n + 1) * NDEC, :], g.mod[1 + n:2 + n, cols].broadcast_to([NDEC, D])).then_inc(s_in, 16)

                def y_rows(t, dst):
                    wait_apart(sp, s_y, t + 2, s_sp)
                    sp.dma_start(dst, xy[0:dst.shape[0], :]).then_inc(s_st, 16)
                    wait_apart(sp, s_st, t * 16 + 16, s_sp)
                with sp.Fori(0, PT - 1) as t:
                    sp.dma_start(xy[:], g.x2[bass.ds(t * P, P), :]).then_inc(s_x, 16)
                    wait_apart(sp, s_hc, t + 1, s_sp)
                    sp.dma_start(h2n[:], g.h2[bass.ds(t * P + P, P), :]).then_inc(s_h, 16)
                    y_rows(t, g.y_p[bass.ds(t * P, P), :])
                sp.dma_start(xy[:], g.x2[NP - P:NP, :]).then_inc(s_x, 16)
                sp.wait_ge(s_hc, PT)
                for n in range(QS):
                    sp.dma_start(h2n[n * NS:(n + 1) * NS, :], g.h2[NP:NT, :]).then_inc(s_h, 16)
                y_rows(PT - 1, g.y_p[NP - P:NP, :])
                sp.dma_start(xy[0:NS, :], g.x2[NP:NT, :]).then_inc(s_x, 16)
                y_rows(PT, g.y_s)

            @block.gpsimd
            def _(pool):
                def gather(t, ring, sems, table, s, freed, ahead):
                    col = idx_s[:, s:s + 1] if isinstance(t, int) and t == PT else idx[:, s // HALF, s % HALF:s % HALF + 1]
                    wait_apart(pool, freed, t * SLOTS + (s + 1 - R + ahead), s_pp)
                    pool.indirect_dma_start(ring[:, s % R, :], None, table,
                                            bass.IndirectOffsetOnAxis(ap=col, axis=0)).then_inc(sems[s % R], 16)

                def body(t, f):
                    pool.wait_ge(s_idx, t + 1)
                    for s in range(SLOTS + CH):
                        if s in (0, 2 * CH):
                            n = 0 if s == 0 else 1
                            wait_apart(pool, s_v, t * SLOTS + (1 if n == 0 else HALF), s_pp)
                            nc.gpsimd.tensor_copy(idx[:, n, :], idx_next[:, n * HALF:(n + 1) * HALF]).then_inc(s_ix[n], 1)
                            wait_apart(pool, s_ix[n], t + 1, s_pp)
                        if s < SLOTS:
                            gather(t, ur, s_ur, g.peer_u, s, s_u, R)
                        if s >= CH:
                            gather(t, vr, s_vr, g.peer_v, s - CH, s_v, HALF)
                tiles(pool, body)
                wait_apart(pool, s_pk, 2 * QS, s_pp)
                for s in range(KS + CH):
                    if s < KS:
                        gather(PT, ur, s_ur, g.peer_u, s, s_u, R)
                    if s >= CH:
                        gather(PT, vr, s_vr, g.peer_v, s - CH, s_v, HALF)

            @block.tensor
            def _(pe):
                pe.sem_inc(s_v, HALF)
                pe.wait_ge(s_key, 32)
                for n, bank in enumerate((ps_t, ps_a)):
                    for k in range(KD):
                        last = nc.tensor.transpose(bank[:, k * P:(k + 1) * P], keys[:, n * KD + k, :], ident[:])
                    last.then_inc(s_kt, 1)
                pe.wait_ge(s_ktc, 2)

                def turn(f, bank, src, sem):
                    r = rows(f)
                    for k in range(KD):
                        last = nc.tensor.transpose(bank[:, k * P:k * P + r], src[0:r, k * P:(k + 1) * P], ident[0:r, 0:r])
                    last.then_inc(sem, 1)

                def query(f):
                    r = rows(f)
                    pe.wait_ge(s_h, f * 16 + (16 if r == P else 16 * QS))
                    pe.wait_ge(s_sc, f * 2 + 2)
                    turn(f, ps_t, h2n, s_ht)
                    pe.wait_ge(s_htc, f + 1)
                    for n, bank in enumerate((ps_a, ps_b)):
                        pe.wait_ge(s_wq[n], 16)
                        for c in range(0, D, CB):
                            for k in range(KD):
                                last = nc.tensor.matmul(bank[0:r, c:c + CB], h2T[:, k, 0:r], wq[:, k, n * D + c:n * D + c + CB],
                                                        start=k == 0, stop=k == KD - 1)
                        last.then_inc(s_q, 1)

                def turn_query(f):
                    pe.wait_ge(s_qc, f * 2 + 2)
                    for n, bank in enumerate((ps_t, ps_a)):
                        turn(f, bank, q[:, n * D:(n + 1) * D], s_qt)

                def scores(f):
                    r = rows(f)
                    pe.wait_ge(s_qtc, f * 2 + 2)
                    for n, bank in enumerate((ps_b, ps_t)):
                        for k in range(KD):
                            last = nc.tensor.matmul(bank[0:r, k * P:(k + 1) * P], qT[:, n * KD + k, 0:r], keysT[:, n * KD + k, :],
                                                    start=True, stop=True)
                        last.then_inc(s_s, 1)

                def add_rows(t, slots, c, m):
                    for s in range(c * CH, (c + 1) * CH):
                        if s == 0:
                            pe.wait_ge(s_y, t + 1)
                        pe.wait_ge(s_vr[s % R], t * (16 * LAPS) + 16 * (s // R + 1))
                        pe.wait_ge(s_dg, t * SLOTS + (s + 1))
                        for b in range(0, D, CB):
                            last = nc.tensor.matmul(ps_y[0:m, b:b + CB], diag[:, s % ND, 0:m], vr[:, s % R, b:b + CB],
                                                    start=s == 0, stop=s == slots - 1)
                        last.then_inc(s_v, 1)

                def body(t, f):
                    query(f)
                    for c in range(NCH):
                        add_rows(t, SLOTS, c, P)
                        if c == 0:
                            turn_query(f)
                        if c == 1:
                            scores(f)
                query(0)
                turn_query(0)
                scores(0)
                tiles(pe, body)
                for c in range(KS // CH):
                    add_rows(PT, KS, c, NS)

            @block.scalar
            def _(act):
                act.sem_inc(s_sc, 2)
                for n, bank in enumerate((ps_t, ps_a)):
                    act.wait_ge(s_kt, n + 1)
                    nc.scalar.activation(keysT[:, n * KD:(n + 1) * KD, :].rearrange("p k c -> p (k c)"), bank[:], ACT.Copy).then_inc(s_ktc, 1)
                turned = lambda bank, r: bank[:].rearrange("p (k c) -> p k c", c=P)[:, :, 0:r]

                def copy_query(f):
                    r = rows(f)
                    act.wait_ge(s_ht, f + 1)
                    nc.scalar.activation(h2T[:, :, 0:r], turned(ps_t, r), ACT.Copy).then_inc(s_htc, 1)
                    wait_if_any(act, s_gate, f)
                    for n, bank in enumerate((ps_a, ps_b)):
                        act.wait_ge(s_q, f * 2 + (n + 1))
                        nc.scalar.activation(q[0:r, n * D:(n + 1) * D], bank[0:r, :], ACT.Copy).then_inc(s_qc, 1)

                def copy_queryT(f):
                    r = rows(f)
                    for n, bank in enumerate((ps_t, ps_a)):
                        act.wait_ge(s_qt, f * 2 + (n + 1))
                        nc.scalar.activation(qT[:, n * KD:(n + 1) * KD, 0:r], turned(bank, r), ACT.Copy).then_inc(s_qtc, 1)

                def copy_scores(f):
                    r = rows(f)
                    for n, bank in enumerate((ps_b, ps_t)):
                        act.wait_ge(s_s, f * 2 + (n + 1))
                        nc.scalar.activation(q[0:r, n * D:(n + 1) * D], bank[0:r, :], ACT.Copy).then_inc(s_sc, 1)

                def gate_exp(f):
                    r = rows(f)
                    act.wait_ge(s_df, f + 1)
                    nc.scalar.activation(best[0:r], best[0:r], ACT.Exp).then_inc(s_ex, 1)

                def weights(t, c, lo, hi, m):
                    cols = slice(c * CH, (c + 1) * CH)
                    if lo == 0:
                        act.wait_ge(s_u, t * SLOTS + ((c + 1) * CH + R))
                        nc.scalar.activation(ge[:, cols], a[:, cols], ACT.Gelu).then_inc(s_ge, 1)
                        act.wait_ge(s_w, t * NCH + (c + 1))
                    for s in range(c * CH + lo, c * CH + hi):
                        act.wait_ge(s_v, t * SLOTS + (s + 1 - ND + HALF))
                        nc.scalar.activation(diag[:, s % ND, 0:m], (ident if m == P else ident4)[:], ACT.Copy,
                                             scale=w[:, s:s + 1]).then_inc(s_dg, 1)

                def body(t, f):
                    copy_query(f)
                    for c in range(NCH):
                        weights(t, c, 0, CH // 2, P)
                        if c == 1:
                            copy_queryT(f)
                        if c == 2:
                            copy_scores(f)
                        if c == NCH - 1:
                            gate_exp(f)
                        weights(t, c, CH // 2, CH, P)
                copy_query(0)
                copy_queryT(0)
                copy_scores(0)
                gate_exp(0)
                act.wait_ge(s_in, NIN)
                tiles(act, body)
                for c in range(KS // CH):
                    weights(PT, c, 0, CH, NS)

            @block.vector
            def _(dve):
                dve.sem_inc(s_u, R)
                dve.sem_inc(s_y, 1)
                dve.wait_ge(s_in, NIN)
                LINKS = 20
                a8, b8 = slice(0, 8), slice(8, 16)
                each = lambda n, step: [step(k) for k in range(n)][-1]

                def linker(f, n):
                    c = [n]

                    def link(ins):
                        c[0] += 1
                        ins.then_inc(s_ch, 1)
                        wait_apart(dve, s_ch, f * LINKS + c[0], s_pv)
                    return link, c

                def half_best(f):
                    r = rows(f)
                    link, c = linker(f, 0)
                    wait_apart(dve, s_sc, f * 2 + 4, s_pv)
                    link(each(HP, lambda k: nc.vector.max(top[0:r, k, a8], sc[0:r, k, :])))
                    link(each(HP, lambda k: nc.vector.match_replace(out=rest[0:r, k, :], in_to_replace=top[0:r, k, a8],
                                                                    in_values=sc[0:r, k, :], imm_value=LOWEST)))
                    link(each(HP, lambda k: nc.vector.max(top[0:r, k, b8], rest[0:r, k, :])))
                    assert c[0] == 3

                def half_places(f):
                    r = rows(f)
                    link, c = linker(f, 3)
                    each(HP, lambda k: nc.vector.max_index(topi[0:r, k, a8], top[0:r, k, a8], sc[0:r, k, :]))
                    link(each(HP, lambda k: nc.vector.max_index(topi[0:r, k, b8], top[0:r, k, b8], rest[0:r, k, :])))
                    link(nc.vector.tensor_copy(topf[0:r], topi[0:r]))
                    half = top[0:r].rearrange("p (h m) k -> p h m k", m=2)
                    cand = q[0:r].rearrange("p (h a b) -> p h a b", h=PH, a=TOPK)
                    link(nc.vector.tensor_tensor(cand, half[:, :, 0, :].unsqueeze(3).broadcast_to([r, PH, TOPK, TOPK]),
                                                 half[:, :, 1, :].unsqueeze(2).broadcast_to([r, PH, TOPK, TOPK]), ALU.add))
                    assert c[0] == 6

                def sum_best(f):
                    r = rows(f)
                    link, c = linker(f, 6)
                    cf = sc[0:r].rearrange("p (h m) c -> p h (m c)", m=2)
                    rf = rest[0:r].rearrange("p (h m) c -> p h (m c)", m=2)
                    link(each(PH, lambda k: nc.vector.max(best[0:r, k, a8], cf[:, k, :])))
                    link(each(PH, lambda k: nc.vector.match_replace(out=rf[:, k, :], in_to_replace=best[0:r, k, a8],
                                                                    in_values=cf[:, k, :], imm_value=LOWEST)))
                    link(each(PH, lambda k: nc.vector.max(best[0:r, k, b8], rf[:, k, :])))
                    each(PH, lambda k: nc.vector.max_index(besti[0:r, k, a8], best[0:r, k, a8], cf[:, k, :]))
                    link(each(PH, lambda k: nc.vector.max_index(besti[0:r, k, b8], best[0:r, k, b8], rf[:, k, :])))
                    link(nc.vector.tensor_copy(rec[0:r, :], best[0:r, :, 0]))
                    nc.vector.tensor_tensor(best[0:r], best[0:r], rec[0:r, :].unsqueeze(2).broadcast_to([r, PH, TOPK]),
                                            ALU.subtract).then_inc(s_df, 1)
                    assert c[0] == 11

                def experts(f):
                    r = rows(f)
                    link, c = linker(f, 11)
                    bi = besti[0:r].rearrange("p h k -> p (h k)")
                    nc.vector.tensor_scalar(part[0:r, 0, :], bi, 4, None, ALU.logical_shift_right)
                    link(nc.vector.tensor_scalar(part[0:r, 1, :], bi, TOPK - 1, None, ALU.bitwise_and))
                    link(nc.vector.tensor_copy(partf[0:r], part[0:r]))
                    tf = topf[0:r].rearrange("p (h m) k -> p h m k", m=2)
                    hot = q[0:r].rearrange("p (h a b) -> p h a b", h=PH, a=TOPK)
                    hot3 = q[0:r].rearrange("p (s b) -> p s b", b=TOPK)
                    flat = rest[0:r].rearrange("p n c -> p (n c)")
                    pick = flat.rearrange("p (h a b) -> p h a b", h=PH, a=TOPK)
                    pick3 = flat.rearrange("p (s b) -> p s b", b=TOPK)
                    io = iota[0:r].unsqueeze(1).broadcast_to([r, SLOTS, TOPK])
                    for m in range(2):
                        link(nc.vector.tensor_tensor(hot3, partf[0:r, m, :].unsqueeze(2).broadcast_to([r, SLOTS, TOPK]), io, ALU.is_equal))
                        link(nc.vector.tensor_tensor(pick, hot, tf[:, :, m, :].unsqueeze(2).broadcast_to([r, PH, TOPK, TOPK]), ALU.mult))
                        link(nc.vector.tensor_reduce(key[0:r, m, :], pick3, AX.X, ALU.add))
                    wait_if_any(dve, s_ix[1], f)
                    nc.vector.scalar_tensor_tensor(out=idx_next[0:r, :], in0=key[0:r, 0, :], scalar=float(NKEYS), in1=key[0:r, 1, :],
                                                   op0=ALU.mult, op1=ALU.add).then_inc(s_idx, 1)
                    assert c[0] == 19

                def gates(f):
                    r = rows(f)
                    link, c = linker(f, 19)
                    dve.wait_ge(s_ex, f + 1)
                    link(nc.vector.tensor_reduce(total[0:r, :], best[0:r], AX.X, ALU.add))
                    nc.vector.reciprocal(rec[0:r, :], total[0:r, :]).then_inc(s_rec, 1)
                    dve.wait_ge(s_rec, f + 1)
                    nc.vector.tensor_tensor(gate[0:r], best[0:r], rec[0:r, :].unsqueeze(2).broadcast_to([r, PH, TOPK]),
                                            ALU.mult).then_inc(s_gate, 1)
                    dve.wait_ge(s_gate, f + 1)
                    assert c[0] == LINKS

                gate_now = gate[:].rearrange("p h k -> p (h k)")

                def now(t, replicas):
                    dve.wait_ge(s_h, t * 16 + 16 * replicas)
                    nc.vector.tensor_copy(h2c[:], h2n[:]).then_inc(s_hc, 1)
                    dve.wait_ge(s_hc, t + 1)

                def dots(t, c, gt):
                    for s in range(c * CH, (c + 1) * CH):
                        dve.wait_ge(s_ur[s % R], t * (16 * LAPS) + 16 * (s // R + 1))
                        nc.vector.tensor_tensor_reduce(ur[:, s % R, :], ur[:, s % R, :], h2c[:], 1.0, 0.0, ALU.mult, ALU.add,
                                                       a[:, s:s + 1]).then_inc(s_u, 1)
                    cols = slice(c * CH, (c + 1) * CH)
                    dve.wait_ge(s_ge, t * NCH + (c + 1))
                    nc.vector.tensor_tensor(w[:, cols], ge[:, cols], gt[:, cols], ALU.mult).then_inc(s_w, 1)

                def result(t, slots, r, m):
                    dve.wait_ge(s_v, t * SLOTS + (slots + HALF))
                    dve.wait_ge(s_x, t * 16 + 16)
                    nc.vector.tensor_tensor(ps_y[0:r, :], ps_y[0:r, :], m[0:r, :], ALU.mult).then_inc(s_gy, 1)
                    dve.wait_ge(s_gy, t + 1)
                    nc.vector.tensor_tensor(xy[0:r, :], ps_y[0:r, :], xy[0:r, :], ALU.add).then_inc(s_y, 1)

                def body(t, f):
                    now(t, 1)
                    for c in range(NCH):
                        dots(t, c, gate_now)
                        if c == 3:
                            half_best(f)
                        if c == 4:
                            half_places(f)
                        if c == 5:
                            sum_best(f)
                        if c == 6:
                            experts(f)
                    gates(f)
                    result(t, SLOTS, P, g2p)
                half_best(0)
                half_places(0)
                sum_best(0)
                experts(0)
                gates(0)
                tiles(dve, body)
                for n in range(QS):
                    nc.vector.tensor_copy(idx_s[n * NS:(n + 1) * NS, :], idx_next[0:NS, n * KS:(n + 1) * KS]).then_inc(s_pk, 1)
                    nc.vector.tensor_copy(gate_s[n * NS:(n + 1) * NS, :], gate_now[0:NS, n * KS:(n + 1) * KS]).then_inc(s_pk, 1)
                dve.wait_ge(s_pk, 2 * QS)
                now(PT, QS)
                for c in range(KS // CH):
                    dots(PT, c, gate_s)
                result(PT, KS, NS, g2s)


def build(nc, ins, outs):
    g = Shared()
    with ExitStack() as ctx:
        used = []

        def sem(name):
            used.append(nc.alloc_semaphore(name=name))
            return used[-1]

        def run(phase):
            phase(nc, g)
            nc.clear_and_free_semaphores(used)
            nc.all_engine_barrier()
            used.clear()
        g.sem = sem
        g.c_prompt = ins["c_prompt"]
        g.c_sample = ins["c_sample"]
        g.page_table = ins["page_table"]
        g.ident = ins["ident"]
        g.rope = ins["rope"]
        g.mask = ins["mask"]
        g.new_mask = ins["new_mask"]
        g.prow = ins["prow"]
        g.b_ada = ins["b_ada"]
        g.norm1_g = ins["norm1_g"]
        g.norm2_g = ins["norm2_g"]
        g.q_norm_g = ins["q_norm_g"]
        g.k_norm_g = ins["k_norm_g"]
        g.subln_g = ins["subln_g"]
        g.gm_v_norm_g = ins["gm_v_norm_g"]
        g.lambda_q1 = ins["lambda_q1"]
        g.lambda_k1 = ins["lambda_k1"]
        g.lambda_q2 = ins["lambda_q2"]
        g.lambda_k2 = ins["lambda_k2"]
        g.lower_T = ins["lower_T"]
        g.ident4 = ins["ident4"]
        g.iota16 = ins["iota16"]
        g.w_ada = ins["w_ada"].rearrange("a p n -> (a p) n")
        g.w_in = ins["w_in"].rearrange("a p n -> (a p) n")
        g.w_att_out = ins["w_att_out"].rearrange("a p n -> (a p) n")
        g.w_gm_out = ins["w_gm_out"].rearrange("a p n -> (a p) n")
        g.w_out = ins["w_out"].rearrange("a p n -> (a p) n")
        g.peer_w_q = ins["peer_w_q"].rearrange("a p n -> (a p) n")
        g.peer_u = ins["peer_u"].rearrange("a p n -> (a p) n")
        g.peer_v = ins["peer_v"].rearrange("a p n -> (a p) n")
        g.x_prompt = ins["x_prompt"].rearrange("b t d -> (b t) d")
        g.x_sample = ins["x_sample"].rearrange("b t d -> (b t) d")
        g.y_p = outs[0].rearrange("b t d -> (b t) d")
        g.y_s = outs[1].rearrange("b t d -> (b t) d")
        g.o_kp = outs[2].rearrange("a b t h m d -> (a b t) (h m d)")
        g.o_vp = outs[3].rearrange("a b t h d -> (a b t) (h d)")
        g.o_ks = outs[4].rearrange("a b t h m d -> (a b t) (h m d)")
        g.o_vs = outs[5].rearrange("a b t h d -> (a b t) (h d)")
        g.o_gv = outs[6].rearrange("a b t d -> (a b t) d")
        g.mod = nc.dram_tensor("scratch_mod", [1 + NSEQ, MODS * D], F32, kind="Internal").ap()
        g.z = nc.dram_tensor("scratch_z", [NT, ZW], F32, kind="Internal").ap()
        g.att = nc.dram_tensor("scratch_att", [NT, D], F32, kind="Internal").ap()
        g.x2 = nc.dram_tensor("scratch_x2", [NT, D], F32, kind="Internal").ap()
        g.h2 = nc.dram_tensor("scratch_h2", [NT, D], F32, kind="Internal").ap()
        g.gm_ws = ins["gm_ws"].rearrange("a g i j -> (a g) i j")
        g.gm_bs = ins["gm_bs"].rearrange("a g i -> (a g) i")
        g.subkeys = ins["peer_subkeys"].rearrange("a h m k d -> (a h m) k d")
        g.lam = ctx.enter_context(nc.sbuf_tensor("lambda", [P, 1], F32))
        g.cache_k = ins["cache_k"].rearrange("a n p h m d -> (a n p) (h m d)")
        g.cache_v = ins["cache_v"].rearrange("a n p h d -> (a n p) (h d)")
        run(adaln_phase)
        run(projection_phase)
        run(prompt_attention_phase)
        run(sample_attention_phase)
        run(mix_phase)
        run(peer_phase)


_INS = ['x_prompt', 'x_sample', 'cache_k', 'cache_v', 'page_table', 'c_prompt', 'c_sample', 'w_ada', 'b_ada', 'norm1_g',
        'w_in', 'q_norm_g', 'k_norm_g', 'lambda_q1', 'lambda_k1', 'lambda_q2', 'lambda_k2', 'subln_g', 'gm_v_norm_g',
        'gm_ws', 'gm_bs', 'w_att_out', 'w_gm_out', 'w_out', 'norm2_g', 'peer_w_q', 'peer_subkeys', 'peer_u', 'peer_v']
_OUTS = [(1, 1024, 1024), (8, 4, 1024), (1, 1, 1024, 8, 2, 64), (1, 1, 1024, 8, 128), (1, 8, 4, 8, 2, 64),
         (1, 8, 4, 8, 128), (1, 8, 4, 1024)]


def _constants():
    import numpy as np
    f = np.float32
    pos = np.concatenate([np.arange(NP), PAST + np.tile(np.arange(NDEC), NSEQ)]).astype(f)
    inv = (f(1.0) / np.power(f(10000.0), np.arange(0, DH, 2, dtype=f) / f(DH))).astype(f)
    ang = (pos[:, None] * inv[None, :]).astype(f)
    cos, sin = np.cos(ang).astype(f), np.sin(ang).astype(f)
    rope = np.stack([np.concatenate([cos, cos], 1), np.concatenate([-sin, sin], 1)], 1)
    upper = np.triu(np.full((P, P), NEG, f), 1)
    new_mask = np.tile(upper[0:NDEC, 0:NDEC], (2 * H, 1))
    return {"ident": np.eye(P, dtype=f), "rope": np.ascontiguousarray(rope), "mask": upper, "new_mask": new_mask,
            "lower_T": np.triu(np.ones((P, P), f)), "ident4": np.tile(np.eye(NS, dtype=f), (P // NS, 1)),
            "iota16": np.arange(TOPK, dtype=f)[None, :], "prow": np.arange(P, dtype=f)[:, None]}


def kernel(**inputs):
    import numpy as _np
    import concourse.bacc as _bacc
    from concourse.bass_utils import run_bass_kernel_spmd as _run

    nc = _bacc.Bacc("TRN2", target_bir_lowering=False, num_devices=1)
    arrays, args = {}, {}
    named = {n: inputs[n] for n in _INS}
    named.update(_constants())
    for name, a in named.items():
        a = _np.ascontiguousarray(a)
        arrays[f"in_{name}"] = a
        args[name] = nc.dram_tensor(f"in_{name}", a.shape, mybir.dt.from_np(a.dtype), kind="ExternalInput").ap()
    outs = [nc.dram_tensor(f"out_{i}", shape, F32, kind="ExternalOutput").ap() for i, shape in enumerate(_OUTS)]
    build(nc, args, outs)
    r = _run(nc, [arrays], core_ids=[0])
    return tuple(r.results[0][f"out_{i}"] for i in range(len(_OUTS)))
```
